# Optimizing a Trainium2 kernel written in Bass

```python
import math
import jax
import jax.numpy as jnp
from jax import lax
import numpy as np

D_MODEL = 1024
BATCH = 1
SEQ = 512
DEPTH = 1

ATTN_HEADS = 8
ATTN_HEAD_DIM = 64
ATTN_V_DIM = 2 * ATTN_HEAD_DIM
ATTN_QBLOCK = 128
LAMBDA_BASE = 0.8
LAMBDA_SCALE = 0.6
LAMBDA_DECAY = 0.3
NUM_BUCKETS = 32
MAX_DISTANCE = 128
SSM_EXPAND = 2
D_INNER = SSM_EXPAND * D_MODEL
SSM_HEAD_DIM = 64
SSM_HEADS = D_INNER // SSM_HEAD_DIM
SSM_GROUPS = 8
SSM_HEADS_PER_GROUP = SSM_HEADS // SSM_GROUPS
D_STATE = 128
CONV_WIDTH = 4
SSM_CHUNK = 128
CONV_DIM = D_INNER + 2 * SSM_GROUPS * D_STATE
N_BRANCHES = 2
N_EXPERTS = 32
TOP_K = 4
D_EXPERT = D_MODEL
SWIGLU_LIMIT = 7.0
SWIGLU_ALPHA = 1.702
MOE_BLOCK = 128
RMS_EPS = 1e-6
SSM_EPS = 1e-5
Q_COLS = ATTN_HEADS * 2 * ATTN_HEAD_DIM
K_COLS = ATTN_HEADS * 2 * ATTN_HEAD_DIM
V_COLS = ATTN_HEADS * ATTN_V_DIM
Z_COLS = D_INNER
XBC_COLS = CONV_DIM
DT_COLS = SSM_HEADS
GATE_COLS = N_BRANCHES * D_MODEL
IN_COLS = Q_COLS + K_COLS + V_COLS + Z_COLS + XBC_COLS + DT_COLS + GATE_COLS

kernel_name = 'hybrid_diffattn_mamba2_moe_block'

def _rms_norm(x, g, eps):
    xf = x.astype(jnp.float32)
    y = xf * lax.rsqrt(jnp.mean(xf * xf, axis=-1, keepdims=True) + eps)
    return (y * g.astype(jnp.float32)).astype(x.dtype)

def _t5_bucket(dist):
    n = jnp.maximum(dist, 0)
    max_exact = NUM_BUCKETS // 2
    scaled = jnp.log(jnp.maximum(n, 1).astype(jnp.float32) / max_exact) / math.log(MAX_DISTANCE / max_exact)
    large = max_exact + (scaled * (NUM_BUCKETS - max_exact)).astype(jnp.int32)
    large = jnp.minimum(large, NUM_BUCKETS - 1)
    return jnp.where(n < max_exact, n, large)

def _diff_attention(q, k, v, lam, lambda_init, q_g, k_g, sub_g, rel_bias):
    b, s = q.shape[:2]
    q = _rms_norm(q.reshape(b, s, ATTN_HEADS, 2, ATTN_HEAD_DIM), q_g, RMS_EPS) * (ATTN_HEAD_DIM ** -0.5)
    k = _rms_norm(k.reshape(b, s, ATTN_HEADS, 2, ATTN_HEAD_DIM), k_g, RMS_EPS)
    q = q.transpose(0, 2, 3, 1, 4)
    k = k.transpose(0, 2, 3, 1, 4)
    v = v.reshape(b, s, ATTN_HEADS, ATTN_V_DIM).transpose(0, 2, 1, 3)
    k_pos = jnp.arange(s, dtype=jnp.int32)

    def q_block(i):
        start = i * ATTN_QBLOCK
        q_blk = lax.dynamic_slice_in_dim(q, start, ATTN_QBLOCK, axis=3)
        dist = (start + jnp.arange(ATTN_QBLOCK, dtype=jnp.int32))[:, None] - k_pos[None, :]
        bias = jnp.moveaxis(rel_bias[_t5_bucket(dist)], -1, 0).astype(jnp.float32)
        logits = jnp.einsum('bhmqd,bhmkd->bhmqk', q_blk, k).astype(jnp.float32) + bias[None, :, None]
        logits = jnp.where(dist >= 0, logits, -jnp.inf)
        p = jax.nn.softmax(logits, axis=-1)
        diff = p[:, :, 0] - lam * p[:, :, 1]
        return jnp.einsum('bhqk,bhkv->bhqv', diff.astype(v.dtype), v)

    o = lax.map(q_block, jnp.arange(s // ATTN_QBLOCK))
    o = o.transpose(1, 0, 3, 2, 4).reshape(b, s, ATTN_HEADS, ATTN_V_DIM)
    o = _rms_norm(o, sub_g, RMS_EPS) * (1.0 - lambda_init)
    return o.reshape(b, s, ATTN_HEADS * ATTN_V_DIM)

def _ssd_scan(xs, dt, a_log, bm, cm):
    b, s = xs.shape[:2]
    nc = s // SSM_CHUNK
    a = dt * (-jnp.exp(a_log.astype(jnp.float32)))

    def chunks(t):
        t = t.reshape((b, nc, SSM_CHUNK) + t.shape[2:])
        return jnp.moveaxis(t, 1, 0)

    gr = (SSM_GROUPS, SSM_HEADS_PER_GROUP)
    xs_c = chunks(xs.reshape((b, s) + gr + (SSM_HEAD_DIM,)))
    dt_c = chunks(dt.reshape((b, s) + gr))
    a_c = chunks(a.reshape((b, s) + gr))
    b_c = chunks(bm)
    c_c = chunks(cm)
    causal = jnp.tril(jnp.ones((SSM_CHUNK, SSM_CHUNK), dtype=bool))[None, :, :, None, None]

    def step(state, inp):
        xk, dtk, ak, bk, ck = inp
        acum = jnp.cumsum(ak, axis=1)
        seg = acum[:, :, None] - acum[:, None, :]
        decay = jnp.exp(jnp.where(causal, seg, -jnp.inf))
        cb = jnp.einsum('blgn,bsgn->blsg', ck, bk)
        mix = cb[..., None] * decay * dtk[:, None]
        y_diag = jnp.einsum('blsgr,bsgrp->blgrp', mix, xk)
        y_off = jnp.einsum('blgn,bgrpn->blgrp', ck, state) * jnp.exp(acum)[..., None]
        a_end = acum[:, -1]
        w_end = jnp.exp(a_end[:, None] - acum) * dtk
        state = state * jnp.exp(a_end)[..., None, None] + jnp.einsum('bsgn,bsgrp->bgrpn', bk, xk * w_end[..., None])
        return state, y_diag + y_off

    init = jnp.zeros((b, SSM_GROUPS, SSM_HEADS_PER_GROUP, SSM_HEAD_DIM, D_STATE), jnp.float32)
    _, ys = lax.scan(step, init, (xs_c, dt_c, a_c, b_c, c_c))
    return jnp.moveaxis(ys, 0, 1).reshape(b, s, SSM_HEADS, SSM_HEAD_DIM)

def _mamba2_mixer(z, xbc, dt_raw, conv_w, conv_b, dt_bias, a_log, d_skip, norm_g):
    b, s = z.shape[:2]
    xbc = lax.conv_general_dilated(
        xbc, conv_w[:, None, :].astype(xbc.dtype), window_strides=(1,),
        padding=[(CONV_WIDTH - 1, 0)], dimension_numbers=('NWC', 'WIO', 'NWC'),
        feature_group_count=CONV_DIM)
    xbc = jax.nn.silu(xbc + conv_b)
    xs, bm, cm = jnp.split(xbc, [D_INNER, D_INNER + SSM_GROUPS * D_STATE], axis=-1)
    xs = xs.reshape(b, s, SSM_HEADS, SSM_HEAD_DIM).astype(jnp.float32)
    bm = bm.reshape(b, s, SSM_GROUPS, D_STATE).astype(jnp.float32)
    cm = cm.reshape(b, s, SSM_GROUPS, D_STATE).astype(jnp.float32)
    dt = jax.nn.softplus(dt_raw.astype(jnp.float32) + dt_bias.astype(jnp.float32))
    y = _ssd_scan(xs, dt, a_log, bm, cm) + d_skip.astype(jnp.float32)[:, None] * xs
    y = y.reshape(b, s, D_INNER) * jax.nn.silu(z.astype(jnp.float32))
    y = _rms_norm(y.reshape(b, s, SSM_GROUPS, D_INNER // SSM_GROUPS), norm_g.reshape(SSM_GROUPS, -1), SSM_EPS)
    return y.reshape(b, s, D_INNER).astype(z.dtype)

def _moe(h, w_router, b_router, w1, b1, w2, b2):
    b, s, d = h.shape
    t = b * s
    hf = h.reshape(t, d)
    logits = jnp.einsum('td,de->te', hf, w_router).astype(jnp.float32) + b_router.astype(jnp.float32)
    top_val, top_idx = lax.top_k(logits, TOP_K)
    top_w = jax.nn.softmax(top_val, axis=-1)
    na = t * TOP_K
    flat_e = top_idx.reshape(na).astype(jnp.int32)
    flat_tok = jnp.arange(na, dtype=jnp.int32) // TOP_K
    flat_w = top_w.reshape(na)
    order = jnp.argsort(flat_e)
    sorted_e = flat_e[order]
    counts = jnp.zeros((N_EXPERTS,), jnp.int32).at[flat_e].add(1)
    padded = (counts + MOE_BLOCK - 1) // MOE_BLOCK * MOE_BLOCK
    start_raw = jnp.cumsum(counts) - counts
    end_pad = jnp.cumsum(padded)
    start_pad = end_pad - padded
    rank = jnp.arange(na, dtype=jnp.int32) - start_raw[sorted_e]
    dest = start_pad[sorted_e] + rank
    n_rows = na + N_EXPERTS * MOE_BLOCK
    n_blocks = n_rows // MOE_BLOCK
    buf_tok = jnp.full((n_rows,), t, jnp.int32).at[dest].set(flat_tok[order])
    buf_w = jnp.zeros((n_rows,), jnp.float32).at[dest].set(flat_w[order])
    block_start = jnp.arange(n_blocks, dtype=jnp.int32) * MOE_BLOCK
    block_e = jnp.minimum(jnp.searchsorted(end_pad, block_start, side='right'), N_EXPERTS - 1).astype(jnp.int32)
    h_pad = jnp.concatenate([hf, jnp.zeros((1, d), hf.dtype)], axis=0)

    def expert_block(args):
        tok, wts, e = args
        xb = h_pad[tok]
        gu = xb @ w1[e] + b1[e]
        gate, up = gu[:, :D_EXPERT], gu[:, D_EXPERT:]
        gate = jnp.minimum(gate, SWIGLU_LIMIT)
        up = jnp.clip(up, -SWIGLU_LIMIT, SWIGLU_LIMIT)
        act = (up + 1.0) * (gate * jax.nn.sigmoid(SWIGLU_ALPHA * gate))
        yb = act @ w2[e] + b2[e]
        return yb * wts[:, None].astype(yb.dtype)

    yb = lax.map(expert_block, (buf_tok.reshape(n_blocks, MOE_BLOCK), buf_w.reshape(n_blocks, MOE_BLOCK), block_e))
    out = jnp.zeros((t + 1, d), hf.dtype).at[buf_tok].add(yb.reshape(n_rows, d).astype(hf.dtype))
    return out[:t].reshape(b, s, d)

def setup_inputs(seed: int = 0) -> dict:
    key = jax.random.key(seed)
    ks = jax.random.split(key, 28)
    f32 = jnp.float32

    def nrm(k, shape, scale):
        return jax.random.normal(k, shape, f32) * scale

    def gain(k, shape):
        return 1.0 + 0.02 * jax.random.normal(k, shape, f32)

    dt0 = jnp.exp(jax.random.uniform(ks[14], (DEPTH, SSM_HEADS), f32, math.log(1e-3), math.log(1e-1)))
    return {
        'x': nrm(ks[0], (BATCH, SEQ, D_MODEL), 1.0),
        'g_mix': gain(ks[1], (DEPTH, D_MODEL)),
        'w_in': nrm(ks[2], (DEPTH, D_MODEL, IN_COLS), D_MODEL ** -0.5),
        'q_norm_g': gain(ks[3], (DEPTH, ATTN_HEAD_DIM)),
        'k_norm_g': gain(ks[4], (DEPTH, ATTN_HEAD_DIM)),
        'lambda_q1': nrm(ks[5], (DEPTH, ATTN_HEAD_DIM), 0.1),
        'lambda_k1': nrm(ks[6], (DEPTH, ATTN_HEAD_DIM), 0.1),
        'lambda_q2': nrm(ks[7], (DEPTH, ATTN_HEAD_DIM), 0.1),
        'lambda_k2': nrm(ks[8], (DEPTH, ATTN_HEAD_DIM), 0.1),
        'attn_sub_g': gain(ks[9], (DEPTH, ATTN_V_DIM)),
        'rel_bias': nrm(ks[10], (NUM_BUCKETS, ATTN_HEADS), 0.3),
        'w_attn_o': nrm(ks[11], (DEPTH, ATTN_HEADS * ATTN_V_DIM, D_MODEL), (ATTN_HEADS * ATTN_V_DIM) ** -0.5),
        'conv_w': nrm(ks[12], (DEPTH, CONV_WIDTH, CONV_DIM), CONV_WIDTH ** -0.5),
        'conv_b': nrm(ks[13], (DEPTH, CONV_DIM), 0.02),
        'dt_bias': dt0 + jnp.log(-jnp.expm1(-dt0)),
        'a_log': jnp.log(jax.random.uniform(ks[15], (DEPTH, SSM_HEADS), f32, 1.0, 16.0)),
        'd_skip': 1.0 + 0.1 * jax.random.normal(ks[16], (DEPTH, SSM_HEADS), f32),
        'ssm_norm_g': gain(ks[17], (DEPTH, D_INNER)),
        'w_ssm_o': nrm(ks[18], (DEPTH, D_INNER, D_MODEL), D_INNER ** -0.5),
        'w_out': nrm(ks[19], (DEPTH, D_MODEL, D_MODEL), D_MODEL ** -0.5),
        'g_ffn': gain(ks[20], (DEPTH, D_MODEL)),
        'w_router': nrm(ks[21], (DEPTH, D_MODEL, N_EXPERTS), D_MODEL ** -0.5),
        'b_router': nrm(ks[22], (DEPTH, N_EXPERTS), 0.01),
        'w1': nrm(ks[23], (DEPTH, N_EXPERTS, D_MODEL, 2 * D_EXPERT), D_MODEL ** -0.5),
        'b1': nrm(ks[24], (DEPTH, N_EXPERTS, 2 * D_EXPERT), 0.02),
        'w2': nrm(ks[25], (DEPTH, N_EXPERTS, D_EXPERT, D_MODEL), D_EXPERT ** -0.5),
        'b2': nrm(ks[26], (DEPTH, N_EXPERTS, D_MODEL), 0.02),
    }

def reference(x, g_mix, w_in, q_norm_g, k_norm_g, lambda_q1, lambda_k1, lambda_q2, lambda_k2,
              attn_sub_g, rel_bias, w_attn_o, conv_w, conv_b, dt_bias, a_log, d_skip, ssm_norm_g,
              w_ssm_o, w_out, g_ffn, w_router, b_router, w1, b1, w2, b2):
    b, s, d = x.shape
    sizes = (Q_COLS, K_COLS, V_COLS, Z_COLS, XBC_COLS, DT_COLS)
    split_pts = [sum(sizes[:i + 1]) for i in range(len(sizes))]
    for l in range(DEPTH):
        lambda_init = LAMBDA_BASE - LAMBDA_SCALE * math.exp(-LAMBDA_DECAY * l)
        h = _rms_norm(x, g_mix[l], RMS_EPS)
        proj = jnp.einsum('bsd,dc->bsc', h, w_in[l])
        q, k, v, z, xbc, dt_raw, gate_logits = jnp.split(proj, split_pts, axis=-1)
        lam = (jnp.exp(jnp.sum(lambda_q1[l].astype(jnp.float32) * lambda_k1[l].astype(jnp.float32)))
               - jnp.exp(jnp.sum(lambda_q2[l].astype(jnp.float32) * lambda_k2[l].astype(jnp.float32)))
               + lambda_init)
        attn = _diff_attention(q, k, v, lam, lambda_init, q_norm_g[l], k_norm_g[l], attn_sub_g[l], rel_bias)
        attn_out = jnp.einsum('bsc,cd->bsd', attn, w_attn_o[l])
        ssm = _mamba2_mixer(z, xbc, dt_raw, conv_w[l], conv_b[l], dt_bias[l], a_log[l], d_skip[l], ssm_norm_g[l])
        ssm_out = jnp.einsum('bsc,cd->bsd', ssm, w_ssm_o[l])
        gates = jax.nn.sigmoid(gate_logits.astype(jnp.float32)).reshape(b, s, N_BRANCHES, d).astype(x.dtype)
        merged = gates[:, :, 0] * attn_out + gates[:, :, 1] * ssm_out
        x = x + jnp.einsum('bsd,de->bse', merged, w_out[l])
        x = x + _moe(_rms_norm(x, g_ffn[l], RMS_EPS), w_router[l], b_router[l], w1[l], b1[l], w2[l], b2[l])
    return x


_drawn_inputs = setup_inputs


def setup_inputs(seed=0):
    import zlib

    import numpy as np

    out = dict(_drawn_inputs(seed))
    spreads = {}
    factors = {'lambda_q1': 38.252, 'b1': 5.945, 'b2': 6.836, 'k_norm_g': 2.864}
    for name, (base, spread) in spreads.items():
        noise = np.random.default_rng([zlib.crc32(name.encode()), seed]).standard_normal(out[name].shape)
        drawn = base * np.exp(spread * noise) if base else spread * noise
        out[name] = jnp.asarray(drawn.astype(out[name].dtype))
    for name, factor in factors.items():
        out[name] = (out[name] * factor).astype(out[name].dtype)
    return out
```

```python
import math
from contextlib import ExitStack

import numpy as np
import concourse.bass as bass
from concourse import mybir

F32 = mybir.dt.float32
I32 = mybir.dt.int32
U32 = mybir.dt.uint32
ALU = mybir.AluOpType
ACT = mybir.ActivationFunctionType
AX = mybir.AxisListType.X

P = 128
D = 1024
T = 512
KT = D // P
NT = T // P
HEADS = 8
HD = 64
HPG = 4
SSM_H = 32
GW = 256
VZ = P + GW
CHT = 8
NPAR = 22
E = 32
TOPK = 4
CAP = 96
MAXQ = (T - 1) // CAP
NOV = (T * TOPK) // CAP
NB = E + NOV + 1
ROWS = T + CAP
RMS_EPS = 1e-6
SSM_EPS = 1e-5
LAMBDA_INIT = 0.8 - 0.6 * math.exp(0.0)
SWIGLU_LIMIT = 7.0
SWIGLU_ALPHA = 1.702
NEG = -1e30
GL = 384

SMALL = {}
_o = 0
for _n, _w in (("g_mix", KT), ("qg", 1), ("kg", 1), ("subg", 1), ("lq1", HD), ("lk1", HD), ("lq2", HD),
               ("lk2", HD), ("dt_bias", SSM_H), ("a_log", SSM_H), ("d_skip", SSM_H), ("b_router", E)):
    SMALL[_n] = (_o, _w)
    _o += _w
N_SMALL = _o
CONST = {}
_o = 0
for _n, _w in (("ident", P), ("tri", P), ("after", P), ("ones", P), ("block", P),
               ("iota_e", E), ("iota_b", NOV + 1)):
    CONST[_n] = (_o, _w)
    _o += _w
N_CONST = _o


class Signal:

    def __init__(self, sem, per_step=1, unit=1):
        self.sem, self.per_step, self.unit = sem, per_step, unit
        self.first = 1 if unit == 1 else 0

    def at(self, step, k):
        assert k > 0 or self.first or not isinstance(step, int) or step > 0
        return step * (self.per_step * self.unit) + (k * self.unit + self.first)


def prime(eng, *signals):
    for s in signals:
        eng.sem_inc(s.sem, 1)


class Chain:

    def __init__(self, sem, per_step=0):
        self.sem, self.per_step, self.base, self.n = sem, per_step, 0, 0
        self.eng = self.step = None

    def start(self, eng, step=None):
        self.eng, self.step, self.n = eng, step, 0

    def link(self, ins):
        self.n += 1
        ins.then_inc(self.sem, 1)
        at = self.base + self.n
        self.eng.wait_ge(self.sem, at if self.step is None else self.step * self.per_step + at)

    def end(self, steps=1):
        if self.step is not None:
            assert self.n == self.per_step, ("links per step", self.n, self.per_step)
        self.base += self.n * steps
        self.n = 0


class Arena:

    def __init__(self, tensor, size):
        self.t, self.size, self.at = tensor, size, 0

    def reset(self, at=0):
        self.at = at

    def take(self, *shape):
        n = int(np.prod(shape))
        assert self.at + n <= self.size, ("arena", self.at + n, self.size)
        v = self.t[:, self.at:self.at + n]
        self.at += n
        if len(shape) == 2:
            v = v.rearrange("p (a b) -> p a b", a=shape[0])
        elif len(shape) == 3:
            v = v.rearrange("p (a b c) -> p a b c", a=shape[0], b=shape[1])
        return v


def apart(eng, sem):
    eng.wait_ge(sem, 80)


def bcast_inner(ap, n):
    return ap.unsqueeze(2).to_broadcast([ap.shape[0], ap.shape[1], n])


def bcast_mid(ap, n):
    return ap.unsqueeze(1).to_broadcast([ap.shape[0], n, ap.shape[1]])


DVE_LINKS, ACT_LINKS, MOE_LINKS = 40, 21, 17


def decoder_layer(nc, x, small, consts, onehot_rows, gffn, rel_bias, par, w_mix, w_vz, w_dt, w_o, w_out, w_rt, w1, w2, b12,
                  tok_ids, pads, out):
    with ExitStack() as ctx:
        def sb(name, shape, dt=F32):
            return ctx.enter_context(nc.sbuf_tensor(name, shape, dt))

        def sem(name):
            return ctx.enter_context(nc.semaphore(name))

        def sig(name, per_step=1, unit=1):
            return Signal(sem(name), per_step, unit)

        h2_rows = nc.dram_tensor("h2_rows", (ROWS, D), F32, kind="Internal").ap()
        dist_rows = nc.dram_tensor("dist_rows", (HEADS, GL), F32, kind="Internal").ap()
        bias_rows = nc.dram_tensor("bias_rows", (HEADS, P, 2 * P), F32, kind="Internal").ap()
        slot_rows = nc.dram_tensor("slot_rows", (CAP * NB, 2), I32, kind="Internal").ap()

        bank = [ctx.enter_context(nc.psum_tensor(f"bank{b}", [P, 512], F32)) for b in range(8)]
        proj_b = bank[0:2]
        s_b = bank[2:4]
        m0_b, m1_b, seg_b, y_b = bank[4:8]

        smalls = sb("smalls", [P, N_SMALL])
        cst = sb("cst", [P, N_CONST])
        eps = sb("eps", [P, 4])
        lam_t = sb("lam_t", [P, HD + 4])

        def sm(name):
            o, w = SMALL[name]
            return smalls[:, o:o + w]

        def cn(name, a=0, n=None):
            o, w = CONST[name]
            return cst[:, o + a:o + (w if n is None else a + n)]

        ident, tri, after, ones, block_ones = cn("ident"), cn("tri"), cn("after"), cn("ones"), cn("block")
        big = sb("big", [P, 24576])
        keep = sb("keep", [P, 23552])
        loop_mem, keep_mem = Arena(big, 24576), Arena(keep, 23552)
        par_sb = sb("par_sb", [P, HEADS * NPAR])
        far = sb("far", [P, HEADS])

        attnT = keep_mem.take(HEADS, T)
        ssmT = keep_mem.take(2 * HEADS, T)
        gateT = keep_mem.take(2, HEADS, T)
        wo_sb = keep_mem.take(3, KT, P)
        hT = loop_mem.take(KT, T)
        wm_sb = loop_mem.take(CHT, KT, P)
        wvz_sb = loop_mem.take(KT, VZ)
        loop_mark = loop_mem.at
        conv = loop_mem.take(4, T)
        xb = loop_mem.take(NT, 3 * P)
        qk = loop_mem.take(2, T)
        vz = loop_mem.take(NT, VZ)
        aux = sb("aux", [P, 2048])
        aux_mem = Arena(aux, 2048)
        L = aux_mem.take(2, T)
        diff = aux_mem.take(T)
        am = aux_mem.take(HPG, P)
        ext_mem = Arena(keep, 23552)
        ext_mem.reset(23552 - 3 * KT * P)
        sqx = keep[:, 23552 - 3 * KT * P:23552 - 3 * KT * P + D]
        sq = ext_mem.take(2, T)
        decay = ext_mem.take(HPG, P)
        mix = ext_mem.take(HPG, P)
        state = ext_mem.take(GW)
        xdt = ext_mem.take(GW)
        xw = ext_mem.take(GW)
        xd = ext_mem.take(GW)
        st = sb("st", [P, 32])
        yn = sb("yn", [P, GW])
        biasT = sb("biasT", [P, GW])
        dT = loop_mem.take(NT, T)
        ez = loop_mem.take(GW)
        ybuf = loop_mem.take(GW)
        ytmp = loop_mem.take(GW)
        cbm = loop_mem.take(P)
        dtv = sb("dtv", [P, NT, SSM_H])
        a_all = sb("a_all", [P, NT, SSM_H])
        eacum = sb("eacum", [P, NT, SSM_H])
        wend = sb("wend", [P, NT, SSM_H])
        eaend = sb("eaend", [P, NT, SSM_H])

        consts_in, x_in, wdt_in = sem("consts_in"), [sem(f"x_in{t}") for t in range(NT)], sem("wdt_in")
        h_ready, hT_banks, hT_read = sem("h_ready"), sem("hT_banks"), sem("hT_read")
        dt_ready, dt_read, a_ready, cums_ready, decays_ready = (
            sem("dt_ready"), sem("dt_read"), sem("a_ready"), sem("cums_ready"), sem("decays_ready"))
        dist_ready, dist_read, dist_out, lam_ready = sem("dist_ready"), sem("dist_read"), sem("dist_out"), sem("lam_ready")
        w_in_sig = [sig(f"w_tile{n}_in", 1, 16) for n in range(CHT)]
        wvz_in = sig("wvz_in", 1, 16)
        bias_in = sig("bias_in", 1, 16)
        proj_done = sig("proj_done", 12)
        taps_ready = sig("taps_ready", 4)
        conv_ready = sig("conv_ready", 4)
        silu_ready = sig("silu_ready", 4)
        proj_read = sig("proj_read", 8)
        z_ready = sig("z_ready", 4)
        sums_ready = sig("sums_ready", 2)
        root_ready = sig("root_ready", 2)
        qk_ready = sig("qk_ready", 2)
        m0_ready, m0_read = sig("m0_ready", 12), sig("m0_read", 12)
        m1_ready, m1_read = sig("m1_ready", 8), sig("m1_read", 8)
        am_ready = sig("am_ready", 4)
        xs_ready = sig("xs_ready", 4)
        seg_ready, decay_ready = sig("seg_ready", 4), sig("decay_ready", 4)
        scores_ready, logits_ready = sig("scores_ready", 4), sig("logits_ready", 4)
        max_ready, exp_ready, diff_ready = sig("max_ready", 4), sig("exp_ready", 4), sig("diff_ready", 4)
        cbm_ready, mix_ready = sig("cbm_ready", 4), sig("mix_ready", 4)
        ydiag_ready, y_read, y_ready, yn_ready = (sig("ydiag_ready", 4), sig("y_read", 4), sig("y_ready", 4),
                                                  sig("yn_ready", 4))
        osq_ready, osum_ready, oroot_ready = sig("osq_ready"), sig("osum_ready"), sig("oroot_ready")
        dve_step, act_step = Chain(sem("dve_step")), Chain(sem("act_step"))
        dve_loop, act_loop = Chain(sem("dve_loop"), DVE_LINKS), Chain(sem("act_loop"), ACT_LINKS)
        sigm_ready = sem("sigm_ready")
        wo_in = [sig(f"wo_in{n}", 1, 16) for n in range(3)]
        attn_out_ready, ssm_out_ready = sig("attn_out_ready"), sig("ssm_out_ready")
        attn_out_read, ssm_out_read, merged_ready = sig("attn_out_read"), sig("ssm_out_read"), sig("merged_ready")
        dve_merge = Chain(sem("dve_merge"), 0)
        wout_in, gffn_in, xr_in = sem("wout_in"), sem("gffn_in"), [sem(f"xr_in{t}") for t in range(NT)]
        res_ready, x1_ready, x1n_ready, h2_ready = sem("res_ready"), sem("x1_ready"), sem("x1n_ready"), sem("h2_ready")
        x1_out, h2_out, pads_out, zero_ready = sem("x1_out"), sem("h2_out"), sem("pads_out"), sem("zero_ready")
        h2T_ready, h2T_read, logit_ready = sem("h2T_ready"), sem("h2T_read"), sem("logit_ready")
        rt_exp, mask_ready, pos_ready, dest_ready, wrt_in = (
            sem("rt_exp"), sem("mask_ready"), sem("pos_ready"), sem("dest_ready"), sem("wrt_in"))
        slots_out, slots_in = sem("slots_out"), sem("slots_in")
        w1_in = [sig(f"w1_in{j}", 1, 16) for j in range(8)]
        w2_in = [sig(f"w2_in{k}", 1, 16) for k in range(8)]
        gather_in, scatter_done = sig("gather_in", 1, 16), sig("scatter_done", 1, 16)
        gu_ready, gu_read, gate_ready, swish_ready, act_ready = (
            sig("gu_ready", 8), sig("gu_read", 8), sig("gate_ready", 8), sig("swish_ready", 8), sig("act_ready", 8))
        w2_used, yT_ready, xt_ready, xt_read = sig("w2_used", 8), sig("yT_ready", 2), sig("xt_ready", 2), sig("xt_read", 2)
        yt_ready, yrow_ready, idx_ready = sig("yt_ready", 2), sig("yrow_ready", 2), sig("idx_ready", 2)
        dve_moe = Chain(sem("dve_moe"), MOE_LINKS)

        w1_sb = big[:, 0:8 * 2048].rearrange("p (j n) -> p j n", j=8)
        w2_sb = big[:, 8 * 2048:24576].rearrange("p (k n) -> p k n", k=8)
        wout_sb = w2_sb
        tail = Arena(big, 16384)
        tail.reset(12288)
        xr_sb, gffn_sb, wrt_sb = tail.take(2, D), tail.take(D), tail.take(KT, E)
        zeros = tail.take(32)
        x1_buf = keep[:, 0:2048].rearrange("p (a n) -> p a n", a=2)
        h2_buf = keep[:, 2048:4096].rearrange("p (a n) -> p a n", a=2)
        route_mem = Arena(keep, 12288)
        route_mem.reset(4096 + 4096)
        h2T = route_mem.take(KT, P)
        rt = Arena(keep, 23552)
        rt.reset(12288 + 4096)
        lg, onehot, mask, pos, quo = (rt.take(NT, E), rt.take(NT * TOPK, E), rt.take(NT, E), rt.take(NT, E),
                                      rt.take(NT, E))
        blk, dest, sel = rt.take(NT, E), rt.take(NT, E), rt.take(NT * TOPK, E)
        mv, mif, wgt, wsum, cnt, ov, ova, ovb, ovbase = (
            rt.take(NT, 8), rt.take(NT, TOPK), rt.take(NT, TOPK), rt.take(NT), rt.take(E), rt.take(E), rt.take(E),
            rt.take(E), rt.take(E))
        ovcmp, ovexp, destf = rt.take(NOV + 1, E), rt.take(NOV + 1), rt.take(NT * TOPK)
        mi = sb("mi", [P, NT, 8], U32)
        desti = sb("desti", [P, NT * TOPK], I32)
        pay = sb("pay", [P, NT * TOPK, 2], I32)
        slots = sb("slots", [CAP, NB, 2], I32)
        ovexp_i = sb("ovexp_i", [P, NOV + 2], I32)
        ex = Arena(keep, 8192)
        xg, xT, actT = ex.take(D), ex.take(KT, CAP), ex.take(KT, CAP)
        g_buf, u_buf, s_buf = ex.take(2, CAP), ex.take(2, CAP), ex.take(2, CAP)
        yT, y_rows, b12_sb, b_cur = ex.take(KT, CAP), ex.take(D), ex.take(E * 24), ex.take(24)
        spare = sb("spare", [CAP, 3])
        spare_used = [sig("spare_used0"), sig("spare_used1")]
        g_idx, s_idx = sb("g_idx", [CAP, 1], I32), sb("s_idx", [CAP, 1], I32)
        w_cur = sb("w_cur", [CAP, 1])
        b12_in, spare_ready = sem("b12_in"), sem("spare_ready")

        x_rows = x.rearrange("a s d -> (a s) d")

        with nc.Block() as block:
            MIX_ORDER = (1, 2, 3, 4, 5, 6, 11, 12)

            @block.sync
            def _(sp):
                sp.dma_start(cst[:], consts).then_inc(consts_in, 16)
                sp.dma_start(smalls[:], small).then_inc(consts_in, 16)
                xin = wm_sb.rearrange("p a b c -> p (a b c)")
                for t in range(NT):
                    sp.dma_start(xin[:, t * D:(t + 1) * D], x_rows[t * P:(t + 1) * P, :]).then_inc(x_in[t], 16)
                sp.dma_start(dT.rearrange("p a b -> p (a b)")[:, 0:KT * SSM_H], w_dt).then_inc(wdt_in, 16)
                sp.dma_start(par_sb[:], par).then_inc(consts_in, 16)
                sp.dma_start(conv.rearrange("p a b -> p (a b)")[0:32, 0:HEADS], rel_bias).then_inc(consts_in, 16)
                sp.dma_start(conv[0:32, 2, 0:GL], onehot_rows).then_inc(consts_in, 16)
                sp.dma_start(wvz_sb.rearrange("p a b -> p (a b)"), w_vz[0]).then_inc(wvz_in.sem, 16)
                sp.wait_ge(dist_read, 1)
                sp.dma_start(dist_rows, conv[0:HEADS, 1, 0:GL]).then_inc(dist_out, 16)
                sp.wait_ge(dist_out, 16)
                sp.dma_start(bias_rows, toeplitz(dist_rows)).then_inc(dist_out, 16)
                sp.wait_ge(dist_out, 32)
                sp.wait_ge(hT_banks, 2 * NT)
                for n in range(CHT):
                    sp.dma_start(wm_sb[:, n].rearrange("p a b -> p (a b)"), w_mix[0, :, n]).then_inc(
                        w_in_sig[n].sem, 16)
                sp.dma_start(biasT[:], bias_rows[0]).then_inc(bias_in.sem, 16)
                with sp.Fori(0, HEADS - 1) as i:
                    for n in range(6):
                        sp.wait_ge(proj_done.sem, proj_done.at(i, MIX_ORDER[n]))
                        sp.dma_start(wm_sb[:, n].rearrange("p a b -> p (a b)"),
                                     w_mix[bass.ds(i + 1, 1), :, n].rearrange("a p n -> (a p) n")).then_inc(
                            w_in_sig[n].sem, 16)
                    sp.wait_ge(proj_done.sem, proj_done.at(i, 10))
                    sp.dma_start(wvz_sb.rearrange("p a b -> p (a b)"),
                                 w_vz[bass.ds(i + 1, 1)].rearrange("a p n -> (a p) n")).then_inc(wvz_in.sem, 16)
                    sp.wait_ge(logits_ready.sem, logits_ready.at(i, 4))
                    sp.dma_start(biasT[:], bias_rows[bass.ds(i + 1, 1)].rearrange("a p n -> (a p) n")).then_inc(bias_in.sem, 16)
                    for n in (6, 7):
                        sp.wait_ge(proj_done.sem, proj_done.at(i, MIX_ORDER[n]))
                        sp.dma_start(wm_sb[:, n].rearrange("p a b -> p (a b)"),
                                     w_mix[bass.ds(i + 1, 1), :, n].rearrange("a p n -> (a p) n")).then_inc(
                            w_in_sig[n].sem, 16)

                sp.wait_ge(m0_read.sem, m0_read.at(HEADS, 0))
                sp.wait_ge(m1_read.sem, m1_read.at(HEADS, 0))
                for n in range(3):
                    sp.dma_start(wo_sb[:, n].rearrange("p a b -> p (a b)"), w_o[0, :, n]).then_inc(wo_in[n].sem, 16)
                sp.dma_start(wout_sb.rearrange("p k n -> p (k n)"), w_out).then_inc(wout_in, 16)
                sp.dma_start(gffn_sb, gffn).then_inc(gffn_in, 16)
                sp.dma_start(wrt_sb.rearrange("p a b -> p (a b)"), w_rt).then_inc(wrt_in, 16)
                for t in range(2):
                    sp.dma_start(xr_sb[:, t], x_rows[t * P:(t + 1) * P, :]).then_inc(xr_in[t], 16)
                sp.dma_start(slot_rows.rearrange("(s b) c -> s (b c)", s=CAP), pads).then_inc(pads_out, 16)
                sp.dma_start(pay[:].rearrange("p a b -> p (a b)"), tok_ids).then_inc(wrt_in, 16)
                for j in range(6):
                    sp.dma_start(w1_sb[:, j], w1[0, j]).then_inc(w1_in[j].sem, 16)

            @block.gpsimd
            def _(pool):
                prime(pool, am_ready, xs_ready, idx_ready, *spare_used)
                pool.wait_ge(decays_ready, 3)
                with pool.Fori(0, HEADS) as i:
                    h4 = i * HPG

                    def heads(table, u):
                        return table[:, u, bass.ds(h4, HPG)]

                    def make_am(u):
                        pool.wait_ge(seg_ready.sem, seg_ready.at(i, u))
                        pool.tensor_tensor(am, bcast_mid(tri, HPG), bcast_inner(heads(a_all, u), P),
                                           ALU.mult).then_inc(am_ready.sem, 1)

                    def make_xs(u):
                        pool.wait_ge(m0_read.sem, m0_read.at(i, u + 1))
                        pool.wait_ge(m1_ready.sem, m1_ready.at(i, min(2 * u, 6)))
                        pool.wait_ge(ydiag_ready.sem, ydiag_ready.at(i, u))
                        pool.wait_ge(y_read.sem, y_read.at(i, u))
                        xv = xb[:, u, 0:GW].rearrange("p (h c) -> p h c", h=HPG)
                        for dst, src in ((xdt, heads(dtv, u)), (xw, heads(wend, u))):
                            pool.tensor_tensor(dst.rearrange("p (h c) -> p h c", h=HPG), xv,
                                               bcast_inner(src, HD), ALU.mult)
                        dsk = SMALL["d_skip"][0]
                        pool.tensor_tensor(xd.rearrange("p (h c) -> p h c", h=HPG), xv,
                                           bcast_inner(smalls[:, bass.ds(h4 + dsk, HPG)], HD),
                                           ALU.mult).then_inc(xs_ready.sem, 1)

                    for u in range(NT):
                        make_am(u)
                        make_xs(u)

            @block.scalar
            def _(act):
                prime(act, taps_ready, silu_ready, proj_read, root_ready, m0_read, decay_ready, exp_ready, yn_ready,
                      osq_ready, oroot_ready, swish_ready, xt_read, yrow_ready)
                ch = act_step
                ch.start(act)
                act.preload_act_table_set("natural_log_exp_and_others")
                xin = wm_sb.rearrange("p a b c -> p (a b c)")

                act.wait_ge(consts_in, 80)
                act.wait_ge(lam_ready, 1)
                for t in range(NT):
                    xt = xin[:, t * D:(t + 1) * D]
                    act.wait_ge(x_in[t], 16)
                    ch.link(act.activation(sqx, xt, ACT.Square, accum_out=st[:, t:t + 1]))
                    ch.link(act.activation(st[:, t:t + 1], st[:, t:t + 1], ACT.Ln, bias=eps[:, 0:1], scale=1.0 / D))
                    ch.link(act.activation(st[:, t:t + 1], st[:, t:t + 1], ACT.Exp, scale=-0.5))
                    act.activation(xt, xt, ACT.Copy, scale=st[:, t:t + 1]).then_inc(h_ready, 1)
                act.wait_ge(lam_ready, 2)
                ch.link(act.activation(lam_t[:, HD:HD + 2], lam_t[:, HD:HD + 2], ACT.Exp))
                act.activation(ez[:, 0:SSM_H], sm("a_log"), ACT.Exp).then_inc(lam_ready, 1)
                act.wait_ge(dt_read, 1)
                ch.link(act.activation(eacum[:], wend[:], ACT.Exp, scale=-1.0))
                act.activation(eacum[:], eacum[:], ACT.Ln, bias=1.0).then_inc(dt_read, 1)
                act.wait_ge(cums_ready, 1)
                cum = y_b[:, 0:384].rearrange("p (k c h) -> p k c h", k=3, c=NT)
                act.activation(eacum[:], cum[:, 0], ACT.Exp).then_inc(decays_ready, 1)
                act.activation(wend[:], cum[:, 1], ACT.Exp)
                act.activation(eaend[:], cum[:, 2], ACT.Exp).then_inc(decays_ready, 1)
                ch.end()

                ch = act_loop
                with act.Fori(0, HEADS) as i:
                    ch.start(act, i)

                    def tap(n):
                        act.wait_ge(proj_done.sem, proj_done.at(i, n + 1))
                        act.wait_ge(m0_ready.sem, m0_ready.at(i, 0))
                        apart(act, consts_in)
                        p0 = i * NPAR
                        act.activation(conv[:, n], proj_b[n % 2][:], ACT.Identity,
                                       scale=par_sb[:, bass.ds(p0 + (4 * n + 3), 1)],
                                       bias=par_sb[:, bass.ds(p0 + (16 + n), 1)]).then_inc(taps_ready.sem, 1)

                    def silu(n):
                        act.wait_ge(conv_ready.sem, conv_ready.at(i, n + 1))
                        act.activation(conv[:, n], conv[:, n], ACT.Silu).then_inc(silu_ready.sem, 1)

                    def squares(n):
                        act.wait_ge(proj_done.sem, proj_done.at(i, 5 + n))
                        act.wait_ge(scores_ready.sem, scores_ready.at(i, 0))
                        act.wait_ge(m1_read.sem, m1_read.at(i, 0))
                        ch.link(act.activation(qk[:, n], proj_b[n][:], ACT.Copy))
                        act.activation(sq[:, n], proj_b[n][:], ACT.Square).then_inc(proj_read.sem, 1)

                    def root(n):
                        act.wait_ge(sums_ready.sem, sums_ready.at(i, n + 1))
                        ch.link(act.activation(sq[:, n], s_b[n][:], ACT.Ln, bias=eps[:, 0:1], scale=1.0 / HD))
                        act.activation(sq[:, n], sq[:, n], ACT.Exp, scale=-0.5).then_inc(root_ready.sem, 1)

                    def take_vz(t):
                        act.wait_ge(proj_done.sem, proj_done.at(i, 7 + t))
                        if t:
                            act.wait_ge(z_ready.sem, z_ready.at(i, t))
                        else:
                            act.wait_ge(m1_ready.sem, m1_ready.at(i, 0))
                            act.wait_ge(y_ready.sem, y_ready.at(i, 0))
                        ch.link(act.activation(vz[:, t], proj_b[t % 2][:, 0:VZ], ACT.Copy))
                        act.activation(ez, proj_b[t % 2][:, P:VZ], ACT.Exp, scale=-1.0).then_inc(proj_read.sem, 1)

                    def take_xb(u):
                        act.wait_ge(m0_ready.sem, m0_ready.at(i, u + 1))
                        act.wait_ge(xs_ready.sem, xs_ready.at(i, 0))
                        act.activation(xb[:, u], m0_b[:, 0:3 * P], ACT.Copy).then_inc(m0_read.sem, 1)

                    def make_decay(u):
                        act.wait_ge(seg_ready.sem, seg_ready.at(i, u + 1))
                        act.wait_ge(mix_ready.sem, mix_ready.at(i, u))
                        act.activation(decay.rearrange("p a b -> p (a b)"), seg_b[:], ACT.Exp).then_inc(
                            decay_ready.sem, 1)

                    def softmax_exp(u):
                        n = (u + 1) * P
                        act.wait_ge(max_ready.sem, max_ready.at(i, u + 1))
                        for m in range(2):
                            ins = act.activation(L[:, m, 0:n], L[:, m, 0:n], ACT.Exp, bias=st[:, 8 + m:9 + m],
                                                 accum_out=st[:, 10 + m:11 + m])
                        ins.then_inc(exp_ready.sem, 1)

                    def take_diff(u, k):
                        act.wait_ge(m0_ready.sem, m0_ready.at(i, k))
                        act.wait_ge(m1_ready.sem, m1_ready.at(i, 0))
                        src = m0_b[:, 0:(u + 1) * P].rearrange("p (a b) -> p a b", a=u + 1)
                        act.activation(dT[:, 0:u + 1, u * P:(u + 1) * P], src, ACT.Copy).then_inc(m0_read.sem, 1)

                    def norm_y(u, k):
                        act.wait_ge(y_ready.sem, y_ready.at(i, u + 1))
                        act.wait_ge(m0_ready.sem, m0_ready.at(i, k))
                        ch.link(act.activation(yn[:], ybuf, ACT.Square, accum_out=st[:, 16:17]))
                        ch.link(act.activation(st[:, 16:17], st[:, 16:17], ACT.Ln, bias=eps[:, 1:2], scale=1.0 / GW))
                        ch.link(act.activation(st[:, 16:17], st[:, 16:17], ACT.Exp, scale=-0.5))
                        act.activation(yn[:], ybuf, ACT.Copy, scale=st[:, 16:17]).then_inc(yn_ready.sem, 1)

                    def take_y(u, k):
                        act.wait_ge(m0_ready.sem, m0_ready.at(i, k))
                        apart(act, consts_in)
                        for j in range(2):
                            dst = ssmT[:, bass.ds(i * 2 + j, 1), u * P:(u + 1) * P].rearrange("p a b -> p (a b)")
                            ins = act.activation(dst, m0_b[:, j * P:(j + 1) * P], ACT.Copy,
                                                 scale=par_sb[:, bass.ds(i * NPAR + (20 + j), 1)])
                        ins.then_inc(m0_read.sem, 1)

                    def take_gate(n):
                        act.wait_ge(proj_done.sem, proj_done.at(i, 11 + n))
                        apart(act, consts_in)
                        dst = gateT[:, n, bass.ds(i, 1), :].rearrange("p a b -> p (a b)")
                        act.activation(dst, proj_b[n][:], ACT.Copy).then_inc(proj_read.sem, 1)

                    tap(0)
                    tap(1)
                    silu(0)
                    tap(2)
                    silu(1)
                    tap(3)
                    silu(2)
                    silu(3)
                    act.preload_act_table_set("natural_log_exp_and_others")
                    squares(0)
                    squares(1)
                    take_vz(0)
                    for u in range(NT):
                        take_xb(u)
                    root(0)
                    root(1)
                    take_vz(1)
                    make_decay(0)
                    softmax_exp(0)
                    take_vz(2)
                    norm_y(0, 0)
                    make_decay(1)
                    softmax_exp(1)
                    take_vz(3)
                    take_diff(0, 5)
                    make_decay(2)
                    softmax_exp(2)
                    take_diff(1, 6)
                    take_y(0, 7)
                    norm_y(1, 7)
                    make_decay(3)
                    softmax_exp(3)
                    take_gate(0)
                    take_diff(2, 8)
                    take_y(1, 9)
                    norm_y(2, 9)
                    take_diff(3, 10)
                    take_y(2, 11)
                    norm_y(3, 11)
                    act.wait_ge(m1_ready.sem, m1_ready.at(i, 8))
                    act.activation(sq[:, 0], m1_b[:], ACT.Square).then_inc(osq_ready.sem, 1)
                    take_gate(1)
                    act.wait_ge(osum_ready.sem, osum_ready.at(i, 1))
                    ch.link(act.activation(sq[:, 1], s_b[0][:], ACT.Ln, bias=eps[:, 0:1], scale=1.0 / P))
                    act.activation(sq[:, 1], sq[:, 1], ACT.Exp, scale=-0.5).then_inc(oroot_ready.sem, 1)
                    take_y(3, 12)
                ch.end(HEADS)
                act.wait_ge(proj_read.sem, proj_read.at(HEADS, 0))
                with act.Fori(0, KT) as i:
                    act.activation(gateT[:, 0, bass.ds(i, 1), :].rearrange("p a b -> p (a b)"),
                                   gateT[:, 0, bass.ds(i, 1), :].rearrange("p a b -> p (a b)"), ACT.Sigmoid)
                    act.activation(gateT[:, 1, bass.ds(i, 1), :].rearrange("p a b -> p (a b)"),
                                   gateT[:, 1, bass.ds(i, 1), :].rearrange("p a b -> p (a b)"),
                                   ACT.Sigmoid).then_inc(sigm_ready, 1)

            @block.vector
            def _(dve):
                prime(dve, conv_ready, z_ready, qk_ready, m1_read, logits_ready, max_ready, diff_ready, cbm_ready,
                      mix_ready, y_read, y_ready, attn_out_read, ssm_out_read, merged_ready, gu_read, gate_ready,
                      act_ready, yT_ready)
                ch = dve_step
                ch.start(dve)
                dve.memset(eps[:, 0:1], RMS_EPS)
                ch.link(dve.memset(eps[:, 1:2], SSM_EPS))
                dve.wait_ge(consts_in, 80)
                ch.link(dve.tensor_scalar(sm("qg"), sm("qg"), HD ** -0.5, None, ALU.mult))
                dve.tensor_scalar(sm("subg"), sm("subg"), 1.0 - LAMBDA_INIT, None, ALU.mult).then_inc(lam_ready, 1)
                ch.link(dve.tensor_tensor_reduce(lam_t[:, 0:HD], sm("lq1"), sm("lk1"), 1.0, 0.0, ALU.mult, ALU.add,
                                                 lam_t[:, HD:HD + 1]))
                dve.tensor_tensor_reduce(lam_t[:, 0:HD], sm("lq2"), sm("lk2"), 1.0, 0.0, ALU.mult, ALU.add,
                                         lam_t[:, HD + 1:HD + 2]).then_inc(lam_ready, 1)
                dve.wait_ge(dist_ready, 1)
                ch.link(dve.tensor_copy(conv[0:HEADS, 1, 0:GL], s_b[0][0:HEADS, 0:GL]))
                ch.link(dve.tensor_copy(far[:], s_b[1][:, 0:HEADS]))
                dve.memset(conv[0:HEADS, 1, 256:GL], NEG).then_inc(dist_read, 1)
                dve.wait_ge(lam_ready, 3)
                ch.link(dve.tensor_tensor(eps[:, 2:3], lam_t[:, HD + 1:HD + 2], lam_t[:, HD:HD + 1], ALU.subtract))
                ch.link(dve.tensor_scalar(eps[:, 2:3], eps[:, 2:3], -LAMBDA_INIT, None, ALU.add))
                for b in range(2 * NT):
                    t, half = b // 2, b % 2
                    dve.wait_ge(hT_banks, b + 1)
                    dve.tensor_tensor(hT[:, 4 * half:4 * half + 4, t * P:(t + 1) * P],
                                      bank[b % 2][:].rearrange("p (a b) -> p a b", a=4),
                                      bcast_inner(smalls[:, 4 * half:4 * half + 4], P), ALU.mult).then_inc(hT_read, 1)
                dve.wait_ge(dt_ready, 1)
                dproj = m0_b[:, 0:NT * SSM_H].rearrange("p (c h) -> p c h", c=NT)
                ch.link(dve.tensor_tensor(dtv[:], dproj, bcast_mid(sm("dt_bias"), NT), ALU.add))
                ch.link(dve.tensor_scalar(a_all[:], dtv[:], -1.0, None, ALU.mult))
                ch.link(dve.tensor_scalar(eaend[:], dtv[:], 0.0, None, ALU.max))
                dve.tensor_tensor(wend[:], dtv[:], a_all[:], ALU.max).then_inc(dt_read, 1)
                dve.wait_ge(dt_read, 2)
                ch.link(dve.tensor_tensor(dtv[:], eaend[:], eacum[:], ALU.add))
                ch.link(dve.tensor_tensor(a_all[:], dtv[:], bcast_mid(ez[:, 0:SSM_H], NT), ALU.mult))
                dve.tensor_scalar(a_all[:], a_all[:], -1.0, None, ALU.mult).then_inc(a_ready, 1)
                dve.wait_ge(decays_ready, 2)
                dve.tensor_tensor(wend[:], wend[:], dtv[:], ALU.mult).then_inc(decays_ready, 1)
                ch.end()

                ch = dve_loop
                with dve.Fori(0, HEADS) as i:
                    ch.start(dve, i)

                    def taps(n):
                        dve.wait_ge(taps_ready.sem, taps_ready.at(i, n + 1))
                        for s in (1, 2, 3):
                            w = par_sb[:, bass.ds(i * NPAR + (4 * n + 3 - s), 1)]
                            ins = dve.scalar_tensor_tensor(out=conv[:, n, s:T], in0=proj_b[n % 2][:, 0:T - s],
                                                           scalar=w, in1=conv[:, n, s:T], op0=ALU.mult, op1=ALU.add)
                            if s < 3:
                                ch.link(ins)
                        ins.then_inc(conv_ready.sem, 1)

                    def silu_z(t):
                        dve.wait_ge(proj_read.sem, proj_read.at(i, 3 + t))
                        ch.link(dve.tensor_scalar(ez, ez, 1.0, None, ALU.add))
                        ch.link(dve.reciprocal(ez, ez))
                        dve.tensor_tensor(vz[:, t, P:VZ], vz[:, t, P:VZ], ez, ALU.mult).then_inc(z_ready.sem, 1)

                    def norm_qk(n):
                        dve.wait_ge(root_ready.sem, root_ready.at(i, n + 1))
                        dve.scalar_tensor_tensor(out=qk[:, n], in0=qk[:, n], scalar=sm("qg" if n == 0 else "kg"),
                                                 in1=sq[:, n], op0=ALU.mult, op1=ALU.mult).then_inc(qk_ready.sem, 1)

                    def masked_cb(u):
                        dve.wait_ge(m1_ready.sem, m1_ready.at(i, 2 * u + 1))
                        dve.tensor_tensor(cbm, m1_b[:, 0:P], tri, ALU.mult).then_inc(m1_read.sem, 1)

                    def logits(u):
                        n = (u + 1) * P
                        near = min(2 * P, n)
                        dve.wait_ge(scores_ready.sem, scores_ready.at(i, u + 1))
                        if u == 0:
                            dve.wait_ge(bias_in.sem, bias_in.at(i, 1))
                        for m in range(2):
                            if n > near:
                                dve.tensor_scalar(L[:, m, 0:n - near], s_b[m][:, 0:n - near],
                                                  far[:, bass.ds(i, 1)], None, ALU.add)
                            ins = dve.tensor_tensor(L[:, m, n - near:n], s_b[m][:, n - near:n],
                                                    biasT[:, 2 * P - near:2 * P], ALU.add)
                        ins.then_inc(logits_ready.sem, 1)
                        dve.wait_ge(logits_ready.sem, logits_ready.at(i, u + 1))
                        ch.link(dve.tensor_reduce(st[:, 8:10], L[:, :, 0:n], AX, ALU.max))
                        dve.tensor_scalar(st[:, 8:10], st[:, 8:10], -1.0, None, ALU.mult).then_inc(max_ready.sem, 1)

                    def make_mix(u):
                        dve.wait_ge(decay_ready.sem, decay_ready.at(i, u + 1))
                        dve.wait_ge(m1_read.sem, m1_read.at(i, 2 * u + 1))
                        dve.wait_ge(ydiag_ready.sem, ydiag_ready.at(i, u))
                        dve.tensor_tensor(mix, decay, bcast_mid(cbm, HPG), ALU.mult).then_inc(mix_ready.sem, 1)

                    def make_diff(u, k):
                        n = (u + 1) * P
                        dve.wait_ge(exp_ready.sem, exp_ready.at(i, u + 1))
                        dve.wait_ge(m0_ready.sem, m0_ready.at(i, k))
                        ch.link(dve.reciprocal(st[:, 12:14], st[:, 10:12]))
                        ch.link(dve.tensor_tensor(st[:, 13:14], st[:, 13:14], eps[:, 2:3], ALU.mult))
                        ch.link(dve.tensor_scalar(diff[:, 0:n], L[:, 0, 0:n], st[:, 12:13], None, ALU.mult))
                        dve.scalar_tensor_tensor(out=diff[:, 0:n], in0=L[:, 1, 0:n], scalar=st[:, 13:14],
                                                 in1=diff[:, 0:n], op0=ALU.mult, op1=ALU.add).then_inc(
                            diff_ready.sem, 1)

                    def next_state(u):
                        dve.wait_ge(m1_ready.sem, m1_ready.at(i, 2 * u + 2))
                        new = m1_b[:, P:P + GW]
                        if u == 0:
                            dve.tensor_copy(state, new).then_inc(m1_read.sem, 1)
                            return
                        s4 = state.rearrange("p (h c) -> p h c", h=HPG)
                        ch.link(dve.tensor_tensor(s4, s4, bcast_inner(eaend[:, u, bass.ds(i * HPG, HPG)], HD),
                                                  ALU.mult))
                        dve.tensor_tensor(state, state, new, ALU.add).then_inc(m1_read.sem, 1)

                    def make_y(u):
                        dve.wait_ge(ydiag_ready.sem, ydiag_ready.at(i, u + 1))
                        dve.wait_ge(xs_ready.sem, xs_ready.at(i, u + 1))
                        dve.wait_ge(yn_ready.sem, yn_ready.at(i, u))
                        if u:
                            ch.link(dve.tensor_tensor(ybuf, y_b[:, 0:GW], xd, ALU.add))
                            dve.tensor_tensor(ytmp.rearrange("p (h c) -> p h c", h=HPG),
                                              y_b[:, GW:2 * GW].rearrange("p (h c) -> p h c", h=HPG),
                                              bcast_inner(eacum[:, u, bass.ds(i * HPG, HPG)], HD),
                                              ALU.mult).then_inc(y_read.sem, 1)
                            dve.wait_ge(y_read.sem, y_read.at(i, u + 1))
                            ch.link(dve.tensor_tensor(ybuf, ybuf, ytmp, ALU.add))
                        else:
                            dve.tensor_tensor(ybuf, y_b[:, 0:GW], xd, ALU.add).then_inc(y_read.sem, 1)
                            dve.wait_ge(y_read.sem, y_read.at(i, u + 1))
                        dve.wait_ge(z_ready.sem, z_ready.at(i, u + 1))
                        dve.tensor_tensor(ybuf, ybuf, vz[:, u, P:VZ], ALU.mult).then_inc(y_ready.sem, 1)

                    for n in range(4):
                        taps(n)
                    silu_z(0)
                    norm_qk(0)
                    norm_qk(1)
                    silu_z(1)
                    masked_cb(0)
                    logits(0)
                    silu_z(2)
                    make_mix(0)
                    make_diff(0, 0)
                    next_state(0)
                    make_y(0)
                    masked_cb(1)
                    logits(1)
                    silu_z(3)
                    make_mix(1)
                    make_diff(1, 5)
                    next_state(1)
                    make_y(1)
                    masked_cb(2)
                    logits(2)
                    make_mix(2)
                    make_diff(2, 6)
                    next_state(2)
                    make_y(2)
                    masked_cb(3)
                    logits(3)
                    make_mix(3)
                    make_diff(3, 8)
                    make_y(3)
                    dve.wait_ge(oroot_ready.sem, oroot_ready.at(i, 1))
                    dve.scalar_tensor_tensor(out=attnT[:, bass.ds(i, 1), :].rearrange("p a b -> p (a b)"),
                                             in0=m1_b[:], scalar=sm("subg"), in1=sq[:, 1], op0=ALU.mult,
                                             op1=ALU.mult).then_inc(m1_read.sem, 1)
                ch.end(HEADS)

            @block.tensor
            def _(pe):
                prime(pe, proj_done, sums_ready, m0_ready, m1_ready, seg_ready, scores_ready, ydiag_ready, osum_ready,
                      attn_out_ready, ssm_out_ready, gu_ready, w2_used, xt_ready, yt_ready)
                pe.wait_ge(consts_in, 80)
                rb = conv.rearrange("p a b -> p (a b)")[0:32, 0:HEADS]
                pe.matmul(s_b[0][0:HEADS, 0:GL], rb, conv[0:32, 2, 0:GL], start=True, stop=True)
                pe.matmul(s_b[1][:, 0:HEADS], conv[0:32, 2, 0:1].to_broadcast([32, P]), rb,
                          start=True, stop=True).then_inc(dist_ready, 1)
                xin = wm_sb.rearrange("p a b c -> p (a b c)")
                for b in range(2 * NT):
                    t, half = b // 2, b % 2
                    pe.wait_ge(h_ready, t + 1)
                    if b >= 2:
                        pe.wait_ge(hT_read, b - 1)
                    for k in range(4):
                        c = t * D + (4 * half + k) * P
                        ins = pe.transpose(bank[b % 2][:, k * P:(k + 1) * P], xin[:, c:c + P], ident)
                    ins.then_inc(hT_banks, 1)
                pe.wait_ge(hT_read, 2 * NT)
                pe.wait_ge(wdt_in, 16)
                wdt = dT.rearrange("p a b -> p (a b)")[:, 0:KT * SSM_H].rearrange("p (k h) -> p k h", k=KT)
                for t in range(NT):
                    for k in range(KT):
                        ins = pe.matmul(m0_b[:, t * SSM_H:(t + 1) * SSM_H], hT[:, k, t * P:(t + 1) * P], wdt[:, k],
                                        start=(k == 0), stop=(k == KT - 1))
                ins.then_inc(dt_ready, 1)
                pe.wait_ge(a_ready, 1)
                av = a_all[:].rearrange("p c h -> p (c h)")
                for n, m in enumerate((tri, after, ones)):
                    ins = pe.matmul(y_b[:, n * P:(n + 1) * P], m, av, start=True, stop=True)
                ins.then_inc(cums_ready, 1)
                pe.wait_ge(decays_ready, 3)

                with pe.Fori(0, HEADS) as i:
                    def free_proj(use):
                        if use < 2:
                            pe.wait_ge(proj_read.sem, proj_read.at(i, 0))
                        elif use < 6:
                            pe.wait_ge(conv_ready.sem, conv_ready.at(i, use - 1))
                        else:
                            pe.wait_ge(proj_read.sem, proj_read.at(i, use - 5))

                    def project(n, use, ks=range(KT)):
                        if 0 in ks:
                            free_proj(use)
                            pe.wait_ge(w_in_sig[n].sem, w_in_sig[n].at(i, 1))
                        for k in ks:
                            ins = pe.matmul(proj_b[use % 2][:], wm_sb[:, n, k], hT[:, k], start=(k == 0),
                                            stop=(k == KT - 1))
                        if KT - 1 in ks:
                            ins.then_inc(proj_done.sem, 1)

                    def project_vz(t):
                        free_proj(6 + t)
                        if t == 0:
                            pe.wait_ge(wvz_in.sem, wvz_in.at(i, 1))
                        for k in range(KT):
                            ins = pe.matmul(proj_b[t % 2][:, 0:VZ], hT[:, k, t * P:(t + 1) * P], wvz_sb[:, k],
                                            start=(k == 0), stop=(k == KT - 1))
                        ins.then_inc(proj_done.sem, 1)

                    def turn_xb(u):
                        if u == 0:
                            pe.wait_ge(silu_ready.sem, silu_ready.at(i, 4))
                        pe.wait_ge(m0_read.sem, m0_read.at(i, u))
                        for n in range(3):
                            ins = pe.transpose(m0_b[:, n * P:(n + 1) * P], conv[:, n, u * P:(u + 1) * P], ident)
                        ins.then_inc(m0_ready.sem, 1)

                    def sum_squares(n):
                        pe.wait_ge(proj_read.sem, proj_read.at(i, n + 1))
                        if n == 0:
                            pe.wait_ge(oroot_ready.sem, oroot_ready.at(i, 0))
                            pe.wait_ge(logits_ready.sem, logits_ready.at(i, 0))
                        pe.matmul(s_b[n][:], block_ones, sq[:, n], start=True, stop=True).then_inc(sums_ready.sem, 1)

                    def seg(u):
                        pe.wait_ge(am_ready.sem, am_ready.at(i, u + 1))
                        pe.wait_ge(decay_ready.sem, decay_ready.at(i, u))
                        pe.matmul(seg_b[:], after, am.rearrange("p a b -> p (a b)"), start=True,
                                  stop=True).then_inc(seg_ready.sem, 1)

                    def scores(u):
                        n = (u + 1) * P
                        if u == 0:
                            pe.wait_ge(qk_ready.sem, qk_ready.at(i, 2))
                            pe.wait_ge(root_ready.sem, root_ready.at(i, 2))
                        pe.wait_ge(logits_ready.sem, logits_ready.at(i, u))
                        for m in range(2):
                            r = slice(m * HD, (m + 1) * HD)
                            ins = pe.matmul(s_b[m][:, 0:n], qk[r, 0, u * P:(u + 1) * P], qk[r, 1, 0:n], start=True,
                                            stop=True)
                        ins.then_inc(scores_ready.sem, 1)

                    def cb(u):
                        pe.wait_ge(m1_read.sem, m1_read.at(i, 2 * u))
                        c = slice(u * P, (u + 1) * P)
                        pe.matmul(m1_b[:, 0:P], conv[:, 2, c], conv[:, 3, c], start=True, stop=True).then_inc(
                            m1_ready.sem, 1)

                    def y_and_state(u):
                        pe.wait_ge(y_read.sem, y_read.at(i, u))
                        pe.wait_ge(mix_ready.sem, mix_ready.at(i, u + 1))
                        pe.wait_ge(xs_ready.sem, xs_ready.at(i, u + 1))
                        for h in range(HPG):
                            ins = pe.matmul(y_b[:, h * HD:(h + 1) * HD], mix[:, h], xdt[:, h * HD:(h + 1) * HD],
                                            start=True, stop=True)
                        if u:
                            pe.wait_ge(m1_read.sem, m1_read.at(i, 2 * u))
                            ins = pe.matmul(y_b[:, GW:2 * GW], conv[:, 3, u * P:(u + 1) * P], state, start=True,
                                            stop=True)
                        ins.then_inc(ydiag_ready.sem, 1)
                        if u < NT - 1:
                            pe.wait_ge(m1_read.sem, m1_read.at(i, 2 * u + 1))
                            pe.matmul(m1_b[:, P:P + GW], xb[:, u, 2 * P:3 * P], xw, start=True, stop=True).then_inc(
                                m1_ready.sem, 1)

                    def turn_diff(u, k):
                        pe.wait_ge(diff_ready.sem, diff_ready.at(i, u + 1))
                        pe.wait_ge(m0_read.sem, m0_read.at(i, k))
                        for j in range(u + 1):
                            ins = pe.transpose(m0_b[:, j * P:(j + 1) * P], diff[:, j * P:(j + 1) * P], ident)
                        ins.then_inc(m0_ready.sem, 1)

                    def turn_y(u, k):
                        pe.wait_ge(yn_ready.sem, yn_ready.at(i, u + 1))
                        pe.wait_ge(m0_read.sem, m0_read.at(i, k))
                        for j in range(2):
                            ins = pe.transpose(m0_b[:, j * P:(j + 1) * P], yn[:, j * P:(j + 1) * P], ident)
                        ins.then_inc(m0_ready.sem, 1)

                    for n in range(6):
                        project(n, n)
                    project_vz(0)
                    for u in range(NT):
                        turn_xb(u)
                    sum_squares(0)
                    sum_squares(1)
                    project_vz(1)
                    seg(0)
                    cb(0)
                    scores(0)
                    project_vz(2)
                    y_and_state(0)
                    seg(1)
                    scores(1)
                    cb(1)
                    project_vz(3)
                    turn_diff(0, 4)
                    y_and_state(1)
                    seg(2)
                    scores(2)
                    cb(2)
                    project(6, 10, range(0, KT // 2))
                    turn_diff(1, 5)
                    turn_y(0, 6)
                    y_and_state(2)
                    seg(3)
                    scores(3)
                    cb(3)
                    project(6, 10, range(KT // 2, KT))
                    turn_diff(2, 7)
                    turn_y(1, 8)
                    y_and_state(3)
                    project(7, 11, range(0, KT // 2))
                    turn_diff(3, 9)
                    turn_y(2, 10)
                    pe.wait_ge(m1_read.sem, m1_read.at(i, 7))
                    pe.wait_ge(m0_read.sem, m0_read.at(i, 10))
                    pe.wait_ge(proj_read.sem, proj_read.at(i, 6))
                    for k in range(NT):
                        ins = pe.matmul(m1_b[:, k * P:T], vz[:, k, 0:P], dT[:, k, k * P:T], start=(k == 0),
                                        stop=(k == NT - 1))
                    ins.then_inc(m1_ready.sem, 1)
                    project(7, 11, range(KT // 2, KT))
                    pe.wait_ge(osq_ready.sem, osq_ready.at(i, 1))
                    pe.wait_ge(logits_ready.sem, logits_ready.at(i, 4))
                    pe.matmul(s_b[0][:], ones, sq[:, 0], start=True, stop=True).then_inc(osum_ready.sem, 1)
                    turn_y(3, 11)

        with nc.Block() as block:
            out_rows = out

            @block.sync
            def _(sp):
                with sp.Fori(0, KT - 1) as i:
                    sp.wait_ge(attn_out_ready.sem, attn_out_ready.at(i, 1))
                    for n in range(3):
                        if n == 1:
                            sp.wait_ge(ssm_out_ready.sem, ssm_out_ready.at(i, 1))
                        sp.dma_start(wo_sb[:, n].rearrange("p a b -> p (a b)"),
                                     w_o[bass.ds(i + 1, 1), :, n].rearrange("a p n -> (a p) n")).then_inc(
                            wo_in[n].sem, 16)
                sp.wait_ge(zero_ready, 1)
                sp.dma_start(h2_rows[T:ROWS, :], zero_rows(zeros)).then_inc(pads_out, 16)
                sp.dma_start(out_rows[T:ROWS, :], zero_rows(zeros)).then_inc(pads_out, 16)
                sp.wait_ge(pads_out, 48)
                for t in range(NT):
                    rows = slice(t * P, (t + 1) * P)
                    sp.wait_ge(x1_ready, 2 * (t + 1))
                    if t < 2:
                        sp.dma_start(xr_sb[:, t], x_rows[(t + 2) * P:(t + 3) * P, :]).then_inc(
                            xr_in[t + 2], 16)
                    sp.dma_start(out_rows[rows, :], x1_buf[:, t % 2]).then_inc(x1_out, 16)
                    sp.wait_ge(h2_ready, t + 1)
                    sp.dma_start(h2_rows[rows, :], h2_buf[:, t % 2]).then_inc(h2_out, 16)
                    sp.wait_ge(x1_out, 16 * (t + 1))
                    sp.wait_ge(h2_out, 16 * (t + 1))
                sp.wait_ge(res_ready, 2 * NT)
                for k in range(8):
                    sp.dma_start(w2_sb[:, k], w2[0, k]).then_inc(w2_in[k].sem, 16)
                sp.wait_ge(logit_ready, NT)
                for j in (6, 7):
                    sp.dma_start(w1_sb[:, j], w1[0, j]).then_inc(w1_in[j].sem, 16)
                sp.dma_start(b12_sb, b12).then_inc(b12_in, 16)
                sp.wait_ge(slots_out, 16 * NT * TOPK)
                sp.dma_start(slots[:].rearrange("s b c -> s (b c)"),
                             slot_rows.rearrange("(s b) c -> s (b c)", s=CAP)).then_inc(slots_in, 16)

            @block.tensor
            def _(pe):
                with pe.Fori(0, KT) as i:
                    pe.wait_ge(attn_out_read.sem, attn_out_read.at(i, 0))
                    pe.wait_ge(wo_in[0].sem, wo_in[0].at(i, 1))
                    for k in range(KT):
                        ins = pe.matmul(bank[0][:], wo_sb[:, 0, k], attnT[:, k], start=(k == 0), stop=(k == KT - 1))
                    ins.then_inc(attn_out_ready.sem, 1)
                    pe.wait_ge(ssm_out_read.sem, ssm_out_read.at(i, 0))
                    for k in range(2 * KT):
                        if k % KT == 0:
                            pe.wait_ge(wo_in[1 + k // KT].sem, wo_in[1 + k // KT].at(i, 1))
                        ins = pe.matmul(bank[1][:], wo_sb[:, 1 + k // KT, k % KT], ssmT[:, k], start=(k == 0),
                                        stop=(k == 2 * KT - 1))
                    ins.then_inc(ssm_out_ready.sem, 1)
                pe.wait_ge(merged_ready.sem, merged_ready.at(KT, 0))
                pe.wait_ge(wout_in, 16)

                def residual(t):
                    if t:
                        pe.wait_ge(x1_ready, 2 * t)
                    for half in range(2):
                        for k in range(KT):
                            ins = pe.matmul(bank[2 + half][:], gateT[:, 0, k, t * P:(t + 1) * P],
                                            wout_sb[:, k, half * 512:(half + 1) * 512], start=(k == 0),
                                            stop=(k == KT - 1))
                        ins.then_inc(res_ready, 1)

                def router(t):
                    pe.wait_ge(h2_ready, t + 1)
                    if t:
                        pe.wait_ge(h2T_read, 2 * t)
                    for half in range(2):
                        for k in range(4):
                            c = (4 * half + k) * P
                            ins = pe.transpose(bank[4 + half][:, k * P:(k + 1) * P], h2_buf[:, t % 2, c:c + P], ident)
                        ins.then_inc(h2T_ready, 1)
                    pe.wait_ge(h2T_read, 2 * (t + 1))
                    pe.wait_ge(wrt_in, 32)
                    for k in range(KT):
                        ins = pe.matmul(bank[6][:, t * E:(t + 1) * E], h2T[:, k], wrt_sb[:, k], start=(k == 0),
                                        stop=(k == KT - 1))
                    ins.then_inc(logit_ready, 1)

                residual(0)
                for t in range(1, NT):
                    residual(t)
                    router(t - 1)
                router(NT - 1)
                pe.wait_ge(mask_ready, 1)
                for t in range(NT):
                    for s in range(t + 1):
                        ins = pe.matmul(bank[7][:, t * E:(t + 1) * E], tri if s == t else ones, mask[:, s],
                                        start=(s == 0), stop=(s == t))
                for s in range(NT):
                    ins = pe.matmul(bank[7][:, NT * E:(NT + 1) * E], ones, mask[:, s], start=(s == 0),
                                    stop=(s == NT - 1))
                ins.then_inc(pos_ready, 1)

            @block.scalar
            def _(act):
                ch = act_step
                ch.start(act)
                act.preload_act_table_set("natural_log_exp_and_others")
                for t in range(NT):
                    act.wait_ge(x1_ready, 2 * (t + 1))
                    if t >= 2:
                        act.wait_ge(h2_out, 16 * (t - 1))
                        act.wait_ge(h2T_ready, 2 * (t - 1))
                    else:
                        act.wait_ge(merged_ready.sem, merged_ready.at(KT, 0))
                    h2 = h2_buf[:, t % 2]
                    ch.link(act.activation(h2, x1_buf[:, t % 2], ACT.Square, accum_out=st[:, 20:21]))
                    ch.link(act.activation(st[:, 20:21], st[:, 20:21], ACT.Ln, bias=eps[:, 0:1], scale=1.0 / D))
                    ch.link(act.activation(st[:, 20:21], st[:, 20:21], ACT.Exp, scale=-0.5))
                    act.activation(h2, x1_buf[:, t % 2], ACT.Copy, scale=st[:, 20:21]).then_inc(x1n_ready, 1)
                    for half in range(2):
                        act.wait_ge(h2T_ready, 2 * t + half + 1)
                        if t:
                            act.wait_ge(logit_ready, t)
                        act.activation(h2T[:, 4 * half:4 * half + 4],
                                       bank[4 + half][:].rearrange("p (a b) -> p a b", a=4),
                                       ACT.Copy).then_inc(h2T_read, 1)
                act.wait_ge(rt_exp, 1)
                act.activation(wgt, wgt, ACT.Exp).then_inc(rt_exp, 1)
                ch.end()

            @block.vector
            def _(dve):
                with dve.Fori(0, KT) as i:
                    g0 = gateT[:, 0, bass.ds(i, 1), :].rearrange("p a b -> p (a b)")
                    g1 = gateT[:, 1, bass.ds(i, 1), :].rearrange("p a b -> p (a b)")
                    dve.wait_ge(attn_out_ready.sem, attn_out_ready.at(i, 1))
                    dve.wait_ge(merged_ready.sem, merged_ready.at(i, 0))
                    dve.tensor_tensor(L[:, 0], bank[0][:], g0, ALU.mult).then_inc(attn_out_read.sem, 1)
                    dve.wait_ge(ssm_out_ready.sem, ssm_out_ready.at(i, 1))
                    dve.tensor_tensor(L[:, 1], bank[1][:], g1, ALU.mult).then_inc(ssm_out_read.sem, 1)
                    dve.wait_ge(attn_out_read.sem, attn_out_read.at(i, 1))
                    dve.wait_ge(ssm_out_read.sem, ssm_out_read.at(i, 1))
                    dve.tensor_tensor(g0, L[:, 0], L[:, 1], ALU.add).then_inc(merged_ready.sem, 1)
                dve.memset(zeros, 0.0).then_inc(zero_ready, 1)
                ch = dve_step
                ch.start(dve)
                dve.wait_ge(gffn_in, 16)

                def residual(t):
                    dve.wait_ge(xr_in[t], 16)
                    if t >= 2:
                        dve.wait_ge(x1_out, 16 * (t - 1))
                        dve.wait_ge(x1n_ready, t - 1)
                    for half in range(2):
                        c = slice(half * 512, (half + 1) * 512)
                        dve.wait_ge(res_ready, 2 * t + half + 1)
                        dve.tensor_tensor(x1_buf[:, t % 2, c], bank[2 + half][:], xr_sb[:, t % 2, c],
                                          ALU.add).then_inc(x1_ready, 1)

                def gain(t):
                    dve.wait_ge(x1n_ready, t + 1)
                    dve.tensor_tensor(h2_buf[:, t % 2], h2_buf[:, t % 2], gffn_sb, ALU.mult).then_inc(h2_ready, 1)

                for t in range(NT):
                    residual(t)
                    gain(t)
                dve.wait_ge(logit_ready, NT)
                ch.link(dve.tensor_tensor(lg, bank[6][:, 0:NT * E].rearrange("p (t e) -> p t e", t=NT),
                                          bcast_mid(sm("b_router"), NT), ALU.add))
                for t in range(NT):
                    ch.link(dve.max(mv[:, t], lg[:, t]))
                    ch.link(dve.max_index(mi[:, t], mv[:, t], lg[:, t]))
                ch.link(dve.tensor_copy(mif, mi[:, :, 0:TOPK]))
                dve.tensor_tensor(wgt, mv[:, :, 0:TOPK], mv[:, :, 0:1].to_broadcast([P, NT, TOPK]),
                                  ALU.subtract).then_inc(rt_exp, 1)
                iota_e = cn("iota_e")
                ch.link(dve.tensor_tensor(onehot, bcast_mid(iota_e, NT * TOPK),
                                          bcast_inner(mif.rearrange("p t k -> p (t k)"), E), ALU.is_equal))
                for t in range(NT):
                    ins = dve.tensor_reduce(mask[:, t], onehot[:, TOPK * t:TOPK * (t + 1)].rearrange("p k e -> p e k"),
                                            AX, ALU.add)
                ins.then_inc(mask_ready, 1)
                dve.wait_ge(rt_exp, 2)
                ch.link(dve.tensor_reduce(wsum, wgt, AX, ALU.add))
                ch.link(dve.reciprocal(wsum, wsum))
                dve.wait_ge(wrt_in, 32)
                ch.link(dve.tensor_tensor(pay[:, :, 1:2].bitcast(F32).rearrange("p (t k) o -> p t (k o)", t=NT), wgt,
                                          bcast_inner(wsum, TOPK), ALU.mult))
                dve.wait_ge(pos_ready, 1)
                dve.wait_ge(mask_ready, 1)
                ch.link(dve.tensor_tensor(pos, bank[7][:, 0:NT * E].rearrange("p (t e) -> p t e", t=NT), mask,
                                          ALU.subtract))
                ch.link(dve.tensor_copy(cnt, bank[7][:, NT * E:(NT + 1) * E]))
                ch.link(dve.tensor_scalar(quo, pos, float(CAP), None, ALU.is_ge))
                ch.link(dve.tensor_scalar(ov, cnt, float(CAP), None, ALU.is_gt))
                for j in range(2, MAXQ + 1):
                    ch.link(dve.scalar_tensor_tensor(out=quo, in0=pos, scalar=float(j * CAP), in1=quo,
                                                     op0=ALU.is_ge, op1=ALU.add))
                    ch.link(dve.scalar_tensor_tensor(out=ov, in0=cnt, scalar=float(j * CAP), in1=ov,
                                                     op0=ALU.is_gt, op1=ALU.add))
                src, dst = ov, ova
                for s in (1, 2, 4, 8, 16):
                    ch.link(dve.tensor_copy(dst[:, 0:s], src[:, 0:s]))
                    ch.link(dve.tensor_tensor(dst[:, s:E], src[:, s:E], src[:, 0:E - s], ALU.add))
                    src, dst = dst, (ovb if dst is ova else ova)
                ovend = src
                ch.link(dve.tensor_tensor(ovbase, ovend, ov, ALU.subtract))
                ch.link(dve.tensor_tensor(ovbase, ovbase, iota_e, ALU.subtract))
                ch.link(dve.tensor_scalar(ovbase, ovbase, float(E - 1), None, ALU.add))
                ch.link(dve.tensor_tensor(blk, quo, bcast_mid(ovbase, NT), ALU.add))
                ch.link(dve.scalar_tensor_tensor(out=blk, in0=quo, scalar=1.0, in1=blk, op0=ALU.is_ge,
                                                 op1=ALU.mult))
                ch.link(dve.tensor_tensor(blk, blk, bcast_mid(iota_e, NT), ALU.add))
                ch.link(dve.scalar_tensor_tensor(out=dest, in0=quo, scalar=-float(CAP), in1=pos, op0=ALU.mult,
                                                 op1=ALU.add))
                ch.link(dve.scalar_tensor_tensor(out=dest, in0=dest, scalar=float(NB), in1=blk, op0=ALU.mult,
                                                 op1=ALU.add))
                for t in range(NT):
                    ch.link(dve.tensor_tensor(sel[:, TOPK * t:TOPK * (t + 1)], onehot[:, TOPK * t:TOPK * (t + 1)],
                                              bcast_mid(dest[:, t], TOPK), ALU.mult))
                ch.link(dve.tensor_reduce(destf, sel, AX, ALU.add))
                dve.tensor_copy(desti[:], destf).then_inc(dest_ready, 1)
                ch.link(dve.tensor_tensor(ovcmp, bcast_mid(ovend, NOV + 1), bcast_inner(cn("iota_b"), E), ALU.is_le))
                ch.link(dve.tensor_reduce(ovexp, ovcmp, AX, ALU.add))
                ch.link(dve.tensor_scalar(ovexp, ovexp, float(E - 1), None, ALU.min))
                ch.link(dve.tensor_copy(ovexp_i[:, 0:NOV + 1], ovexp))
                dve.tensor_copy(ovexp_i[:, NOV + 1:NOV + 2], ovend[:, E - 1:E]).then_inc(dest_ready, 1)
                ch.end()

            @block.gpsimd
            def _(pool):
                pool.wait_ge(dest_ready, 1)
                pool.wait_ge(pads_out, 48)
                for n in range(NT * TOPK):
                    pool.indirect_dma_start(slot_rows, bass.IndirectOffsetOnAxis(ap=desti[:, n:n + 1], axis=0),
                                            pay[:, n, :], None).then_inc(slots_out, 16)
                pool.wait_ge(slots_out, 16 * NT * TOPK)

        with nc.Block() as block:
            def blocks(eng, body):
                many = eng.value_load(ovexp_i[0:1, NOV + 1:NOV + 2], min_val=0, max_val=NOV)
                with eng.Fori(0, E) as b:
                    body(b, b)
                with eng.Fori(0, NOV) as o:
                    with eng.If(o < many):
                        body(o + E, o)

            @block.sync
            def _(sp):
                sp.wait_ge(dest_ready, 2)
                many = sp.value_load(ovexp_i[0:1, NOV + 1:NOV + 2], min_val=0, max_val=NOV)

                def load(b, e):
                    for j in range(8):
                        sp.wait_ge(gu_ready.sem, gu_ready.at(b, j + 1))
                        sp.dma_start(w1_sb[:, j], w1[bass.ds(e, 1), j].rearrange("a p n -> (a p) n")).then_inc(
                            w1_in[j].sem, 16)
                    for k in range(8):
                        sp.wait_ge(w2_used.sem, w2_used.at(b, k + 1))
                        sp.dma_start(w2_sb[:, k], w2[bass.ds(e, 1), k].rearrange("a p n -> (a p) n")).then_inc(
                            w2_in[k].sem, 16)

                with sp.Fori(0, E - 1) as b:
                    load(b, b + 1)
                with sp.Fori(0, NOV) as o:
                    with sp.If(o < many):
                        load(o + (E - 1), sp.value_load(ovexp_i[0:1, bass.ds(o, 1)], min_val=0, max_val=E - 1))

            @block.tensor
            def _(pe):
                def turn_x(b):
                    pe.wait_ge(gather_in.sem, gather_in.at(b, 1))
                    pe.wait_ge(xt_read.sem, xt_read.at(b, 0))
                    for half in range(2):
                        for k in range(4):
                            c = (4 * half + k) * P
                            ins = pe.transpose(bank[4 + half][:, k * CAP:(k + 1) * CAP], xg[0:CAP, c:c + P],
                                               ident[0:CAP, 0:CAP])
                        ins.then_inc(xt_ready.sem, 1)

                def body(b, _):
                    pe.wait_ge(xt_read.sem, xt_read.at(b, 2))
                    for j in range(8):
                        pe.wait_ge(w1_in[j].sem, w1_in[j].at(b, 1))
                        pe.wait_ge(gu_read.sem, gu_read.at(b, max(j - 1, 0)))
                        w = w1_sb[:, j].rearrange("p (g k n) -> p g k n", g=2, k=KT)
                        for g in range(2):
                            for k in range(KT):
                                ins = pe.matmul(bank[j % 2][:, g * CAP:(g + 1) * CAP], w[:, g, k], xT[:, k],
                                                start=(k == 0), stop=(k == KT - 1))
                        ins.then_inc(gu_ready.sem, 1)
                    pe.wait_ge(yT_ready.sem, yT_ready.at(b, 0))
                    for k in range(8):
                        pe.wait_ge(w2_in[k].sem, w2_in[k].at(b, 1))
                        pe.wait_ge(act_ready.sem, act_ready.at(b, k + 1))
                        for d in range(KT):
                            ins = pe.matmul(bank[2 + d // 4][:, (d % 4) * CAP:(d % 4 + 1) * CAP],
                                            w2_sb[:, k, d * P:(d + 1) * P], actT[:, k],
                                            start=(k == 0 and d % 4 == 0), stop=(k == 7), skip_group_check=True)
                        ins.then_inc(w2_used.sem, 1)
                    turn_x(b + 1)
                    pe.wait_ge(yrow_ready.sem, yrow_ready.at(b, 0))
                    for half in range(2):
                        pe.wait_ge(yT_ready.sem, yT_ready.at(b, half + 1))
                        for k in range(4):
                            ins = pe.transpose(bank[6 + half][0:CAP, k * P:(k + 1) * P], yT[:, 4 * half + k], ident)
                        ins.then_inc(yt_ready.sem, 1)

                pe.wait_ge(dest_ready, 2)
                turn_x(0)
                blocks(pe, body)

            @block.scalar
            def _(act):
                def take_x(b):
                    for half in range(2):
                        act.wait_ge(xt_ready.sem, xt_ready.at(b, half + 1))
                        act.activation(xT[:, 4 * half:4 * half + 4],
                                       bank[4 + half][:, 0:4 * CAP].rearrange("p (a b) -> p a b", a=4),
                                       ACT.Copy).then_inc(xt_read.sem, 1)

                def body(b, _):
                    for j in range(8):
                        act.wait_ge(gate_ready.sem, gate_ready.at(b, j + 1))
                        act.wait_ge(act_ready.sem, act_ready.at(b, max(j - 1, 0)))
                        act.activation(s_buf[:, j % 2], g_buf[:, j % 2], ACT.Sigmoid,
                                       scale=SWIGLU_ALPHA).then_inc(swish_ready.sem, 1)
                    take_x(b + 1)
                    act.wait_ge(idx_ready.sem, idx_ready.at(b, 2))
                    for half in range(2):
                        act.wait_ge(yt_ready.sem, yt_ready.at(b, half + 1))
                        act.activation(y_rows[0:CAP, half * 512:(half + 1) * 512], bank[6 + half][0:CAP, :], ACT.Copy,
                                       scale=w_cur[:, 0:1]).then_inc(yrow_ready.sem, 1)

                act.wait_ge(dest_ready, 2)
                act.wait_ge(slots_in, 16)
                take_x(0)
                blocks(act, body)

            @block.vector
            def _(dve):
                ch = dve_moe

                def block_body(b, e):
                    ch.start(dve, b)
                    dve.wait_ge(yT_ready.sem, yT_ready.at(b, 0))
                    ch.link(dve.tensor_copy(b_cur, b12_sb[:, bass.ds(e * 24, 24)]))

                    def clamp(j):
                        dve.wait_ge(act_ready.sem, act_ready.at(b, max(j - 1, 0)))
                        dve.wait_ge(gu_ready.sem, gu_ready.at(b, j + 1))
                        dve.tensor_scalar(g_buf[:, j % 2], bank[j % 2][:, 0:CAP], b_cur[:, j:j + 1], SWIGLU_LIMIT,
                                          ALU.add, ALU.min).then_inc(gate_ready.sem, 1)
                        dve.tensor_scalar(u_buf[:, j % 2], bank[j % 2][:, CAP:2 * CAP], b_cur[:, 8 + j:9 + j],
                                          SWIGLU_LIMIT, ALU.add, ALU.min).then_inc(gu_read.sem, 1)
                        dve.wait_ge(gu_read.sem, gu_read.at(b, j + 1))
                        ch.link(dve.tensor_scalar(u_buf[:, j % 2], u_buf[:, j % 2], -SWIGLU_LIMIT, 1.0, ALU.max,
                                                  ALU.add))

                    def swiglu(j):
                        dve.wait_ge(swish_ready.sem, swish_ready.at(b, j + 1))
                        ch.link(dve.tensor_tensor(g_buf[:, j % 2], g_buf[:, j % 2], s_buf[:, j % 2], ALU.mult))
                        dve.tensor_tensor(actT[:, j], g_buf[:, j % 2], u_buf[:, j % 2], ALU.mult).then_inc(
                            act_ready.sem, 1)

                    clamp(0)
                    for j in range(1, 8):
                        clamp(j)
                        swiglu(j - 1)
                    swiglu(7)
                    dve.wait_ge(w2_used.sem, w2_used.at(b, 8))
                    dve.wait_ge(yt_ready.sem, yt_ready.at(b, 0))
                    for half in range(2):
                        dve.tensor_tensor(yT[:, 4 * half:4 * half + 4],
                                          bank[2 + half][:, 0:4 * CAP].rearrange("p (a b) -> p a b", a=4),
                                          bcast_inner(b_cur[:, 16 + 4 * half:20 + 4 * half], CAP),
                                          ALU.add).then_inc(yT_ready.sem, 1)
                    assert ch.n == ch.per_step, ("links per block", ch.n)

                def body(b, o):
                    if o is b:
                        block_body(b, b)
                    else:
                        block_body(b, dve.value_load(ovexp_i[0:1, bass.ds(o, 1)], min_val=0, max_val=E - 1))

                dve.wait_ge(dest_ready, 2)
                dve.wait_ge(b12_in, 16)
                blocks(dve, body)

            @block.gpsimd
            def _(pool):
                def carry_waits(n, b):
                    pool.wait_ge(spare_used[n].sem, spare_used[n].at(b, 0))
                    pool.tensor_tensor(spare[:, n:n + 1], spare[:, 2:3], spare[:, 2:3], ALU.add).then_inc(
                        spare_used[n].sem, 1)

                def gather(b):
                    pool.tensor_copy(g_idx[:], slots[:, bass.ds(b, 1), 0:1].rearrange("s a c -> s (a c)")).then_inc(
                        idx_ready.sem, 1)
                    pool.wait_ge(idx_ready.sem, idx_ready.at(b, 1))
                    carry_waits(0, b)
                    pool.indirect_dma_start(xg[0:CAP, :], None, h2_rows,
                                            bass.IndirectOffsetOnAxis(ap=g_idx[:, 0:1], axis=0)).then_inc(
                        gather_in.sem, 16)

                def body(b, _):
                    pool.wait_ge(yrow_ready.sem, yrow_ready.at(b, 0))
                    pool.tensor_copy(w_cur[:], slots[:].bitcast(F32)[:, bass.ds(b, 1), 1:2].rearrange("s a c -> s (a c)"))
                    pool.tensor_copy(s_idx[:], slots[:, bass.ds(b, 1), 0:1].rearrange("s a c -> s (a c)")).then_inc(
                        idx_ready.sem, 1)
                    pool.wait_ge(xt_ready.sem, xt_ready.at(b, 2))
                    gather(b + 1)
                    pool.wait_ge(yrow_ready.sem, yrow_ready.at(b, 2))
                    carry_waits(1, b)
                    pool.indirect_dma_start(out, bass.IndirectOffsetOnAxis(ap=s_idx[:, 0:1], axis=0),
                                            y_rows[0:CAP, :], None, compute_op=ALU.add).then_inc(
                        scatter_done.sem, 16)
                    pool.wait_ge(scatter_done.sem, scatter_done.at(b, 1))

                pool.memset(spare[:], 0).then_inc(spare_ready, 1)
                pool.wait_ge(spare_ready, 1)
                pool.wait_ge(slots_in, 16)
                pool.wait_ge(dest_ready, 2)
                pool.wait_ge(h2_out, 16 * NT)
                pool.wait_ge(x1_out, 16 * NT)
                gather(0)
                blocks(pool, body)


def toeplitz(rows):
    return bass.AP(tensor=rows.tensor, offset=rows.offset + (P - 1), ap=[[GL, HEADS], [-1, P], [1, 2 * P]])


def zero_rows(zeros):
    return zeros[0:CAP].unsqueeze(1).to_broadcast([CAP, D // 32, 32])


def constants():
    c = np.zeros((P, N_CONST), np.float32)
    r = np.arange(P)

    def put(name, a):
        o, w = CONST[name]
        c[:a.shape[0], o:o + w] = a

    put("ident", np.eye(P))
    put("tri", r[:, None] <= r[None, :])
    put("after", r[:, None] > r[None, :])
    put("ones", np.ones((P, P)))
    put("block", r[:, None] // HD == r[None, :] // HD)
    dist = np.maximum(2 * P - 1 - np.arange(GL), 0)
    exact = 16
    scaled = np.log(np.maximum(dist, 1).astype(np.float32) / exact) / np.float32(math.log(128 / exact))
    large = np.minimum(exact + (scaled * exact).astype(np.int32), 31)
    bucket = np.where(dist < exact, dist, large)
    onehot = (np.arange(32)[:, None] == bucket[None, :]).astype(np.float32)
    put("iota_e", np.tile(np.arange(E), (P, 1)))
    put("iota_b", np.tile(np.arange(NOV + 1), (P, 1)))
    ids = np.zeros((P, NT * TOPK, 2), np.int32)
    ids[:, :, 0] = np.arange(NT * TOPK)[None, :] // TOPK * P + r[:, None]
    pads = np.zeros((CAP, NB, 2), np.int32)
    pads[:, :, 0] = T + np.arange(CAP)[:, None]
    return c, onehot, ids.reshape(P, -1), pads.reshape(CAP, -1)


def lay_out(i):
    def rep(a):
        return np.broadcast_to(np.asarray(a).reshape(1, -1), (P, np.asarray(a).size))

    def cols(a):
        return np.asarray(a).reshape(-1, P).T

    parts = {"g_mix": cols(i["g_mix"]), "qg": np.tile(i["q_norm_g"][0], 2)[:, None],
             "kg": np.tile(i["k_norm_g"][0], 2)[:, None], "subg": i["attn_sub_g"][0][:, None],
             "lq1": rep(i["lambda_q1"]), "lk1": rep(i["lambda_k1"]), "lq2": rep(i["lambda_q2"]),
             "lk2": rep(i["lambda_k2"]), "dt_bias": rep(i["dt_bias"]), "a_log": rep(i["a_log"]),
             "d_skip": rep(i["d_skip"]), "b_router": rep(i["b_router"])}
    small = np.concatenate([parts[n] for n in SMALL], axis=1)
    w = np.asarray(i["w_in"][0]).reshape(KT, P, -1)
    q0, k0, v0, z0, x0, b0, c0, dt0, g0 = 0, 1024, 2048, 3072, 5120, 7168, 8192, 9216, 9248

    def step(n):
        starts = (x0 + n * GW, x0 + n * GW + P, b0 + n * P, c0 + n * P, q0 + n * P, k0 + n * P, g0 + n * P,
                  g0 + D + n * P)
        return np.stack([w[:, :, s:s + P] for s in starts])

    w_mix = np.stack([step(n) for n in range(HEADS)]).transpose(0, 3, 1, 2, 4).reshape(HEADS, P, CHT, KT * P)
    w_vz = np.stack([np.concatenate([w[:, :, v0 + n * P:v0 + (n + 1) * P], w[:, :, z0 + n * GW:z0 + (n + 1) * GW]], 2)
                     for n in range(HEADS)]).transpose(0, 2, 1, 3).reshape(HEADS, P, KT * VZ)
    w_dt = w[:, :, dt0:dt0 + SSM_H].transpose(1, 0, 2).reshape(P, -1)
    taps = np.concatenate([np.asarray(i["conv_w"][0]), np.asarray(i["conv_b"])])
    par = []
    for n in range(HEADS):
        tiles = [taps[:, s:s + P] for s in (n * GW, n * GW + P, 2048 + n * P, 3072 + n * P)]
        par += [t[j] for t in tiles for j in range(4)] + [t[4] for t in tiles]
        par += [np.asarray(i["ssm_norm_g"][0])[n * GW + j * P:n * GW + (j + 1) * P] for j in range(2)]
    par = np.stack(par, 1)
    wo = np.concatenate([np.asarray(i["w_attn_o"][0]), np.asarray(i["w_ssm_o"][0])])
    w_o = wo.reshape(3, KT, P, KT, P).transpose(3, 2, 0, 1, 4).reshape(KT, P, 3, KT * P)
    w_out = np.asarray(i["w_out"][0]).reshape(KT, P, D).transpose(1, 0, 2).reshape(P, -1)
    w_rt = np.asarray(i["w_router"][0]).reshape(KT, P, E).transpose(1, 0, 2).reshape(P, -1)
    w1 = np.asarray(i["w1"][0]).reshape(E, KT, P, 2, 8, P).transpose(0, 4, 2, 3, 1, 5).reshape(E, 8, P, 2 * D)
    w2 = np.asarray(i["w2"][0]).reshape(E, 8, P, D)
    b12 = np.concatenate([np.asarray(i["b1"][0]).reshape(E, 16, P), np.asarray(i["b2"][0]).reshape(E, 8, P)], 1)
    b12 = b12.transpose(2, 0, 1).reshape(P, -1)
    consts, onehot, ids, pads = constants()
    return {"x": i["x"], "small": small, "consts": consts, "onehot": onehot, "gffn": rep(i["g_ffn"]), "rel_bias": i["rel_bias"],
            "par": par, "w_mix": w_mix, "w_vz": w_vz, "w_dt": w_dt, "w_o": w_o, "w_out": w_out, "w_rt": w_rt,
            "w1": w1, "w2": w2, "b12": b12, "tok_ids": ids, "pads": pads}


def kernel(**inputs):
    import concourse.bacc as bacc
    from concourse.bass_utils import run_bass_kernel_spmd as run

    nc = bacc.Bacc("TRN2", target_bir_lowering=False, num_devices=1)
    arrays, args = {}, []
    for name, a in lay_out(inputs).items():
        a = np.ascontiguousarray(a)
        arrays[f"in_{name}"] = a
        args.append(nc.dram_tensor(f"in_{name}", a.shape, mybir.dt.from_np(a.dtype), kind="ExternalInput").ap())
    args.append(nc.dram_tensor("out_rows", (ROWS, D), F32, kind="ExternalOutput").ap())
    decoder_layer(nc, *args)
    r = run(nc, [arrays], core_ids=[0])
    return r.results[0]["out_rows"][:T].reshape(1, T, D)
```

```python
import math
from contextlib import ExitStack

import numpy as np
import concourse.bass as bass
from concourse import mybir

F32 = mybir.dt.float32
F32R = mybir.dt.float32r
I32 = mybir.dt.int32
U32 = mybir.dt.uint32
ALU = mybir.AluOpType
ACT = mybir.ActivationFunctionType
AX = mybir.AxisListType.X

P = 128
D = 1024
T = 512
KT = D // P
NT = T // P
HEADS = 8
HD = 64
HPG = 4
SSM_H = 32
GW = 256
VZ = P + GW
CHT = 8
NPAR = 22
E = 32
TOPK = 4
CAP = 128
MAXQ = (T - 1) // CAP
NOV = (T * TOPK) // CAP
NB = E + NOV + 1
SLABS = 24
RAW, SPLIT = 12, 6
ROWS = T + CAP
RMS_EPS = 1e-6
SSM_EPS = 1e-5
LAMBDA_INIT = 0.8 - 0.6 * math.exp(0.0)
SWIGLU_LIMIT = 7.0
SWIGLU_ALPHA = 1.702
NEG = -1e30
GL = 384

SMALL = {}
_o = 0
for _n, _w in (("g_mix", KT), ("qg", 1), ("kg", 1), ("subg", 1), ("lq1", HD), ("lk1", HD), ("lq2", HD),
               ("lk2", HD), ("dt_bias", SSM_H), ("a_log", SSM_H), ("d_skip", SSM_H), ("b_router", E)):
    SMALL[_n] = (_o, _w)
    _o += _w
N_SMALL = _o
CONST = {}
_o = 0
for _n, _w in (("ident", P), ("tri", P), ("after", P), ("ones", P), ("block", P),
               ("iota_e", E), ("iota_b", NOV + 1), ("pick", E)):
    CONST[_n] = (_o, _w)
    _o += _w
N_CONST = _o


class Signal:

    def __init__(self, sem, per_step=1, unit=1):
        self.sem, self.per_step, self.unit = sem, per_step, unit
        self.first = 1 if unit == 1 else 0

    def at(self, step, k):
        assert k > 0 or self.first or not isinstance(step, int) or step > 0
        return step * (self.per_step * self.unit) + (k * self.unit + self.first)


def prime(eng, *signals):
    for s in signals:
        eng.sem_inc(s.sem, 1)


class Chain:

    def __init__(self, sem, per_step=0):
        self.sem, self.per_step, self.base, self.n = sem, per_step, 0, 0
        self.eng = self.step = None

    def start(self, eng, step=None):
        self.eng, self.step, self.n = eng, step, 0

    def link(self, ins):
        self.n += 1
        ins.then_inc(self.sem, 1)
        at = self.base + self.n
        self.eng.wait_ge(self.sem, at if self.step is None else self.step * self.per_step + at)

    def end(self, steps=1):
        if self.step is not None:
            assert self.n == self.per_step, ("links per step", self.n, self.per_step)
        self.base += self.n * steps
        self.n = 0


class Arena:

    def __init__(self, tensor, size):
        self.t, self.size, self.at = tensor, size, 0

    def reset(self, at=0):
        self.at = at

    def take(self, *shape):
        n = int(np.prod(shape))
        assert self.at + n <= self.size, ("arena", self.at + n, self.size)
        v = self.t[:, self.at:self.at + n]
        self.at += n
        if len(shape) == 2:
            v = v.rearrange("p (a b) -> p a b", a=shape[0])
        elif len(shape) == 3:
            v = v.rearrange("p (a b c) -> p a b c", a=shape[0], b=shape[1])
        return v


def apart(eng, sem):
    eng.wait_ge(sem, 80)


def bcast_inner(ap, n):
    return ap.unsqueeze(2).to_broadcast([ap.shape[0], ap.shape[1], n])


def bcast_mid(ap, n):
    return ap.unsqueeze(1).to_broadcast([ap.shape[0], n, ap.shape[1]])


DVE_LINKS, ACT_LINKS, MOE_LINKS = 40, 21, 4


def decoder_layer(nc, x, small, consts, onehot_rows, gffn, rel_bias, par, w_mix, w_vz, w_dt, w_o, w_out, w_rt, w1, w2, b12,
                  tok_ids, pads, out):
    with ExitStack() as ctx:
        def sb(name, shape, dt=F32):
            return ctx.enter_context(nc.sbuf_tensor(name, shape, dt))

        def sem(name):
            return ctx.enter_context(nc.semaphore(name))

        def sig(name, per_step=1, unit=1):
            return Signal(sem(name), per_step, unit)

        h2_rows = nc.dram_tensor("h2_rows", (ROWS, D), F32, kind="Internal").ap()
        dist_rows = nc.dram_tensor("dist_rows", (HEADS, GL), F32, kind="Internal").ap()
        bias_rows = nc.dram_tensor("bias_rows", (HEADS, P, 2 * P), F32, kind="Internal").ap()
        slot_rows = nc.dram_tensor("slot_rows", (CAP * NB, 2), I32, kind="Internal").ap()

        bank = [ctx.enter_context(nc.psum_tensor(f"bank{b}", [P, 512], F32)) for b in range(8)]
        proj_b = bank[0:2]
        s_b = bank[2:4]
        m0_b, m1_b, seg_b, y_b = bank[4:8]

        big = sb("big", [P, 24576])
        big_base = nc.sbuf_base - 4 * 24576
        keep = sb("keep", [P, 23552])
        keep_base = nc.sbuf_base - 4 * 23552
        smalls = sb("smalls", [P, N_SMALL])
        cst = sb("cst", [P, N_CONST])
        eps = sb("eps", [P, 4])
        lam_t = sb("lam_t", [P, HD + 4])

        def sm(name):
            o, w = SMALL[name]
            return smalls[:, o:o + w]

        def cn(name, a=0, n=None):
            o, w = CONST[name]
            return cst[:, o + a:o + (w if n is None else a + n)]

        ident, tri, after, ones, block_ones = cn("ident"), cn("tri"), cn("after"), cn("ones"), cn("block")
        loop_mem, keep_mem = Arena(big, 24576), Arena(keep, 23552)
        par_sb = sb("par_sb", [P, HEADS * NPAR])
        far = sb("far", [P, HEADS])

        attnT = keep_mem.take(HEADS, T)
        ssmT = keep_mem.take(2 * HEADS, T)
        gateT = keep_mem.take(2, HEADS, T)
        wo_sb = keep_mem.take(3, KT, P)
        hT = loop_mem.take(KT, T)
        wm_sb = loop_mem.take(CHT, KT, P)
        wvz_sb = loop_mem.take(KT, VZ)
        loop_mark = loop_mem.at
        conv = loop_mem.take(4, T)
        xb = loop_mem.take(NT, 3 * P)
        qk = loop_mem.take(2, T)
        vz = loop_mem.take(NT, VZ)
        aux = sb("aux", [P, 2048])
        aux_mem = Arena(aux, 2048)
        L = aux_mem.take(2, T)
        diff = aux_mem.take(T)
        am = aux_mem.take(HPG, P)
        ext_mem = Arena(keep, 23552)
        ext_mem.reset(23552 - 3 * KT * P)
        sqx = keep[:, 23552 - 3 * KT * P:23552 - 3 * KT * P + D]
        sq = ext_mem.take(2, T)
        decay = ext_mem.take(HPG, P)
        mix = ext_mem.take(HPG, P)
        state = ext_mem.take(GW)
        xdt = ext_mem.take(GW)
        xw = ext_mem.take(GW)
        xd = ext_mem.take(GW)
        st = sb("st", [P, 32])
        yn = sb("yn", [P, GW])
        biasT = sb("biasT", [P, GW])
        dT = loop_mem.take(NT, T)
        ez = loop_mem.take(GW)
        ybuf = loop_mem.take(GW)
        ytmp = loop_mem.take(GW)
        cbm = loop_mem.take(P)
        dtv = sb("dtv", [P, NT, SSM_H])
        a_all = sb("a_all", [P, NT, SSM_H])
        eacum = sb("eacum", [P, NT, SSM_H])
        wend = sb("wend", [P, NT, SSM_H])
        eaend = sb("eaend", [P, NT, SSM_H])

        consts_in, x_in, wdt_in = sem("consts_in"), [sem(f"x_in{t}") for t in range(NT)], sem("wdt_in")
        h_ready, hT_banks, hT_read = sem("h_ready"), sem("hT_banks"), sem("hT_read")
        dt_ready, dt_read, a_ready, cums_ready, decays_ready = (
            sem("dt_ready"), sem("dt_read"), sem("a_ready"), sem("cums_ready"), sem("decays_ready"))
        dist_ready, dist_read, dist_out, lam_ready = sem("dist_ready"), sem("dist_read"), sem("dist_out"), sem("lam_ready")
        w_in_sig = [sig(f"w_tile{n}_in", 1, 16) for n in range(CHT)]
        wvz_in = sig("wvz_in", 1, 16)
        bias_in = sig("bias_in", 1, 16)
        proj_done = sig("proj_done", 12)
        taps_ready = sig("taps_ready", 4)
        conv_ready = sig("conv_ready", 4)
        silu_ready = sig("silu_ready", 4)
        proj_read = sig("proj_read", 8)
        z_ready = sig("z_ready", 4)
        sums_ready = sig("sums_ready", 2)
        root_ready = sig("root_ready", 2)
        qk_ready = sig("qk_ready", 2)
        m0_ready, m0_read = sig("m0_ready", 12), sig("m0_read", 12)
        m1_ready, m1_read = sig("m1_ready", 8), sig("m1_read", 8)
        am_ready = sig("am_ready", 4)
        xs_ready = sig("xs_ready", 4)
        seg_ready, decay_ready = sig("seg_ready", 4), sig("decay_ready", 4)
        scores_ready, logits_ready = sig("scores_ready", 4), sig("logits_ready", 4)
        max_ready, exp_ready, diff_ready = sig("max_ready", 4), sig("exp_ready", 4), sig("diff_ready", 4)
        cbm_ready, mix_ready = sig("cbm_ready", 4), sig("mix_ready", 4)
        ydiag_ready, y_read, y_ready, yn_ready = (sig("ydiag_ready", 4), sig("y_read", 4), sig("y_ready", 4),
                                                  sig("yn_ready", 4))
        osq_ready, osum_ready, oroot_ready = sig("osq_ready"), sig("osum_ready"), sig("oroot_ready")
        dve_step, act_step = Chain(sem("dve_step")), Chain(sem("act_step"))
        dve_loop, act_loop = Chain(sem("dve_loop"), DVE_LINKS), Chain(sem("act_loop"), ACT_LINKS)
        sigm_ready = sem("sigm_ready")
        wo_in = [sig(f"wo_in{n}", 1, 16) for n in range(3)]
        attn_out_ready, ssm_out_ready = sig("attn_out_ready"), sig("ssm_out_ready")
        attn_out_read, ssm_out_read, merged_ready = sig("attn_out_read"), sig("ssm_out_read"), sig("merged_ready")
        dve_merge = Chain(sem("dve_merge"), 0)
        wout_in, gffn_in, xr_in = sem("wout_in"), sem("gffn_in"), [sem(f"xr_in{t}") for t in range(NT)]
        res_ready, x1_ready, x1n_ready, h2_ready = sem("res_ready"), sem("x1_ready"), sem("x1n_ready"), sem("h2_ready")
        x1_out, h2_out, pads_out, zero_ready = sem("x1_out"), sem("h2_out"), sem("pads_out"), sem("zero_ready")
        h2T_ready, h2T_read, logit_ready = sem("h2T_ready"), sem("h2T_read"), sem("logit_ready")
        rt_exp, mask_ready, pos_ready, dest_ready, wrt_in = (
            sem("rt_exp"), sem("mask_ready"), sem("pos_ready"), sem("dest_ready"), sem("wrt_in"))
        slots_out, slots_in = sem("slots_out"), sem("slots_in")
        raw_in = [sem(f"raw_in{n}") for n in range(RAW)]
        hi_ready, lo_ready, slab_used = sig("hi_ready"), sig("lo_ready"), sig("slab_used")
        gather_in, scatter_done = sig("gather_in", 1, 16), sig("scatter_done", 1, 16)
        tx_ready, xh_ready, xl_ready = sig("tx_ready", 2), sig("xh_ready", 2), sig("xl_ready", 2)
        ta_ready, ah_ready, al_ready = sig("ta_ready", 2), sig("ah_ready", 2), sig("al_ready", 2)
        g_ready, s_ready, act_ready, yrow_ready = (sig("g_ready", 2), sig("s_ready", 2), sig("act_ready", 2),
                                                   sig("yrow_ready", 2))
        gidx_ready, sidx_ready, pick_ready = sig("gidx_ready"), sig("sidx_ready"), sig("pick_ready", 2)
        bias_ready = sem("bias_ready")
        dve_moe = Chain(sem("dve_moe"), MOE_LINKS)

        raw = big[:, 0:RAW * D].rearrange("p (s n) -> p s n", s=RAW)
        wout_sb = big[:, 8 * 2048:24576].rearrange("p (k n) -> p k n", k=8)
        tail = Arena(big, 16384)
        tail.reset(12288)
        xr_sb, gffn_sb, wrt_sb = tail.take(2, D), tail.take(D), tail.take(KT, E)
        zeros = tail.take(32)
        x1_buf = keep[:, 0:2048].rearrange("p (a n) -> p a n", a=2)
        h2_buf = keep[:, 2048:4096].rearrange("p (a n) -> p a n", a=2)
        route_mem = Arena(keep, 12288)
        route_mem.reset(4096 + 4096)
        h2T = route_mem.take(KT, P)
        rt = Arena(keep, 23552)
        rt.reset(12288 + 4096)
        lg, onehot, mask, pos, quo = (rt.take(NT, E), rt.take(NT * TOPK, E), rt.take(NT, E), rt.take(NT, E),
                                      rt.take(NT, E))
        blk, dest, sel = rt.take(NT, E), rt.take(NT, E), rt.take(NT * TOPK, E)
        mv, mif, wgt, wsum, cnt, ov, ova, ovb, ovbase = (
            rt.take(NT, 8), rt.take(NT, TOPK), rt.take(NT, TOPK), rt.take(NT), rt.take(E), rt.take(E), rt.take(E),
            rt.take(E), rt.take(E))
        ovcmp, ovexp, destf = rt.take(NOV + 1, E), rt.take(NOV + 1), rt.take(NT * TOPK)
        mi = sb("mi", [P, NT, 8], U32)
        desti = sb("desti", [P, NT * TOPK], I32)
        pay = sb("pay", [P, NT * TOPK, 2], I32)
        slots = sb("slots", [CAP, NB, 2], I32)
        blk_exp = sb("blk_exp", [P, NB + 1], I32)
        ex = Arena(keep, 8192)
        xg, act_rows, y_rows = ex.take(D), ex.take(D), ex.take(D)
        g_buf, u_buf, s_buf = ex.take(2, 512), ex.take(2, 512), ex.take(2, 512)
        b12_raw = keep[:, 20480:20480 + 3 * D]

        def parts(name, shape, base, at):
            return nc.alloc_sbuf_tensor_at(name, shape, F32R, offset=base + 4 * at)

        w_hi = parts("w_hi", [P, SPLIT, D], big_base, RAW * D)
        w_lo = parts("w_lo", [P, SPLIT, D], big_base, (RAW + SPLIT) * D)
        x_hi, x_lo = parts("x_hi", [P, KT, P], keep_base, 9216), parts("x_lo", [P, KT, P], keep_base, 9216 + D)
        a_hi, a_lo = parts("a_hi", [P, KT, P], keep_base, 9216 + 2 * D), parts("a_lo", [P, KT, P], keep_base, 9216 + 3 * D)
        bias_hl = parts("bias_hl", [2 * E, 3 * D], keep_base, 13312)
        pick1, pick2 = parts("pick1", [2 * E, P], keep_base, 8192), parts("pick2", [2 * E, P], keep_base, 8192 + P)
        spare = sb("spare", [CAP, 3])
        spare_used = [sig("spare_used0"), sig("spare_used1")]
        g_idx, s_idx = sb("g_idx", [CAP, 1], I32), sb("s_idx", [CAP, 1], I32)
        w_cur = sb("w_cur", [CAP, 1])
        b12_in, spare_ready = sem("b12_in"), sem("spare_ready")

        x_rows = x.rearrange("a s d -> (a s) d")

        with nc.Block() as block:
            MIX_ORDER = (1, 2, 3, 4, 5, 6, 11, 12)

            @block.sync
            def _(sp):
                sp.dma_start(cst[:], consts).then_inc(consts_in, 16)
                sp.dma_start(smalls[:], small).then_inc(consts_in, 16)
                xin = wm_sb.rearrange("p a b c -> p (a b c)")
                for t in range(NT):
                    sp.dma_start(xin[:, t * D:(t + 1) * D], x_rows[t * P:(t + 1) * P, :]).then_inc(x_in[t], 16)
                sp.dma_start(dT.rearrange("p a b -> p (a b)")[:, 0:KT * SSM_H], w_dt).then_inc(wdt_in, 16)
                sp.dma_start(par_sb[:], par).then_inc(consts_in, 16)
                sp.dma_start(conv.rearrange("p a b -> p (a b)")[0:32, 0:HEADS], rel_bias).then_inc(consts_in, 16)
                sp.dma_start(conv[0:32, 2, 0:GL], onehot_rows).then_inc(consts_in, 16)
                sp.dma_start(wvz_sb.rearrange("p a b -> p (a b)"), w_vz[0]).then_inc(wvz_in.sem, 16)
                sp.wait_ge(dist_read, 1)
                sp.dma_start(dist_rows, conv[0:HEADS, 1, 0:GL]).then_inc(dist_out, 16)
                sp.wait_ge(dist_out, 16)
                sp.dma_start(bias_rows, toeplitz(dist_rows)).then_inc(dist_out, 16)
                sp.wait_ge(dist_out, 32)
                sp.wait_ge(hT_banks, 2 * NT)
                for n in range(CHT):
                    sp.dma_start(wm_sb[:, n].rearrange("p a b -> p (a b)"), w_mix[0, :, n]).then_inc(
                        w_in_sig[n].sem, 16)
                sp.dma_start(biasT[:], bias_rows[0]).then_inc(bias_in.sem, 16)
                with sp.Fori(0, HEADS - 1) as i:
                    for n in range(6):
                        sp.wait_ge(proj_done.sem, proj_done.at(i, MIX_ORDER[n]))
                        sp.dma_start(wm_sb[:, n].rearrange("p a b -> p (a b)"),
                                     w_mix[bass.ds(i + 1, 1), :, n].rearrange("a p n -> (a p) n")).then_inc(
                            w_in_sig[n].sem, 16)
                    sp.wait_ge(proj_done.sem, proj_done.at(i, 10))
                    sp.dma_start(wvz_sb.rearrange("p a b -> p (a b)"),
                                 w_vz[bass.ds(i + 1, 1)].rearrange("a p n -> (a p) n")).then_inc(wvz_in.sem, 16)
                    sp.wait_ge(logits_ready.sem, logits_ready.at(i, 4))
                    sp.dma_start(biasT[:], bias_rows[bass.ds(i + 1, 1)].rearrange("a p n -> (a p) n")).then_inc(bias_in.sem, 16)
                    for n in (6, 7):
                        sp.wait_ge(proj_done.sem, proj_done.at(i, MIX_ORDER[n]))
                        sp.dma_start(wm_sb[:, n].rearrange("p a b -> p (a b)"),
                                     w_mix[bass.ds(i + 1, 1), :, n].rearrange("a p n -> (a p) n")).then_inc(
                            w_in_sig[n].sem, 16)

                sp.wait_ge(m0_read.sem, m0_read.at(HEADS, 0))
                sp.wait_ge(m1_read.sem, m1_read.at(HEADS, 0))
                for n in range(3):
                    sp.dma_start(wo_sb[:, n].rearrange("p a b -> p (a b)"), w_o[0, :, n]).then_inc(wo_in[n].sem, 16)

            @block.gpsimd
            def _(pool):
                prime(pool, am_ready, xs_ready, gidx_ready, sidx_ready, pick_ready, *spare_used)
                pool.wait_ge(decays_ready, 3)
                with pool.Fori(0, HEADS) as i:
                    h4 = i * HPG

                    def heads(table, u):
                        return table[:, u, bass.ds(h4, HPG)]

                    def make_am(u):
                        pool.wait_ge(seg_ready.sem, seg_ready.at(i, u))
                        pool.tensor_tensor(am, bcast_mid(tri, HPG), bcast_inner(heads(a_all, u), P),
                                           ALU.mult).then_inc(am_ready.sem, 1)

                    def make_xs(u):
                        pool.wait_ge(m0_read.sem, m0_read.at(i, u + 1))
                        pool.wait_ge(m1_ready.sem, m1_ready.at(i, min(2 * u, 6)))
                        pool.wait_ge(ydiag_ready.sem, ydiag_ready.at(i, u))
                        pool.wait_ge(y_read.sem, y_read.at(i, u))
                        xv = xb[:, u, 0:GW].rearrange("p (h c) -> p h c", h=HPG)
                        for dst, src in ((xdt, heads(dtv, u)), (xw, heads(wend, u))):
                            pool.tensor_tensor(dst.rearrange("p (h c) -> p h c", h=HPG), xv,
                                               bcast_inner(src, HD), ALU.mult)
                        dsk = SMALL["d_skip"][0]
                        pool.tensor_tensor(xd.rearrange("p (h c) -> p h c", h=HPG), xv,
                                           bcast_inner(smalls[:, bass.ds(h4 + dsk, HPG)], HD),
                                           ALU.mult).then_inc(xs_ready.sem, 1)

                    for u in range(NT):
                        make_am(u)
                        make_xs(u)

            @block.scalar
            def _(act):
                prime(act, taps_ready, silu_ready, proj_read, root_ready, m0_read, decay_ready, exp_ready, yn_ready,
                      osq_ready, oroot_ready, hi_ready, xh_ready, ah_ready, s_ready, yrow_ready)
                ch = act_step
                ch.start(act)
                act.preload_act_table_set("natural_log_exp_and_others")
                xin = wm_sb.rearrange("p a b c -> p (a b c)")

                act.wait_ge(consts_in, 80)
                act.wait_ge(lam_ready, 1)
                for t in range(NT):
                    xt = xin[:, t * D:(t + 1) * D]
                    act.wait_ge(x_in[t], 16)
                    ch.link(act.activation(sqx, xt, ACT.Square, accum_out=st[:, t:t + 1]))
                    ch.link(act.activation(st[:, t:t + 1], st[:, t:t + 1], ACT.Ln, bias=eps[:, 0:1], scale=1.0 / D))
                    ch.link(act.activation(st[:, t:t + 1], st[:, t:t + 1], ACT.Exp, scale=-0.5))
                    act.activation(xt, xt, ACT.Copy, scale=st[:, t:t + 1]).then_inc(h_ready, 1)
                act.wait_ge(lam_ready, 2)
                ch.link(act.activation(lam_t[:, HD:HD + 2], lam_t[:, HD:HD + 2], ACT.Exp))
                act.activation(ez[:, 0:SSM_H], sm("a_log"), ACT.Exp).then_inc(lam_ready, 1)
                act.wait_ge(dt_read, 1)
                ch.link(act.activation(eacum[:], wend[:], ACT.Exp, scale=-1.0))
                act.activation(eacum[:], eacum[:], ACT.Ln, bias=1.0).then_inc(dt_read, 1)
                act.wait_ge(cums_ready, 1)
                cum = y_b[:, 0:384].rearrange("p (k c h) -> p k c h", k=3, c=NT)
                act.activation(eacum[:], cum[:, 0], ACT.Exp).then_inc(decays_ready, 1)
                act.activation(wend[:], cum[:, 1], ACT.Exp)
                act.activation(eaend[:], cum[:, 2], ACT.Exp).then_inc(decays_ready, 1)
                ch.end()

                ch = act_loop
                with act.Fori(0, HEADS) as i:
                    ch.start(act, i)

                    def tap(n):
                        act.wait_ge(proj_done.sem, proj_done.at(i, n + 1))
                        act.wait_ge(m0_ready.sem, m0_ready.at(i, 0))
                        apart(act, consts_in)
                        p0 = i * NPAR
                        act.activation(conv[:, n], proj_b[n % 2][:], ACT.Identity,
                                       scale=par_sb[:, bass.ds(p0 + (4 * n + 3), 1)],
                                       bias=par_sb[:, bass.ds(p0 + (16 + n), 1)]).then_inc(taps_ready.sem, 1)

                    def silu(n):
                        act.wait_ge(conv_ready.sem, conv_ready.at(i, n + 1))
                        act.activation(conv[:, n], conv[:, n], ACT.Silu).then_inc(silu_ready.sem, 1)

                    def squares(n):
                        act.wait_ge(proj_done.sem, proj_done.at(i, 5 + n))
                        act.wait_ge(scores_ready.sem, scores_ready.at(i, 0))
                        act.wait_ge(m1_read.sem, m1_read.at(i, 0))
                        ch.link(act.activation(qk[:, n], proj_b[n][:], ACT.Copy))
                        act.activation(sq[:, n], proj_b[n][:], ACT.Square).then_inc(proj_read.sem, 1)

                    def root(n):
                        act.wait_ge(sums_ready.sem, sums_ready.at(i, n + 1))
                        ch.link(act.activation(sq[:, n], s_b[n][:], ACT.Ln, bias=eps[:, 0:1], scale=1.0 / HD))
                        act.activation(sq[:, n], sq[:, n], ACT.Exp, scale=-0.5).then_inc(root_ready.sem, 1)

                    def take_vz(t):
                        act.wait_ge(proj_done.sem, proj_done.at(i, 7 + t))
                        if t:
                            act.wait_ge(z_ready.sem, z_ready.at(i, t))
                        else:
                            act.wait_ge(m1_ready.sem, m1_ready.at(i, 0))
                            act.wait_ge(y_ready.sem, y_ready.at(i, 0))
                        ch.link(act.activation(vz[:, t], proj_b[t % 2][:, 0:VZ], ACT.Copy))
                        act.activation(ez, proj_b[t % 2][:, P:VZ], ACT.Exp, scale=-1.0).then_inc(proj_read.sem, 1)

                    def take_xb(u):
                        act.wait_ge(m0_ready.sem, m0_ready.at(i, u + 1))
                        act.wait_ge(xs_ready.sem, xs_ready.at(i, 0))
                        act.activation(xb[:, u], m0_b[:, 0:3 * P], ACT.Copy).then_inc(m0_read.sem, 1)

                    def make_decay(u):
                        act.wait_ge(seg_ready.sem, seg_ready.at(i, u + 1))
                        act.wait_ge(mix_ready.sem, mix_ready.at(i, u))
                        act.activation(decay.rearrange("p a b -> p (a b)"), seg_b[:], ACT.Exp).then_inc(
                            decay_ready.sem, 1)

                    def softmax_exp(u):
                        n = (u + 1) * P
                        act.wait_ge(max_ready.sem, max_ready.at(i, u + 1))
                        for m in range(2):
                            ins = act.activation(L[:, m, 0:n], L[:, m, 0:n], ACT.Exp, bias=st[:, 8 + m:9 + m],
                                                 accum_out=st[:, 10 + m:11 + m])
                        ins.then_inc(exp_ready.sem, 1)

                    def take_diff(u, k):
                        act.wait_ge(m0_ready.sem, m0_ready.at(i, k))
                        act.wait_ge(m1_ready.sem, m1_ready.at(i, 0))
                        src = m0_b[:, 0:(u + 1) * P].rearrange("p (a b) -> p a b", a=u + 1)
                        act.activation(dT[:, 0:u + 1, u * P:(u + 1) * P], src, ACT.Copy).then_inc(m0_read.sem, 1)

                    def norm_y(u, k):
                        act.wait_ge(y_ready.sem, y_ready.at(i, u + 1))
                        act.wait_ge(m0_ready.sem, m0_ready.at(i, k))
                        ch.link(act.activation(yn[:], ybuf, ACT.Square, accum_out=st[:, 16:17]))
                        ch.link(act.activation(st[:, 16:17], st[:, 16:17], ACT.Ln, bias=eps[:, 1:2], scale=1.0 / GW))
                        ch.link(act.activation(st[:, 16:17], st[:, 16:17], ACT.Exp, scale=-0.5))
                        act.activation(yn[:], ybuf, ACT.Copy, scale=st[:, 16:17]).then_inc(yn_ready.sem, 1)

                    def take_y(u, k):
                        act.wait_ge(m0_ready.sem, m0_ready.at(i, k))
                        apart(act, consts_in)
                        for j in range(2):
                            dst = ssmT[:, bass.ds(i * 2 + j, 1), u * P:(u + 1) * P].rearrange("p a b -> p (a b)")
                            ins = act.activation(dst, m0_b[:, j * P:(j + 1) * P], ACT.Copy,
                                                 scale=par_sb[:, bass.ds(i * NPAR + (20 + j), 1)])
                        ins.then_inc(m0_read.sem, 1)

                    def take_gate(n):
                        act.wait_ge(proj_done.sem, proj_done.at(i, 11 + n))
                        apart(act, consts_in)
                        dst = gateT[:, n, bass.ds(i, 1), :].rearrange("p a b -> p (a b)")
                        act.activation(dst, proj_b[n][:], ACT.Copy).then_inc(proj_read.sem, 1)

                    tap(0)
                    tap(1)
                    silu(0)
                    tap(2)
                    silu(1)
                    tap(3)
                    silu(2)
                    silu(3)
                    act.preload_act_table_set("natural_log_exp_and_others")
                    squares(0)
                    squares(1)
                    take_vz(0)
                    take_xb(0)
                    make_decay(0)
                    take_xb(1)
                    take_xb(2)
                    root(0)
                    take_xb(3)
                    root(1)
                    make_decay(1)
                    take_vz(1)
                    norm_y(0, 0)
                    softmax_exp(0)
                    take_vz(2)
                    softmax_exp(1)
                    make_decay(2)
                    take_diff(0, 5)
                    take_vz(3)
                    take_diff(1, 6)
                    take_y(0, 7)
                    softmax_exp(2)
                    norm_y(1, 7)
                    take_diff(2, 8)
                    make_decay(3)
                    softmax_exp(3)
                    take_gate(0)
                    take_y(1, 9)
                    norm_y(2, 9)
                    take_diff(3, 10)
                    take_y(2, 11)
                    norm_y(3, 11)
                    act.wait_ge(m1_ready.sem, m1_ready.at(i, 8))
                    act.activation(sq[:, 0], m1_b[:], ACT.Square).then_inc(osq_ready.sem, 1)
                    take_gate(1)
                    act.wait_ge(osum_ready.sem, osum_ready.at(i, 1))
                    ch.link(act.activation(sq[:, 1], s_b[0][:], ACT.Ln, bias=eps[:, 0:1], scale=1.0 / P))
                    act.activation(sq[:, 1], sq[:, 1], ACT.Exp, scale=-0.5).then_inc(oroot_ready.sem, 1)
                    take_y(3, 12)
                ch.end(HEADS)

            @block.vector
            def _(dve):
                prime(dve, conv_ready, z_ready, qk_ready, m1_read, logits_ready, max_ready, diff_ready, cbm_ready,
                      mix_ready, y_read, y_ready, attn_out_read, ssm_out_read, merged_ready, lo_ready, xl_ready,
                      al_ready, g_ready, act_ready)
                ch = dve_step
                ch.start(dve)
                dve.memset(eps[:, 0:1], RMS_EPS)
                ch.link(dve.memset(eps[:, 1:2], SSM_EPS))
                dve.wait_ge(consts_in, 80)
                ch.link(dve.tensor_scalar(sm("qg"), sm("qg"), HD ** -0.5, None, ALU.mult))
                dve.tensor_scalar(sm("subg"), sm("subg"), 1.0 - LAMBDA_INIT, None, ALU.mult).then_inc(lam_ready, 1)
                ch.link(dve.tensor_tensor_reduce(lam_t[:, 0:HD], sm("lq1"), sm("lk1"), 1.0, 0.0, ALU.mult, ALU.add,
                                                 lam_t[:, HD:HD + 1]))
                dve.tensor_tensor_reduce(lam_t[:, 0:HD], sm("lq2"), sm("lk2"), 1.0, 0.0, ALU.mult, ALU.add,
                                         lam_t[:, HD + 1:HD + 2]).then_inc(lam_ready, 1)
                dve.wait_ge(dist_ready, 1)
                ch.link(dve.tensor_copy(conv[0:HEADS, 1, 0:GL], s_b[0][0:HEADS, 0:GL]))
                ch.link(dve.tensor_copy(far[:], s_b[1][:, 0:HEADS]))
                dve.memset(conv[0:HEADS, 1, 256:GL], NEG).then_inc(dist_read, 1)
                dve.wait_ge(lam_ready, 3)
                ch.link(dve.tensor_tensor(eps[:, 2:3], lam_t[:, HD + 1:HD + 2], lam_t[:, HD:HD + 1], ALU.subtract))
                ch.link(dve.tensor_scalar(eps[:, 2:3], eps[:, 2:3], -LAMBDA_INIT, None, ALU.add))
                for b in range(2 * NT):
                    t, half = b // 2, b % 2
                    dve.wait_ge(hT_banks, b + 1)
                    dve.tensor_tensor(hT[:, 4 * half:4 * half + 4, t * P:(t + 1) * P],
                                      bank[b % 2][:].rearrange("p (a b) -> p a b", a=4),
                                      bcast_inner(smalls[:, 4 * half:4 * half + 4], P), ALU.mult).then_inc(hT_read, 1)
                dve.wait_ge(dt_ready, 1)
                dproj = m0_b[:, 0:NT * SSM_H].rearrange("p (c h) -> p c h", c=NT)
                ch.link(dve.tensor_tensor(dtv[:], dproj, bcast_mid(sm("dt_bias"), NT), ALU.add))
                ch.link(dve.tensor_scalar(a_all[:], dtv[:], -1.0, None, ALU.mult))
                ch.link(dve.tensor_scalar(eaend[:], dtv[:], 0.0, None, ALU.max))
                dve.tensor_tensor(wend[:], dtv[:], a_all[:], ALU.max).then_inc(dt_read, 1)
                dve.wait_ge(dt_read, 2)
                ch.link(dve.tensor_tensor(dtv[:], eaend[:], eacum[:], ALU.add))
                ch.link(dve.tensor_tensor(a_all[:], dtv[:], bcast_mid(ez[:, 0:SSM_H], NT), ALU.mult))
                dve.tensor_scalar(a_all[:], a_all[:], -1.0, None, ALU.mult).then_inc(a_ready, 1)
                dve.wait_ge(decays_ready, 2)
                dve.tensor_tensor(wend[:], wend[:], dtv[:], ALU.mult).then_inc(decays_ready, 1)
                ch.end()

                ch = dve_loop
                with dve.Fori(0, HEADS) as i:
                    ch.start(dve, i)

                    def taps(n):
                        dve.wait_ge(taps_ready.sem, taps_ready.at(i, n + 1))
                        for s in (1, 2, 3):
                            w = par_sb[:, bass.ds(i * NPAR + (4 * n + 3 - s), 1)]
                            ins = dve.scalar_tensor_tensor(out=conv[:, n, s:T], in0=proj_b[n % 2][:, 0:T - s],
                                                           scalar=w, in1=conv[:, n, s:T], op0=ALU.mult, op1=ALU.add)
                            if s < 3:
                                ch.link(ins)
                        ins.then_inc(conv_ready.sem, 1)

                    def silu_z(t):
                        dve.wait_ge(proj_read.sem, proj_read.at(i, 3 + t))
                        ch.link(dve.tensor_scalar(ez, ez, 1.0, None, ALU.add))
                        ch.link(dve.reciprocal(ez, ez))
                        dve.tensor_tensor(vz[:, t, P:VZ], vz[:, t, P:VZ], ez, ALU.mult).then_inc(z_ready.sem, 1)

                    def norm_qk(n):
                        dve.wait_ge(root_ready.sem, root_ready.at(i, n + 1))
                        dve.scalar_tensor_tensor(out=qk[:, n], in0=qk[:, n], scalar=sm("qg" if n == 0 else "kg"),
                                                 in1=sq[:, n], op0=ALU.mult, op1=ALU.mult).then_inc(qk_ready.sem, 1)

                    def masked_cb(u):
                        dve.wait_ge(m1_ready.sem, m1_ready.at(i, 2 * u + 1))
                        dve.wait_ge(mix_ready.sem, mix_ready.at(i, u))
                        dve.tensor_tensor(cbm, m1_b[:, 0:P], tri, ALU.mult).then_inc(m1_read.sem, 1)

                    def logits(u):
                        n = (u + 1) * P
                        near = min(2 * P, n)
                        dve.wait_ge(diff_ready.sem, diff_ready.at(i, u))
                        dve.wait_ge(scores_ready.sem, scores_ready.at(i, u + 1))
                        if u == 0:
                            dve.wait_ge(bias_in.sem, bias_in.at(i, 1))
                        for m in range(2):
                            if n > near:
                                dve.tensor_scalar(L[:, m, 0:n - near], s_b[m][:, 0:n - near],
                                                  far[:, bass.ds(i, 1)], None, ALU.add)
                            ins = dve.tensor_tensor(L[:, m, n - near:n], s_b[m][:, n - near:n],
                                                    biasT[:, 2 * P - near:2 * P], ALU.add)
                        ins.then_inc(logits_ready.sem, 1)
                        dve.wait_ge(logits_ready.sem, logits_ready.at(i, u + 1))
                        ch.link(dve.tensor_reduce(st[:, 8:10], L[:, :, 0:n], AX, ALU.max))
                        dve.tensor_scalar(st[:, 8:10], st[:, 8:10], -1.0, None, ALU.mult).then_inc(max_ready.sem, 1)

                    def make_mix(u):
                        dve.wait_ge(decay_ready.sem, decay_ready.at(i, u + 1))
                        dve.wait_ge(m1_read.sem, m1_read.at(i, 2 * u + 1))
                        dve.wait_ge(ydiag_ready.sem, ydiag_ready.at(i, u))
                        dve.tensor_tensor(mix, decay, bcast_mid(cbm, HPG), ALU.mult).then_inc(mix_ready.sem, 1)

                    def make_diff(u, k):
                        n = (u + 1) * P
                        dve.wait_ge(exp_ready.sem, exp_ready.at(i, u + 1))
                        dve.wait_ge(m0_ready.sem, m0_ready.at(i, k))
                        ch.link(dve.reciprocal(st[:, 12:14], st[:, 10:12]))
                        ch.link(dve.tensor_tensor(st[:, 13:14], st[:, 13:14], eps[:, 2:3], ALU.mult))
                        ch.link(dve.tensor_scalar(diff[:, 0:n], L[:, 0, 0:n], st[:, 12:13], None, ALU.mult))
                        dve.scalar_tensor_tensor(out=diff[:, 0:n], in0=L[:, 1, 0:n], scalar=st[:, 13:14],
                                                 in1=diff[:, 0:n], op0=ALU.mult, op1=ALU.add).then_inc(
                            diff_ready.sem, 1)

                    def next_state(u):
                        dve.wait_ge(m1_ready.sem, m1_ready.at(i, 2 * u + 2))
                        new = m1_b[:, P:P + GW]
                        if u == 0:
                            dve.tensor_copy(state, new).then_inc(m1_read.sem, 1)
                            return
                        s4 = state.rearrange("p (h c) -> p h c", h=HPG)
                        ch.link(dve.tensor_tensor(s4, s4, bcast_inner(eaend[:, u, bass.ds(i * HPG, HPG)], HD),
                                                  ALU.mult))
                        dve.tensor_tensor(state, state, new, ALU.add).then_inc(m1_read.sem, 1)

                    def make_y(u):
                        dve.wait_ge(ydiag_ready.sem, ydiag_ready.at(i, u + 1))
                        dve.wait_ge(xs_ready.sem, xs_ready.at(i, u + 1))
                        dve.wait_ge(yn_ready.sem, yn_ready.at(i, u))
                        if u:
                            ch.link(dve.tensor_tensor(ybuf, y_b[:, 0:GW], xd, ALU.add))
                            dve.tensor_tensor(ytmp.rearrange("p (h c) -> p h c", h=HPG),
                                              y_b[:, GW:2 * GW].rearrange("p (h c) -> p h c", h=HPG),
                                              bcast_inner(eacum[:, u, bass.ds(i * HPG, HPG)], HD),
                                              ALU.mult).then_inc(y_read.sem, 1)
                            dve.wait_ge(y_read.sem, y_read.at(i, u + 1))
                            ch.link(dve.tensor_tensor(ybuf, ybuf, ytmp, ALU.add))
                        else:
                            dve.tensor_tensor(ybuf, y_b[:, 0:GW], xd, ALU.add).then_inc(y_read.sem, 1)
                            dve.wait_ge(y_read.sem, y_read.at(i, u + 1))
                        dve.wait_ge(z_ready.sem, z_ready.at(i, u + 1))
                        dve.tensor_tensor(ybuf, ybuf, vz[:, u, P:VZ], ALU.mult).then_inc(y_ready.sem, 1)

                    for n in range(4):
                        taps(n)
                    silu_z(0)
                    masked_cb(0)
                    make_mix(0)
                    norm_qk(0)
                    norm_qk(1)
                    next_state(0)
                    make_y(0)
                    logits(0)
                    silu_z(1)
                    masked_cb(1)
                    make_mix(1)
                    make_diff(0, 0)
                    logits(1)
                    next_state(1)
                    silu_z(2)
                    make_y(1)
                    make_diff(1, 5)
                    logits(2)
                    masked_cb(2)
                    make_mix(2)
                    silu_z(3)
                    make_diff(2, 6)
                    next_state(2)
                    make_y(2)
                    logits(3)
                    masked_cb(3)
                    make_mix(3)
                    make_diff(3, 8)
                    make_y(3)
                    dve.wait_ge(oroot_ready.sem, oroot_ready.at(i, 1))
                    dve.scalar_tensor_tensor(out=attnT[:, bass.ds(i, 1), :].rearrange("p a b -> p (a b)"),
                                             in0=m1_b[:], scalar=sm("subg"), in1=sq[:, 1], op0=ALU.mult,
                                             op1=ALU.mult).then_inc(m1_read.sem, 1)
                ch.end(HEADS)

            @block.tensor
            def _(pe):
                prime(pe, proj_done, sums_ready, m0_ready, m1_ready, seg_ready, scores_ready, ydiag_ready, osum_ready,
                      attn_out_ready, ssm_out_ready, slab_used, tx_ready, ta_ready)
                pe.wait_ge(consts_in, 80)
                rb = conv.rearrange("p a b -> p (a b)")[0:32, 0:HEADS]
                pe.matmul(s_b[0][0:HEADS, 0:GL], rb, conv[0:32, 2, 0:GL], start=True, stop=True)
                pe.matmul(s_b[1][:, 0:HEADS], conv[0:32, 2, 0:1].to_broadcast([32, P]), rb,
                          start=True, stop=True).then_inc(dist_ready, 1)
                xin = wm_sb.rearrange("p a b c -> p (a b c)")
                for b in range(2 * NT):
                    t, half = b // 2, b % 2
                    pe.wait_ge(h_ready, t + 1)
                    if b >= 2:
                        pe.wait_ge(hT_read, b - 1)
                    for k in range(4):
                        c = t * D + (4 * half + k) * P
                        ins = pe.transpose(bank[b % 2][:, k * P:(k + 1) * P], xin[:, c:c + P], ident)
                    ins.then_inc(hT_banks, 1)
                pe.wait_ge(hT_read, 2 * NT)
                pe.wait_ge(wdt_in, 16)
                wdt = dT.rearrange("p a b -> p (a b)")[:, 0:KT * SSM_H].rearrange("p (k h) -> p k h", k=KT)
                for t in range(NT):
                    for k in range(KT):
                        ins = pe.matmul(m0_b[:, t * SSM_H:(t + 1) * SSM_H], hT[:, k, t * P:(t + 1) * P], wdt[:, k],
                                        start=(k == 0), stop=(k == KT - 1))
                ins.then_inc(dt_ready, 1)
                pe.wait_ge(a_ready, 1)
                av = a_all[:].rearrange("p c h -> p (c h)")
                for n, m in enumerate((tri, after, ones)):
                    ins = pe.matmul(y_b[:, n * P:(n + 1) * P], m, av, start=True, stop=True)
                ins.then_inc(cums_ready, 1)
                pe.wait_ge(decays_ready, 3)

                with pe.Fori(0, HEADS) as i:
                    def free_proj(use):
                        if use < 2:
                            pe.wait_ge(proj_read.sem, proj_read.at(i, 0))
                        elif use < 6:
                            pe.wait_ge(conv_ready.sem, conv_ready.at(i, use - 1))
                        else:
                            pe.wait_ge(proj_read.sem, proj_read.at(i, use - 5))

                    def project(n, use, ks=range(KT)):
                        if 0 in ks:
                            free_proj(use)
                            pe.wait_ge(w_in_sig[n].sem, w_in_sig[n].at(i, 1))
                        for k in ks:
                            ins = pe.matmul(proj_b[use % 2][:], wm_sb[:, n, k], hT[:, k], start=(k == 0),
                                            stop=(k == KT - 1))
                        if KT - 1 in ks:
                            ins.then_inc(proj_done.sem, 1)

                    def project_vz(t):
                        free_proj(6 + t)
                        if t == 0:
                            pe.wait_ge(wvz_in.sem, wvz_in.at(i, 1))
                        for k in range(KT):
                            ins = pe.matmul(proj_b[t % 2][:, 0:VZ], hT[:, k, t * P:(t + 1) * P], wvz_sb[:, k],
                                            start=(k == 0), stop=(k == KT - 1))
                        ins.then_inc(proj_done.sem, 1)

                    def turn_xb(u):
                        if u == 0:
                            pe.wait_ge(silu_ready.sem, silu_ready.at(i, 4))
                        pe.wait_ge(m0_read.sem, m0_read.at(i, u))
                        for n in range(3):
                            ins = pe.transpose(m0_b[:, n * P:(n + 1) * P], conv[:, n, u * P:(u + 1) * P], ident)
                        ins.then_inc(m0_ready.sem, 1)

                    def sum_squares(n):
                        pe.wait_ge(proj_read.sem, proj_read.at(i, n + 1))
                        if n == 0:
                            pe.wait_ge(oroot_ready.sem, oroot_ready.at(i, 0))
                            pe.wait_ge(logits_ready.sem, logits_ready.at(i, 0))
                        pe.matmul(s_b[n][:], block_ones, sq[:, n], start=True, stop=True).then_inc(sums_ready.sem, 1)

                    def seg(u):
                        pe.wait_ge(am_ready.sem, am_ready.at(i, u + 1))
                        pe.wait_ge(decay_ready.sem, decay_ready.at(i, u))
                        pe.matmul(seg_b[:], after, am.rearrange("p a b -> p (a b)"), start=True,
                                  stop=True).then_inc(seg_ready.sem, 1)

                    def scores(u):
                        n = (u + 1) * P
                        if u == 0:
                            pe.wait_ge(qk_ready.sem, qk_ready.at(i, 2))
                            pe.wait_ge(root_ready.sem, root_ready.at(i, 2))
                        pe.wait_ge(logits_ready.sem, logits_ready.at(i, u))
                        for m in range(2):
                            r = slice(m * HD, (m + 1) * HD)
                            ins = pe.matmul(s_b[m][:, 0:n], qk[r, 0, u * P:(u + 1) * P], qk[r, 1, 0:n], start=True,
                                            stop=True)
                        ins.then_inc(scores_ready.sem, 1)

                    def cb(u):
                        pe.wait_ge(m1_read.sem, m1_read.at(i, 2 * u))
                        c = slice(u * P, (u + 1) * P)
                        pe.matmul(m1_b[:, 0:P], conv[:, 2, c], conv[:, 3, c], start=True, stop=True).then_inc(
                            m1_ready.sem, 1)

                    def y_and_state(u):
                        pe.wait_ge(y_read.sem, y_read.at(i, u))
                        pe.wait_ge(mix_ready.sem, mix_ready.at(i, u + 1))
                        pe.wait_ge(xs_ready.sem, xs_ready.at(i, u + 1))
                        for h in range(HPG):
                            ins = pe.matmul(y_b[:, h * HD:(h + 1) * HD], mix[:, h], xdt[:, h * HD:(h + 1) * HD],
                                            start=True, stop=True)
                        if u:
                            pe.wait_ge(m1_read.sem, m1_read.at(i, 2 * u))
                            ins = pe.matmul(y_b[:, GW:2 * GW], conv[:, 3, u * P:(u + 1) * P], state, start=True,
                                            stop=True)
                        ins.then_inc(ydiag_ready.sem, 1)
                        if u < NT - 1:
                            pe.wait_ge(m1_read.sem, m1_read.at(i, 2 * u + 1))
                            pe.matmul(m1_b[:, P:P + GW], xb[:, u, 2 * P:3 * P], xw, start=True, stop=True).then_inc(
                                m1_ready.sem, 1)

                    def turn_diff(u, k):
                        pe.wait_ge(diff_ready.sem, diff_ready.at(i, u + 1))
                        pe.wait_ge(m0_read.sem, m0_read.at(i, k))
                        for j in range(u + 1):
                            ins = pe.transpose(m0_b[:, j * P:(j + 1) * P], diff[:, j * P:(j + 1) * P], ident)
                        ins.then_inc(m0_ready.sem, 1)

                    def turn_y(u, k):
                        pe.wait_ge(yn_ready.sem, yn_ready.at(i, u + 1))
                        pe.wait_ge(m0_read.sem, m0_read.at(i, k))
                        for j in range(2):
                            ins = pe.transpose(m0_b[:, j * P:(j + 1) * P], yn[:, j * P:(j + 1) * P], ident)
                        ins.then_inc(m0_ready.sem, 1)

                    for n in range(6):
                        project(n, n)
                    project_vz(0)
                    turn_xb(0)
                    cb(0)
                    seg(0)
                    turn_xb(1)
                    sum_squares(0)
                    turn_xb(2)
                    sum_squares(1)
                    turn_xb(3)
                    y_and_state(0)
                    seg(1)
                    project_vz(1)
                    scores(0)
                    cb(1)
                    project_vz(2)
                    scores(1)
                    y_and_state(1)
                    seg(2)
                    turn_diff(0, 4)
                    project_vz(3)
                    scores(2)
                    cb(2)
                    turn_diff(1, 5)
                    turn_y(0, 6)
                    project(6, 10, range(0, KT // 2))
                    y_and_state(2)
                    turn_diff(2, 7)
                    seg(3)
                    scores(3)
                    cb(3)
                    project(6, 10, range(KT // 2, KT))
                    turn_y(1, 8)
                    y_and_state(3)
                    project(7, 11, range(0, KT // 2))
                    turn_diff(3, 9)
                    turn_y(2, 10)
                    pe.wait_ge(m1_read.sem, m1_read.at(i, 7))
                    pe.wait_ge(m0_read.sem, m0_read.at(i, 10))
                    pe.wait_ge(proj_read.sem, proj_read.at(i, 6))
                    for k in range(NT):
                        ins = pe.matmul(m1_b[:, k * P:T], vz[:, k, 0:P], dT[:, k, k * P:T], start=(k == 0),
                                        stop=(k == NT - 1))
                    ins.then_inc(m1_ready.sem, 1)
                    project(7, 11, range(KT // 2, KT))
                    pe.wait_ge(osq_ready.sem, osq_ready.at(i, 1))
                    pe.wait_ge(logits_ready.sem, logits_ready.at(i, 4))
                    pe.matmul(s_b[0][:], ones, sq[:, 0], start=True, stop=True).then_inc(osum_ready.sem, 1)
                    turn_y(3, 11)

        with nc.Block() as block:
            out_rows = out

            @block.sync
            def _(sp):
                with sp.Fori(0, KT - 1) as i:
                    sp.wait_ge(attn_out_ready.sem, attn_out_ready.at(i, 1))
                    for n in range(3):
                        if n == 1:
                            sp.wait_ge(ssm_out_ready.sem, ssm_out_ready.at(i, 1))
                        sp.dma_start(wo_sb[:, n].rearrange("p a b -> p (a b)"),
                                     w_o[bass.ds(i + 1, 1), :, n].rearrange("a p n -> (a p) n")).then_inc(
                            wo_in[n].sem, 16)
                sp.dma_start(wout_sb.rearrange("p k n -> p (k n)"), w_out).then_inc(wout_in, 16)
                sp.dma_start(gffn_sb, gffn).then_inc(gffn_in, 16)
                sp.dma_start(wrt_sb.rearrange("p a b -> p (a b)"), w_rt).then_inc(wrt_in, 16)
                for t in range(2):
                    sp.dma_start(xr_sb[:, t], x_rows[t * P:(t + 1) * P, :]).then_inc(xr_in[t], 16)
                sp.dma_start(slot_rows.rearrange("(s b) c -> s (b c)", s=CAP), pads).then_inc(pads_out, 16)
                sp.dma_start(pay[:].rearrange("p a b -> p (a b)"), tok_ids).then_inc(wrt_in, 16)
                for n in range(RAW):
                    sp.dma_start(raw[:, n], w1[0, n // 2, :, (n % 2) * D:(n % 2 + 1) * D]).then_inc(raw_in[n], 16)
                sp.wait_ge(zero_ready, 1)
                sp.dma_start(h2_rows[T:ROWS, :], zero_rows(zeros)).then_inc(pads_out, 16)
                sp.dma_start(out_rows[T:ROWS, :], zero_rows(zeros)).then_inc(pads_out, 16)
                sp.wait_ge(pads_out, 48)
                for t in range(NT):
                    rows = slice(t * P, (t + 1) * P)
                    sp.wait_ge(x1_ready, 2 * (t + 1))
                    if t < 2:
                        sp.dma_start(xr_sb[:, t], x_rows[(t + 2) * P:(t + 3) * P, :]).then_inc(
                            xr_in[t + 2], 16)
                    sp.dma_start(out_rows[rows, :], x1_buf[:, t % 2]).then_inc(x1_out, 16)
                    sp.wait_ge(h2_ready, t + 1)
                    sp.dma_start(h2_rows[rows, :], h2_buf[:, t % 2]).then_inc(h2_out, 16)
                    sp.wait_ge(x1_out, 16 * (t + 1))
                    sp.wait_ge(h2_out, 16 * (t + 1))
                sp.dma_start(b12_raw[0:E, :], b12).then_inc(b12_in, 16)
                sp.wait_ge(slots_out, 16 * NT * TOPK)
                sp.dma_start(slots[:].rearrange("s b c -> s (b c)"),
                             slot_rows.rearrange("(s b) c -> s (b c)", s=CAP)).then_inc(slots_in, 16)
                sp.wait_ge(slots_in, 16)
                sp.wait_ge(b12_in, 16)

            @block.tensor
            def _(pe):
                with pe.Fori(0, KT) as i:
                    pe.wait_ge(attn_out_read.sem, attn_out_read.at(i, 0))
                    pe.wait_ge(wo_in[0].sem, wo_in[0].at(i, 1))
                    for k in range(KT):
                        ins = pe.matmul(bank[0][:], wo_sb[:, 0, k], attnT[:, k], start=(k == 0), stop=(k == KT - 1))
                    ins.then_inc(attn_out_ready.sem, 1)
                    pe.wait_ge(ssm_out_read.sem, ssm_out_read.at(i, 0))
                    for k in range(2 * KT):
                        if k % KT == 0:
                            pe.wait_ge(wo_in[1 + k // KT].sem, wo_in[1 + k // KT].at(i, 1))
                        ins = pe.matmul(bank[1][:], wo_sb[:, 1 + k // KT, k % KT], ssmT[:, k], start=(k == 0),
                                        stop=(k == 2 * KT - 1))
                    ins.then_inc(ssm_out_ready.sem, 1)
                pe.wait_ge(merged_ready.sem, merged_ready.at(KT, 0))
                pe.wait_ge(wout_in, 16)

                def residual(t):
                    if t:
                        pe.wait_ge(x1_ready, 2 * t)
                    for half in range(2):
                        for k in range(KT):
                            ins = pe.matmul(bank[2 + half][:], gateT[:, 0, k, t * P:(t + 1) * P],
                                            wout_sb[:, k, half * 512:(half + 1) * 512], start=(k == 0),
                                            stop=(k == KT - 1))
                        ins.then_inc(res_ready, 1)

                def router(t):
                    pe.wait_ge(h2_ready, t + 1)
                    if t:
                        pe.wait_ge(h2T_read, 2 * t)
                    for half in range(2):
                        for k in range(4):
                            c = (4 * half + k) * P
                            ins = pe.transpose(bank[4 + half][:, k * P:(k + 1) * P], h2_buf[:, t % 2, c:c + P], ident)
                        ins.then_inc(h2T_ready, 1)
                    pe.wait_ge(h2T_read, 2 * (t + 1))
                    pe.wait_ge(wrt_in, 32)
                    for k in range(KT):
                        ins = pe.matmul(bank[6][:, t * E:(t + 1) * E], h2T[:, k], wrt_sb[:, k], start=(k == 0),
                                        stop=(k == KT - 1))
                    ins.then_inc(logit_ready, 1)

                residual(0)
                for t in range(1, NT):
                    residual(t)
                    router(t - 1)
                router(NT - 1)
                pe.wait_ge(mask_ready, 1)
                for t in range(NT):
                    for s in range(t + 1):
                        ins = pe.matmul(bank[7][:, t * E:(t + 1) * E], tri if s == t else ones, mask[:, s],
                                        start=(s == 0), stop=(s == t))
                for s in range(NT):
                    ins = pe.matmul(bank[7][:, NT * E:(NT + 1) * E], ones, mask[:, s], start=(s == 0),
                                    stop=(s == NT - 1))
                ins.then_inc(pos_ready, 1)

            @block.scalar
            def _(act):
                with act.Fori(0, KT) as i:
                    act.activation(gateT[:, 0, bass.ds(i, 1), :].rearrange("p a b -> p (a b)"),
                                   gateT[:, 0, bass.ds(i, 1), :].rearrange("p a b -> p (a b)"), ACT.Sigmoid)
                    act.activation(gateT[:, 1, bass.ds(i, 1), :].rearrange("p a b -> p (a b)"),
                                   gateT[:, 1, bass.ds(i, 1), :].rearrange("p a b -> p (a b)"),
                                   ACT.Sigmoid).then_inc(sigm_ready, 1)
                ch = act_step
                ch.start(act)
                act.preload_act_table_set("natural_log_exp_and_others")
                for t in range(NT):
                    act.wait_ge(x1_ready, 2 * (t + 1))
                    if t >= 2:
                        act.wait_ge(h2_out, 16 * (t - 1))
                        act.wait_ge(h2T_ready, 2 * (t - 1))
                    else:
                        act.wait_ge(merged_ready.sem, merged_ready.at(KT, 0))
                    h2 = h2_buf[:, t % 2]
                    ch.link(act.activation(h2, x1_buf[:, t % 2], ACT.Square, accum_out=st[:, 20:21]))
                    ch.link(act.activation(st[:, 20:21], st[:, 20:21], ACT.Ln, bias=eps[:, 0:1], scale=1.0 / D))
                    ch.link(act.activation(st[:, 20:21], st[:, 20:21], ACT.Exp, scale=-0.5))
                    act.activation(h2, x1_buf[:, t % 2], ACT.Copy, scale=st[:, 20:21]).then_inc(x1n_ready, 1)
                    for half in range(2):
                        act.wait_ge(h2T_ready, 2 * t + half + 1)
                        if t:
                            act.wait_ge(logit_ready, t)
                        act.activation(h2T[:, 4 * half:4 * half + 4],
                                       bank[4 + half][:].rearrange("p (a b) -> p a b", a=4),
                                       ACT.Copy).then_inc(h2T_read, 1)
                act.wait_ge(rt_exp, 1)
                act.activation(wgt, wgt, ACT.Exp).then_inc(rt_exp, 1)
                ch.end()

            @block.vector
            def _(dve):
                with dve.Fori(0, KT) as i:
                    g0 = gateT[:, 0, bass.ds(i, 1), :].rearrange("p a b -> p (a b)")
                    g1 = gateT[:, 1, bass.ds(i, 1), :].rearrange("p a b -> p (a b)")
                    dve.wait_ge(sigm_ready, i + 1)
                    dve.wait_ge(attn_out_ready.sem, attn_out_ready.at(i, 1))
                    dve.wait_ge(merged_ready.sem, merged_ready.at(i, 0))
                    dve.tensor_tensor(L[:, 0], bank[0][:], g0, ALU.mult).then_inc(attn_out_read.sem, 1)
                    dve.wait_ge(ssm_out_ready.sem, ssm_out_ready.at(i, 1))
                    dve.tensor_tensor(L[:, 1], bank[1][:], g1, ALU.mult).then_inc(ssm_out_read.sem, 1)
                    dve.wait_ge(attn_out_read.sem, attn_out_read.at(i, 1))
                    dve.wait_ge(ssm_out_read.sem, ssm_out_read.at(i, 1))
                    dve.tensor_tensor(g0, L[:, 0], L[:, 1], ALU.add).then_inc(merged_ready.sem, 1)
                dve.memset(zeros, 0.0).then_inc(zero_ready, 1)
                ch = dve_step
                ch.start(dve)
                dve.wait_ge(gffn_in, 16)

                def residual(t):
                    dve.wait_ge(xr_in[t], 16)
                    if t >= 2:
                        dve.wait_ge(x1_out, 16 * (t - 1))
                        dve.wait_ge(x1n_ready, t - 1)
                    for half in range(2):
                        c = slice(half * 512, (half + 1) * 512)
                        dve.wait_ge(res_ready, 2 * t + half + 1)
                        dve.tensor_tensor(x1_buf[:, t % 2, c], bank[2 + half][:], xr_sb[:, t % 2, c],
                                          ALU.add).then_inc(x1_ready, 1)

                def gain(t):
                    dve.wait_ge(x1n_ready, t + 1)
                    dve.tensor_tensor(h2_buf[:, t % 2], h2_buf[:, t % 2], gffn_sb, ALU.mult).then_inc(h2_ready, 1)

                for t in range(NT):
                    residual(t)
                    gain(t)
                dve.wait_ge(logit_ready, NT)
                ch.link(dve.tensor_tensor(lg, bank[6][:, 0:NT * E].rearrange("p (t e) -> p t e", t=NT),
                                          bcast_mid(sm("b_router"), NT), ALU.add))
                for t in range(NT):
                    ch.link(dve.max(mv[:, t], lg[:, t]))
                    ch.link(dve.max_index(mi[:, t], mv[:, t], lg[:, t]))
                ch.link(dve.tensor_copy(mif, mi[:, :, 0:TOPK]))
                dve.tensor_tensor(wgt, mv[:, :, 0:TOPK], mv[:, :, 0:1].to_broadcast([P, NT, TOPK]),
                                  ALU.subtract).then_inc(rt_exp, 1)
                iota_e = cn("iota_e")
                ch.link(dve.tensor_tensor(onehot, bcast_mid(iota_e, NT * TOPK),
                                          bcast_inner(mif.rearrange("p t k -> p (t k)"), E), ALU.is_equal))
                for t in range(NT):
                    ins = dve.tensor_reduce(mask[:, t], onehot[:, TOPK * t:TOPK * (t + 1)].rearrange("p k e -> p e k"),
                                            AX, ALU.add)
                ins.then_inc(mask_ready, 1)
                dve.wait_ge(rt_exp, 2)
                ch.link(dve.tensor_reduce(wsum, wgt, AX, ALU.add))
                ch.link(dve.reciprocal(wsum, wsum))
                dve.wait_ge(wrt_in, 32)
                ch.link(dve.tensor_tensor(pay[:, :, 1:2].bitcast(F32).rearrange("p (t k) o -> p t (k o)", t=NT), wgt,
                                          bcast_inner(wsum, TOPK), ALU.mult))
                dve.wait_ge(pos_ready, 1)
                dve.wait_ge(mask_ready, 1)
                ch.link(dve.tensor_tensor(pos, bank[7][:, 0:NT * E].rearrange("p (t e) -> p t e", t=NT), mask,
                                          ALU.subtract))
                ch.link(dve.tensor_copy(cnt, bank[7][:, NT * E:(NT + 1) * E]))
                ch.link(dve.tensor_scalar(quo, pos, float(CAP), None, ALU.is_ge))
                ch.link(dve.tensor_scalar(ov, cnt, float(CAP), None, ALU.is_gt))
                for j in range(2, MAXQ + 1):
                    ch.link(dve.scalar_tensor_tensor(out=quo, in0=pos, scalar=float(j * CAP), in1=quo,
                                                     op0=ALU.is_ge, op1=ALU.add))
                    ch.link(dve.scalar_tensor_tensor(out=ov, in0=cnt, scalar=float(j * CAP), in1=ov,
                                                     op0=ALU.is_gt, op1=ALU.add))
                src, dst = ov, ova
                for s in (1, 2, 4, 8, 16):
                    ch.link(dve.tensor_copy(dst[:, 0:s], src[:, 0:s]))
                    ch.link(dve.tensor_tensor(dst[:, s:E], src[:, s:E], src[:, 0:E - s], ALU.add))
                    src, dst = dst, (ovb if dst is ova else ova)
                ovend = src
                ch.link(dve.tensor_tensor(ovbase, ovend, ov, ALU.subtract))
                ch.link(dve.tensor_tensor(ovbase, ovbase, iota_e, ALU.subtract))
                ch.link(dve.tensor_scalar(ovbase, ovbase, float(E - 1), None, ALU.add))
                ch.link(dve.tensor_tensor(blk, quo, bcast_mid(ovbase, NT), ALU.add))
                ch.link(dve.scalar_tensor_tensor(out=blk, in0=quo, scalar=1.0, in1=blk, op0=ALU.is_ge,
                                                 op1=ALU.mult))
                ch.link(dve.tensor_tensor(blk, blk, bcast_mid(iota_e, NT), ALU.add))
                ch.link(dve.scalar_tensor_tensor(out=dest, in0=quo, scalar=-float(CAP), in1=pos, op0=ALU.mult,
                                                 op1=ALU.add))
                ch.link(dve.scalar_tensor_tensor(out=dest, in0=dest, scalar=float(NB), in1=blk, op0=ALU.mult,
                                                 op1=ALU.add))
                for t in range(NT):
                    ch.link(dve.tensor_tensor(sel[:, TOPK * t:TOPK * (t + 1)], onehot[:, TOPK * t:TOPK * (t + 1)],
                                              bcast_mid(dest[:, t], TOPK), ALU.mult))
                ch.link(dve.tensor_reduce(destf, sel, AX, ALU.add))
                dve.tensor_copy(desti[:], destf).then_inc(dest_ready, 1)
                ch.link(dve.tensor_tensor(ovcmp, bcast_mid(ovend, NOV + 1), bcast_inner(cn("iota_b"), E), ALU.is_le))
                ch.link(dve.tensor_reduce(ovexp, ovcmp, AX, ALU.add))
                ch.link(dve.tensor_scalar(ovexp, ovexp, float(E - 1), None, ALU.min))
                ch.link(dve.tensor_copy(blk_exp[:, E:NB], ovexp))
                ch.link(dve.tensor_copy(blk_exp[:, 0:E], iota_e))
                dve.tensor_copy(blk_exp[:, NB:NB + 1], ovend[:, E - 1:E]).then_inc(dest_ready, 1)
                ch.end()

            @block.gpsimd
            def _(pool):
                pool.wait_ge(dest_ready, 1)
                pool.wait_ge(pads_out, 48)
                for n in range(NT * TOPK):
                    pool.indirect_dma_start(slot_rows, bass.IndirectOffsetOnAxis(ap=desti[:, n:n + 1], axis=0),
                                            pay[:, n, :], None).then_inc(slots_out, 16)
                pool.wait_ge(slots_out, 16 * NT * TOPK)

        with nc.Block() as block:
            def count(b, n):
                return n + 1 if isinstance(b, int) and b == 0 else b * SLABS + (n - 7)

            def place(b, n, ring):
                return (n if isinstance(b, int) and b == 0 else n - 8) % ring

            def raw_count(b, n):
                first = isinstance(b, int) and b == 0
                return (n // RAW + 1) if first else b * (SLABS // RAW) + ((n - 8) // RAW + 1)

            def steps(eng, body, last):
                many = eng.value_load(blk_exp[0:1, NB:NB + 1], min_val=0, max_val=NOV)
                body(0)
                body(1)
                with eng.Fori(2, E) as b:
                    body(b)
                with eng.If(many > 0):
                    with eng.Fori(0, NOV) as o:
                        with eng.If(o < many):
                            body(o + E)
                last(many + E)

            @block.sync
            def _(sp):
                def load(b, n, at_n, e):
                    c = count(b, at_n)
                    if not isinstance(b, int) or b > 0 or at_n >= RAW:
                        sp.wait_ge(lo_ready.sem, c - RAW + 1)
                    if n < 16:
                        src = w1[bass.ds(e, 1), n // 2, :, (n % 2) * D:(n % 2 + 1) * D]
                    else:
                        src = w2[bass.ds(e, 1), n - 16]
                    s = place(b, at_n, RAW)
                    sp.dma_start(raw[:, s], src.rearrange("a p n -> (a p) n")).then_inc(raw_in[s], 16)

                def expert(b):
                    return sp.value_load(blk_exp[0:1, bass.ds(b, 1)], min_val=0, max_val=E - 1)

                def body(b):
                    if isinstance(b, int) and b == 0:
                        for n in range(RAW, 16):
                            load(0, n, n, 0)
                        return
                    e = b if isinstance(b, int) else expert(b)
                    for n in range(16):
                        load(b, n, n, e)
                    e = b - 1 if isinstance(b, int) else expert(b - 1)
                    for n in range(16, SLABS):
                        load(b, n, n, e)

                def last(b):
                    e = expert(b - 1)
                    for n in range(16, SLABS):
                        load(b, n, n - 16, e)

                steps(sp, body, last)

            @block.tensor
            def _(pe):
                def turn_x(b):
                    pe.wait_ge(gather_in.sem, gather_in.at(b, 1))
                    for half in range(2):
                        if not isinstance(b, int) or b > 1:
                            pe.wait_ge(al_ready.sem, al_ready.at(b - 2, half + 1))
                        for k in range(4):
                            c = (4 * half + k) * P
                            ins = pe.transpose(bank[6 + half][:, k * P:(k + 1) * P], xg[:, c:c + P], ident)
                        ins.then_inc(tx_ready.sem, 1)

                def turn_act(b):
                    for half in range(2):
                        pe.wait_ge(act_ready.sem, act_ready.at(b, half + 1))
                        pe.wait_ge(xl_ready.sem, xl_ready.at(b + 1, half + 1))
                        for k in range(4):
                            c = (4 * half + k) * P
                            ins = pe.transpose(bank[6 + half][:, k * P:(k + 1) * P], act_rows[:, c:c + P], ident)
                        ins.then_inc(ta_ready.sem, 1)

                def slab(b, at_n, hi, lo, banks, stop):
                    pe.wait_ge(lo_ready.sem, count(b, at_n) + 1)
                    s = place(b, at_n, SPLIT)
                    for x_part, w_part in ((hi, w_hi), (hi, w_lo), (lo, w_hi)):
                        for c in range(2):
                            ins = pe.matmul(banks[c][:], x_part, w_part[:, s, c * 512:(c + 1) * 512], start=False,
                                            stop=stop and w_part is w_hi and x_part is lo)
                    ins.then_inc(slab_used.sem, 1)

                def first(b):
                    pe.wait_ge(xl_ready.sem, xl_ready.at(b, 2))
                    pe.wait_ge(act_ready.sem, act_ready.at(b, 0))
                    pe.wait_ge(pick_ready.sem, pick_ready.at(b, 1))
                    for c in range(4):
                        pe.matmul(bank[c][:], pick1[:], bias_hl[:, c * 512:(c + 1) * 512], start=True, stop=False)
                    for n in range(16):
                        slab(b, n, x_hi[:, n // 2], x_lo[:, n // 2], bank[2 * (n % 2):2 * (n % 2) + 2], n >= 14)

                def second(b, step, at):
                    pe.wait_ge(al_ready.sem, al_ready.at(b, 2))
                    pe.wait_ge(yrow_ready.sem, yrow_ready.at(b, 0))
                    pe.wait_ge(pick_ready.sem, pick_ready.at(b, 2))
                    for c in range(2):
                        pe.matmul(bank[4 + c][:], pick2[:], bias_hl[:, 2 * D + c * 512:2 * D + (c + 1) * 512],
                                  start=True, stop=False)
                    for n in range(8):
                        slab(step, at + n, a_hi[:, n], a_lo[:, n], bank[4:6], n == 7)

                def body(b):
                    first(b)
                    turn_x(b + 1)
                    if not isinstance(b, int) or b > 0:
                        second(b - 1, b, 16)
                    turn_act(b)

                turn_x(0)
                steps(pe, body, lambda b: second(b - 1, b, 0))

            def take_turned(eng, b, ready, hi, lo, hi_ready_, lo_ready_):
                for half in range(2):
                    src = bank[6 + half][:].rearrange("p (a b) -> p a b", a=4)
                    k = slice(4 * half, 4 * half + 4)
                    if eng is nc.scalar:
                        eng.wait_ge(ready.sem, ready.at(b, half + 1))
                        eng.activation(hi[:, k], src, ACT.Copy).then_inc(hi_ready_.sem, 1)
                    else:
                        eng.wait_ge(hi_ready_.sem, hi_ready_.at(b, half + 1))
                        eng.tensor_tensor(lo[:, k], src, hi[:, k].bitcast(F32), ALU.subtract).then_inc(
                            lo_ready_.sem, 1)

            @block.scalar
            def _(act):
                def split(b, at_n):
                    act.wait_ge(raw_in[place(b, at_n, RAW)], raw_count(b, at_n) * 16)
                    c = count(b, at_n)
                    if not isinstance(b, int) or b > 0 or at_n >= SPLIT:
                        act.wait_ge(slab_used.sem, c - SPLIT + 1)
                    act.activation(w_hi[:, place(b, at_n, SPLIT)], raw[:, place(b, at_n, RAW)], ACT.Copy).then_inc(
                        hi_ready.sem, 1)

                def take_x(b):
                    take_turned(nc.scalar, b, tx_ready, x_hi, x_lo, xh_ready, xl_ready)

                def take_act(b):
                    take_turned(nc.scalar, b, ta_ready, a_hi, a_lo, ah_ready, al_ready)

                def swish(b, c):
                    act.wait_ge(g_ready.sem, g_ready.at(b, c + 1))
                    act.activation(s_buf[:, c], g_buf[:, c], ACT.Sigmoid, scale=SWIGLU_ALPHA).then_inc(s_ready.sem, 1)

                def take_y(b, step, at_n):
                    act.wait_ge(slab_used.sem, count(step, at_n) + 1)
                    act.wait_ge(sidx_ready.sem, sidx_ready.at(b, 1))
                    for c in range(2):
                        act.activation(y_rows[:, c * 512:(c + 1) * 512], bank[4 + c][:], ACT.Copy,
                                       scale=w_cur[:, 0:1]).then_inc(yrow_ready.sem, 1)

                def body(b):
                    peeled = isinstance(b, int)
                    for n in range(SLABS):
                        if n == 5 and (not peeled or b > 0):
                            take_act(b - 1)
                        if n == 6 and (not peeled or b > 1):
                            take_y(b - 2, b - 1, SLABS - 1)
                        if n < 16 or not peeled or b > 0:
                            split(b, n)
                        if n == 20:
                            take_x(b + 1)
                            swish(b, 0)
                        if n == 21:
                            swish(b, 1)

                def last(b):
                    for n in range(8):
                        if n == 5:
                            take_act(b - 1)
                        split(b, n)
                        if n == 5:
                            take_y(b - 2, b - 1, SLABS - 1)
                    take_y(b - 1, b, 7)

                act.activation(bias_hl[0:E, :], b12_raw[0:E, :], ACT.Copy).then_inc(bias_ready, 1)
                take_x(0)
                steps(act, body, last)

            @block.vector
            def _(dve):
                ch = dve_moe

                def split(b, at_n):
                    dve.wait_ge(hi_ready.sem, count(b, at_n) + 1)
                    s = place(b, at_n, SPLIT)
                    dve.tensor_tensor(w_lo[:, s], raw[:, place(b, at_n, RAW)], w_hi[:, s].bitcast(F32),
                                      ALU.subtract).then_inc(lo_ready.sem, 1)

                def take_x(b):
                    take_turned(nc.vector, b, tx_ready, x_hi, x_lo, xh_ready, xl_ready)

                def take_act(b):
                    take_turned(nc.vector, b, ta_ready, a_hi, a_lo, ah_ready, al_ready)

                def clamp_gate(b, c):
                    dve.wait_ge(slab_used.sem, count(b, 15) + 1)
                    dve.wait_ge(act_ready.sem, act_ready.at(b, 0))
                    dve.tensor_scalar(g_buf[:, c], bank[c][:], SWIGLU_LIMIT, None, ALU.min).then_inc(g_ready.sem, 1)

                def swiglu(b, c):
                    ch.link(dve.tensor_scalar(u_buf[:, c], bank[2 + c][:], SWIGLU_LIMIT, -SWIGLU_LIMIT, ALU.min,
                                              ALU.max))
                    dve.wait_ge(s_ready.sem, s_ready.at(b, c + 1))
                    ch.link(dve.tensor_tensor(g_buf[:, c], g_buf[:, c], s_buf[:, c], ALU.mult))
                    dve.wait_ge(ta_ready.sem, ta_ready.at(b, 0))
                    dve.scalar_tensor_tensor(out=act_rows[:, c * 512:(c + 1) * 512], in0=u_buf[:, c], scalar=1.0,
                                             in1=g_buf[:, c], op0=ALU.add, op1=ALU.mult).then_inc(act_ready.sem, 1)

                def body(b):
                    peeled = isinstance(b, int)
                    ch.start(dve, b)
                    for n in range(SLABS):
                        if n == 5 and (not peeled or b > 0):
                            take_act(b - 1)
                        if n < 16 or not peeled or b > 0:
                            split(b, n)
                        if n == 20:
                            take_x(b + 1)
                            clamp_gate(b, 0)
                            clamp_gate(b, 1)
                        if n == 21:
                            swiglu(b, 0)
                        if n == 22:
                            swiglu(b, 1)
                    assert ch.n == ch.per_step, ("links per block", ch.n)

                def last(b):
                    for n in range(8):
                        if n == 5:
                            take_act(b - 1)
                        split(b, n)

                dve.wait_ge(bias_ready, 1)
                dve.tensor_tensor(bias_hl[E:2 * E, :], b12_raw[0:E, :], bias_hl[0:E, :].bitcast(F32),
                                  ALU.subtract).then_inc(bias_ready, 1)
                take_x(0)
                steps(dve, body, last)

            @block.gpsimd
            def _(pool):
                def carry_waits(n, b):
                    pool.wait_ge(spare_used[n].sem, spare_used[n].at(b, 0))
                    pool.tensor_tensor(spare[:, n:n + 1], spare[:, 2:3], spare[:, 2:3], ALU.add).then_inc(
                        spare_used[n].sem, 1)

                def gather(b):
                    pool.tensor_copy(g_idx[:], slots[:, bass.ds(b, 1), 0:1].rearrange("s a c -> s (a c)")).then_inc(
                        gidx_ready.sem, 1)
                    pool.wait_ge(gidx_ready.sem, gidx_ready.at(b, 1))
                    carry_waits(0, b)
                    pool.indirect_dma_start(xg, None, h2_rows,
                                            bass.IndirectOffsetOnAxis(ap=g_idx[:, 0:1], axis=0)).then_inc(
                        gather_in.sem, 16)

                def pick(b, tile):
                    e = pool.value_load(blk_exp[0:1, bass.ds(b, 1)], min_val=0, max_val=E - 1)
                    o = CONST["pick"][0]
                    pool.tensor_copy(tile[:], cst[0:2 * E, bass.ds(e + o, 1)].to_broadcast([2 * E, P])).then_inc(
                        pick_ready.sem, 1)

                def scatter(b):
                    pool.tensor_copy(w_cur[:], slots[:].bitcast(F32)[:, bass.ds(b, 1), 1:2].rearrange(
                        "s a c -> s (a c)"))
                    pool.tensor_copy(s_idx[:], slots[:, bass.ds(b, 1), 0:1].rearrange("s a c -> s (a c)")).then_inc(
                        sidx_ready.sem, 1)
                    pool.wait_ge(yrow_ready.sem, yrow_ready.at(b, 2))
                    carry_waits(1, b)
                    pool.indirect_dma_start(out, bass.IndirectOffsetOnAxis(ap=s_idx[:, 0:1], axis=0),
                                            y_rows, None, compute_op=ALU.add).then_inc(scatter_done.sem, 16)
                    pool.wait_ge(scatter_done.sem, scatter_done.at(b, 1))

                def body(b):
                    peeled = isinstance(b, int)
                    pool.wait_ge(tx_ready.sem, tx_ready.at(b, 2))
                    gather(b + 1)
                    if not peeled or b > 1:
                        scatter(b - 2)
                    if not peeled or b > 0:
                        pool.wait_ge(slab_used.sem, count(b, 16) + 1)
                    else:
                        pool.wait_ge(slab_used.sem, count(b, 0) + 1)
                    pick(b, pick2)
                    pick(b + 1, pick1)

                def last(b):
                    scatter(b - 2)
                    scatter(b - 1)

                pool.memset(spare[:], 0.0).then_inc(spare_ready, 1)
                pool.wait_ge(spare_ready, 1)
                pick(0, pick1)
                gather(0)
                steps(pool, body, last)


def toeplitz(rows):
    return bass.AP(tensor=rows.tensor, offset=rows.offset + (P - 1), ap=[[GL, HEADS], [-1, P], [1, 2 * P]])


def zero_rows(zeros):
    return zeros[0:CAP].unsqueeze(1).to_broadcast([CAP, D // 32, 32])


def constants():
    c = np.zeros((P, N_CONST), np.float32)
    r = np.arange(P)

    def put(name, a):
        o, w = CONST[name]
        c[:a.shape[0], o:o + w] = a

    put("ident", np.eye(P))
    put("tri", r[:, None] <= r[None, :])
    put("after", r[:, None] > r[None, :])
    put("ones", np.ones((P, P)))
    put("block", r[:, None] // HD == r[None, :] // HD)
    dist = np.maximum(2 * P - 1 - np.arange(GL), 0)
    exact = 16
    scaled = np.log(np.maximum(dist, 1).astype(np.float32) / exact) / np.float32(math.log(128 / exact))
    large = np.minimum(exact + (scaled * exact).astype(np.int32), 31)
    bucket = np.where(dist < exact, dist, large)
    onehot = (np.arange(32)[:, None] == bucket[None, :]).astype(np.float32)
    put("iota_e", np.tile(np.arange(E), (P, 1)))
    put("pick", r[:2 * E, None] % E == np.arange(E)[None, :])
    put("iota_b", np.tile(np.arange(NOV + 1), (P, 1)))
    ids = np.zeros((P, NT * TOPK, 2), np.int32)
    ids[:, :, 0] = np.arange(NT * TOPK)[None, :] // TOPK * P + r[:, None]
    pads = np.zeros((CAP, NB, 2), np.int32)
    pads[:, :, 0] = T + np.arange(CAP)[:, None]
    return c, onehot, ids.reshape(P, -1), pads.reshape(CAP, -1)


def lay_out(i):
    def rep(a):
        return np.broadcast_to(np.asarray(a).reshape(1, -1), (P, np.asarray(a).size))

    def cols(a):
        return np.asarray(a).reshape(-1, P).T

    parts = {"g_mix": cols(i["g_mix"]), "qg": np.tile(i["q_norm_g"][0], 2)[:, None],
             "kg": np.tile(i["k_norm_g"][0], 2)[:, None], "subg": i["attn_sub_g"][0][:, None],
             "lq1": rep(i["lambda_q1"]), "lk1": rep(i["lambda_k1"]), "lq2": rep(i["lambda_q2"]),
             "lk2": rep(i["lambda_k2"]), "dt_bias": rep(i["dt_bias"]), "a_log": rep(i["a_log"]),
             "d_skip": rep(i["d_skip"]), "b_router": rep(i["b_router"])}
    small = np.concatenate([parts[n] for n in SMALL], axis=1)
    w = np.asarray(i["w_in"][0]).reshape(KT, P, -1)
    q0, k0, v0, z0, x0, b0, c0, dt0, g0 = 0, 1024, 2048, 3072, 5120, 7168, 8192, 9216, 9248

    def step(n):
        starts = (x0 + n * GW, x0 + n * GW + P, b0 + n * P, c0 + n * P, q0 + n * P, k0 + n * P, g0 + n * P,
                  g0 + D + n * P)
        return np.stack([w[:, :, s:s + P] for s in starts])

    w_mix = np.stack([step(n) for n in range(HEADS)]).transpose(0, 3, 1, 2, 4).reshape(HEADS, P, CHT, KT * P)
    w_vz = np.stack([np.concatenate([w[:, :, v0 + n * P:v0 + (n + 1) * P], w[:, :, z0 + n * GW:z0 + (n + 1) * GW]], 2)
                     for n in range(HEADS)]).transpose(0, 2, 1, 3).reshape(HEADS, P, KT * VZ)
    w_dt = w[:, :, dt0:dt0 + SSM_H].transpose(1, 0, 2).reshape(P, -1)
    taps = np.concatenate([np.asarray(i["conv_w"][0]), np.asarray(i["conv_b"])])
    par = []
    for n in range(HEADS):
        tiles = [taps[:, s:s + P] for s in (n * GW, n * GW + P, 2048 + n * P, 3072 + n * P)]
        par += [t[j] for t in tiles for j in range(4)] + [t[4] for t in tiles]
        par += [np.asarray(i["ssm_norm_g"][0])[n * GW + j * P:n * GW + (j + 1) * P] for j in range(2)]
    par = np.stack(par, 1)
    wo = np.concatenate([np.asarray(i["w_attn_o"][0]), np.asarray(i["w_ssm_o"][0])])
    w_o = wo.reshape(3, KT, P, KT, P).transpose(3, 2, 0, 1, 4).reshape(KT, P, 3, KT * P)
    w_out = np.asarray(i["w_out"][0]).reshape(KT, P, D).transpose(1, 0, 2).reshape(P, -1)
    w_rt = np.asarray(i["w_router"][0]).reshape(KT, P, E).transpose(1, 0, 2).reshape(P, -1)
    w1 = np.asarray(i["w1"][0]).reshape(E, KT, P, 2 * D)
    w2 = np.asarray(i["w2"][0]).reshape(E, 8, P, D)
    b12 = np.concatenate([i["b1"][0], i["b2"][0]], 1)
    consts, onehot, ids, pads = constants()
    return {"x": i["x"], "small": small, "consts": consts, "onehot": onehot, "gffn": rep(i["g_ffn"]), "rel_bias": i["rel_bias"],
            "par": par, "w_mix": w_mix, "w_vz": w_vz, "w_dt": w_dt, "w_o": w_o, "w_out": w_out, "w_rt": w_rt,
            "w1": w1, "w2": w2, "b12": b12, "tok_ids": ids, "pads": pads}


def kernel(**inputs):
    import concourse.bacc as bacc
    from concourse.bass_utils import run_bass_kernel_spmd as run

    nc = bacc.Bacc("TRN2", target_bir_lowering=False, num_devices=1)
    arrays, args = {}, []
    for name, a in lay_out(inputs).items():
        a = np.ascontiguousarray(a)
        arrays[f"in_{name}"] = a
        args.append(nc.dram_tensor(f"in_{name}", a.shape, mybir.dt.from_np(a.dtype), kind="ExternalInput").ap())
    args.append(nc.dram_tensor("out_rows", (ROWS, D), F32, kind="ExternalOutput").ap())
    decoder_layer(nc, *args)
    r = run(nc, [arrays], core_ids=[0])
    return r.results[0]["out_rows"][:T].reshape(1, T, D)
```

```python
import math
from contextlib import ExitStack

import numpy as np
import concourse.bass as bass
from concourse import mybir

F32 = mybir.dt.float32
F32R = mybir.dt.float32r
I32 = mybir.dt.int32
U32 = mybir.dt.uint32
ALU = mybir.AluOpType
ACT = mybir.ActivationFunctionType
AX = mybir.AxisListType.X

P = 128
D = 1024
T = 512
KT = D // P
NT = T // P
HEADS = 8
HD = 64
HPG = 4
SSM_H = 32
GW = 256
VZ = P + GW
PIECES = 9
MRAW, MSPLIT = 3, 3
TILE_PIECES = 5
GRAW, GSPLIT = 2, 2
GSTEP = 2 * TILE_PIECES
NPAR = 22
E = 32
TOPK = 4
CAP = 112
MAXQ = (T - 1) // CAP
NOV = (T * TOPK) // CAP
NB = E + NOV + 1
SLABS = 24
RAW, SPLIT = 12, 6
ROWS = T + CAP
RMS_EPS = 1e-6
SSM_EPS = 1e-5
LAMBDA_INIT = 0.8 - 0.6 * math.exp(0.0)
SWIGLU_LIMIT = 7.0
SWIGLU_ALPHA = 1.702
NEG = -1e30
GL = 384

SMALL = {}
_o = 0
for _n, _w in (("g_mix", KT), ("qg", 1), ("kg", 1), ("subg", 1), ("lq1", HD), ("lk1", HD), ("lq2", HD),
               ("lk2", HD), ("dt_bias", SSM_H), ("a_log", SSM_H), ("d_skip", SSM_H), ("b_router", E)):
    SMALL[_n] = (_o, _w)
    _o += _w
N_SMALL = _o
CONST = {}
_o = 0
for _n, _w in (("ident", P), ("tri", P), ("after", P), ("ones", P), ("block", P),
               ("iota_e", E), ("iota_b", NOV + 1), ("pick", E)):
    CONST[_n] = (_o, _w)
    _o += _w
N_CONST = _o


class Signal:

    def __init__(self, sem, per_step=1, unit=1):
        self.sem, self.per_step, self.unit = sem, per_step, unit
        self.first = 1 if unit == 1 else 0

    def at(self, step, k):
        assert k > 0 or self.first or not isinstance(step, int) or step > 0
        return step * (self.per_step * self.unit) + (k * self.unit + self.first)


def prime(eng, *signals):
    for s in signals:
        eng.sem_inc(s.sem, 1)


class Chain:

    def __init__(self, sem, per_step=0):
        self.sem, self.per_step, self.base, self.n = sem, per_step, 0, 0
        self.eng = self.step = None

    def start(self, eng, step=None):
        self.eng, self.step, self.n = eng, step, 0

    def link(self, ins):
        self.n += 1
        ins.then_inc(self.sem, 1)
        at = self.base + self.n
        self.eng.wait_ge(self.sem, at if self.step is None else self.step * self.per_step + at)

    def end(self, steps=1):
        if self.step is not None:
            assert self.n == self.per_step, ("links per step", self.n, self.per_step)
        self.base += self.n * steps
        self.n = 0


class Arena:

    def __init__(self, tensor, size):
        self.t, self.size, self.at = tensor, size, 0

    def reset(self, at=0):
        self.at = at

    def take(self, *shape):
        n = int(np.prod(shape))
        assert self.at + n <= self.size, ("arena", self.at + n, self.size)
        v = self.t[:, self.at:self.at + n]
        self.at += n
        if len(shape) == 2:
            v = v.rearrange("p (a b) -> p a b", a=shape[0])
        elif len(shape) == 3:
            v = v.rearrange("p (a b c) -> p a b c", a=shape[0], b=shape[1])
        return v


def apart(eng, sem):
    eng.wait_ge(sem, 80)


def bcast_inner(ap, n):
    return ap.unsqueeze(2).to_broadcast([ap.shape[0], ap.shape[1], n])


def bcast_mid(ap, n):
    return ap.unsqueeze(1).to_broadcast([ap.shape[0], n, ap.shape[1]])


DVE_LINKS, ACT_LINKS, MOE_LINKS = 32, 25, 4


def decoder_layer(nc, x, small, consts, onehot_rows, gffn, rel_bias, par, w_mix, w_dt, w_tail, w_rt, w1, w2, b12,
                  tok_ids, pads, out):
    with ExitStack() as ctx:
        def sb(name, shape, dt=F32):
            return ctx.enter_context(nc.sbuf_tensor(name, shape, dt))

        def sem(name):
            return ctx.enter_context(nc.semaphore(name))

        def sig(name, per_step=1, unit=1):
            return Signal(sem(name), per_step, unit)

        h2_rows = nc.dram_tensor("h2_rows", (ROWS, D), F32, kind="Internal").ap()
        dist_rows = nc.dram_tensor("dist_rows", (HEADS, GL), F32, kind="Internal").ap()
        bias_rows = nc.dram_tensor("bias_rows", (HEADS, P, 2 * P), F32, kind="Internal").ap()
        slot_rows = nc.dram_tensor("slot_rows", (CAP * NB, 2), I32, kind="Internal").ap()

        bank = [ctx.enter_context(nc.psum_tensor(f"bank{b}", [P, 512], F32)) for b in range(8)]
        proj_b = bank[0:2]
        s_b = bank[2:4]
        m0_b, m1_b, seg_b, y_b = bank[4:8]

        big = sb("big", [P, 24576])
        big_base = nc.sbuf_base - 4 * 24576
        keep = sb("keep", [P, 23552])
        keep_base = nc.sbuf_base - 4 * 23552
        smalls = sb("smalls", [P, N_SMALL])
        cst = sb("cst", [P, N_CONST])
        eps = sb("eps", [P, 4])
        lam_t = sb("lam_t", [P, HD + 4])

        def sm(name):
            o, w = SMALL[name]
            return smalls[:, o:o + w]

        def cn(name, a=0, n=None):
            o, w = CONST[name]
            return cst[:, o + a:o + (w if n is None else a + n)]

        ident, tri, after, ones, block_ones = cn("ident"), cn("tri"), cn("after"), cn("ones"), cn("block")
        loop_mem, keep_mem = Arena(big, 24576), Arena(keep, 23552)
        par_sb = sb("par_sb", [P, HEADS * NPAR])
        far = sb("far", [P, HEADS])

        attnT = keep_mem.take(HEADS, T)
        ssmT = keep_mem.take(2 * HEADS, T)
        loop_mem.take(KT, T)
        hT = loop_mem.take(KT, T)
        mraw = loop_mem.take(MRAW, D)
        conv = loop_mem.take(4, T)
        xb = loop_mem.take(NT, 3 * P)
        qk = loop_mem.take(2, T)
        vz = loop_mem.take(NT, VZ)
        aux = sb("aux", [P, 2048])
        aux_mem = Arena(aux, 2048)
        L = aux_mem.take(2, T)
        diff = aux_mem.take(T)
        am = aux_mem.take(HPG, P)
        ext_mem = Arena(keep, 23552)
        ext_mem.reset(23552 - 3 * KT * P)
        sqx = keep[:, 23552 - 3 * KT * P:23552 - 3 * KT * P + D]
        sq = ext_mem.take(2, T)
        decay = ext_mem.take(HPG, P)
        mix = ext_mem.take(HPG, P)
        state = ext_mem.take(GW)
        xdt = ext_mem.take(GW)
        xw = ext_mem.take(GW)
        xd = ext_mem.take(GW)
        st = sb("st", [P, 32])
        yn = sb("yn", [P, GW])
        biasT = sb("biasT", [P, GW])
        dT = loop_mem.take(NT, T)
        ez = loop_mem.take(GW)
        ybuf = loop_mem.take(GW)
        ytmp = loop_mem.take(GW)
        cbm = loop_mem.take(P)

        def parts(name, shape, base, at):
            return nc.alloc_sbuf_tensor_at(name, shape, F32R, offset=base + 4 * at)

        h_hi, h_lo = parts("h_hi", [P, KT, T], big_base, 0), parts("h_lo", [P, KT, T], big_base, KT * T)
        vz_hi = parts("vz_hi", [P, KT * VZ], keep_base, 12288)
        vz_lo = parts("vz_lo", [P, KT * VZ], keep_base, 12288 + KT * VZ)
        spots = ((keep_base, 18432), (big_base, loop_mem.at), (big_base, loop_mem.at + 2 * D))
        wm_hi = [parts(f"wm_hi{n}", [P, KT, P], base, at) for n, (base, at) in enumerate(spots)]
        wm_lo = [parts(f"wm_lo{n}", [P, KT, P], base, at + D) for n, (base, at) in enumerate(spots)]
        xin = keep[:, 12288:16384]

        dtv = sb("dtv", [P, NT, SSM_H])
        a_all = sb("a_all", [P, NT, SSM_H])
        eacum = sb("eacum", [P, NT, SSM_H])
        wend = sb("wend", [P, NT, SSM_H])
        eaend = sb("eaend", [P, NT, SSM_H])

        consts_in, x_in, wdt_in = sem("consts_in"), [sem(f"x_in{t}") for t in range(NT)], sem("wdt_in")
        h_ready, hT_banks, hT_read = sem("h_ready"), sem("hT_banks"), sem("hT_read")
        hhi_ready, hlo_ready = sem("hhi_ready"), sem("hlo_ready")
        dt_ready, dt_read, a_ready, cums_ready, decays_ready = (
            sem("dt_ready"), sem("dt_read"), sem("a_ready"), sem("cums_ready"), sem("decays_ready"))
        dist_ready, dist_read, dist_out, lam_ready = sem("dist_ready"), sem("dist_read"), sem("dist_out"), sem("lam_ready")
        piece_in = [sig(f"piece_in{n}", PIECES // MRAW, 16) for n in range(MRAW)]
        phi_ready, plo_ready = sig("phi_ready", PIECES), sig("plo_ready", PIECES)
        bias_in = sig("bias_in", 1, 16)
        proj_done = sig("proj_done", 10)
        taps_ready = sig("taps_ready", 4)
        conv_ready = sig("conv_ready", 4)
        silu_ready = sig("silu_ready", 4)
        proj_read = sig("proj_read", 6)
        sigz_ready = sig("sigz_ready", 4)
        z_ready = sig("z_ready", 4)
        sums_ready = sig("sums_ready", 2)
        root_ready = sig("root_ready", 2)
        qk_ready = sig("qk_ready", 2)
        m0_ready, m0_read = sig("m0_ready", 12), sig("m0_read", 12)
        m1_ready, m1_read = sig("m1_ready", 8), sig("m1_read", 8)
        am_ready = sig("am_ready", 4)
        xs_ready = sig("xs_ready", 4)
        seg_ready, decay_ready = sig("seg_ready", 4), sig("decay_ready", 4)
        scores_ready, logits_ready = sig("scores_ready", 4), sig("logits_ready", 4)
        max_ready, exp_ready, diff_ready = sig("max_ready", 4), sig("exp_ready", 4), sig("diff_ready", 4)
        cbm_ready, mix_ready = sig("cbm_ready", 4), sig("mix_ready", 4)
        ydiag_ready, y_read, y_ready, yn_ready = (sig("ydiag_ready", 4), sig("y_read", 4), sig("y_ready", 4),
                                                  sig("yn_ready", 4))
        osq_ready, osum_ready, oroot_ready = sig("osq_ready"), sig("osum_ready"), sig("oroot_ready")
        dve_step, act_step = Chain(sem("dve_step")), Chain(sem("act_step"))
        dve_loop, act_loop = Chain(sem("dve_loop"), DVE_LINKS), Chain(sem("act_loop"), ACT_LINKS)
        graw_in = [sig(f"graw_in{n}", GSTEP // GRAW, 16) for n in range(GRAW)]
        ghi_ready, glo_ready, gpiece_used = (sig("ghi_ready", GSTEP), sig("glo_ready", GSTEP),
                                             sig("gpiece_used", GSTEP))
        mixhi_ready, mixlo_ready = sem("mixhi_ready"), sem("mixlo_ready")
        sigm_ready, attn_out_read, ssm_out_read = sig("sigm_ready", 4), sig("attn_out_read", 2), sig("ssm_out_read", 2)
        merged_ready, mhi_ready, mlo_ready = sig("merged_ready", 2), sig("mhi_ready", 2), sig("mlo_ready", 2)
        gffn_in, xr_in = sem("gffn_in"), [sem(f"xr_in{t}") for t in range(NT)]
        res_ready, x1_ready, x1n_ready, h2_ready = sem("res_ready"), sem("x1_ready"), sem("x1n_ready"), sem("h2_ready")
        x1_out, h2_out, pads_out, zero_ready = sem("x1_out"), sem("h2_out"), sem("pads_out"), sem("zero_ready")
        h2T_ready, h2T_read, logit_ready = sem("h2T_ready"), sem("h2T_read"), sem("logit_ready")
        rt_exp, mask_ready, pos_ready, dest_ready, wrt_in = (
            sem("rt_exp"), sem("mask_ready"), sem("pos_ready"), sem("dest_ready"), sem("wrt_in"))
        slots_out, slots_in = sem("slots_out"), sem("slots_in")
        raw_in = [sem(f"raw_in{n}") for n in range(RAW)]
        hi_ready, lo_ready, slab_used = sig("hi_ready"), sig("lo_ready"), sig("slab_used")
        gather_in, scatter_done = sig("gather_in", 1, 16), sig("scatter_done", 1, 16)
        tx_ready, xh_ready, xl_ready = sig("tx_ready", 2), sig("xh_ready", 2), sig("xl_ready", 2)
        ta_ready, ah_ready, al_ready = sig("ta_ready", 2), sig("ah_ready", 2), sig("al_ready", 2)
        g_ready, s_ready, act_ready, yrow_ready = (sig("g_ready", 2), sig("s_ready", 2), sig("act_ready", 2),
                                                   sig("yrow_ready", 2))
        gidx_ready, sidx_ready, pick_ready = sig("gidx_ready"), sig("sidx_ready"), sig("pick_ready", 2)
        bias_ready = sem("bias_ready")
        dve_moe = Chain(sem("dve_moe"), MOE_LINKS)

        mix_hi, mix_lo = parts("mix_hi", [P, 3 * KT, T], big_base, 8192), parts("mix_lo", [P, 3 * KT, T], keep_base, 0)
        mixT = keep[:, 0:12288].rearrange("p (a n) -> p a n", a=3 * KT)
        mergedT = keep[:, 12288:16384].rearrange("p (a n) -> p a n", a=KT)
        merged_lo = parts("merged_lo", [P, KT, T], keep_base, 12288)
        merged_hi = parts("merged_hi", [P, KT, T], big_base, 20480)
        graw = keep[:, 20480:20480 + GRAW * D].rearrange("p (s n) -> p s n", s=GRAW)
        g_hi = [parts(f"g_hi{n}", [P, KT, P], keep_base, 16384 + 2 * D * n) for n in range(GSPLIT)]
        g_lo = [parts(f"g_lo{n}", [P, KT, P], keep_base, 16384 + 2 * D * n + D) for n in range(GSPLIT)]
        wout_spots = [(big_base, 2 * D * k) for k in range(6)] + [(keep_base, 16384), (keep_base, 16384 + 2 * D)]
        wout_hi = [parts(f"wout_hi{k}", [P, D], base, at) for k, (base, at) in enumerate(wout_spots)]
        wout_lo = [parts(f"wout_lo{k}", [P, D], base, at + D) for k, (base, at) in enumerate(wout_spots)]
        first_raw = conv[:, 0:2].rearrange("p a b -> p (a b)")
        sg = aux[:, 2 * T:4 * T].rearrange("p (a n) -> p a n", a=2)

        raw = big[:, 0:RAW * D].rearrange("p (s n) -> p s n", s=RAW)
        tail = Arena(big, 20480)
        tail.reset(16384)
        xr_sb, gffn_sb, wrt_sb = tail.take(2, D), tail.take(D), tail.take(KT, E)
        zeros = tail.take(32)
        x1_buf = keep[:, 0:2048].rearrange("p (a n) -> p a n", a=2)
        h2_buf = keep[:, 2048:4096].rearrange("p (a n) -> p a n", a=2)
        route_mem = Arena(keep, 12288)
        route_mem.reset(4096 + 4096)
        h2T = route_mem.take(KT, P)
        rt = Arena(keep, 23552)
        rt.reset(12288 + 4096)
        lg, onehot, mask, pos, quo = (rt.take(NT, E), rt.take(NT * TOPK, E), rt.take(NT, E), rt.take(NT, E),
                                      rt.take(NT, E))
        blk, dest, sel = rt.take(NT, E), rt.take(NT, E), rt.take(NT * TOPK, E)
        mv, mif, wgt, wsum, cnt, ov, ova, ovb, ovbase = (
            rt.take(NT, 8), rt.take(NT, TOPK), rt.take(NT, TOPK), rt.take(NT), rt.take(E), rt.take(E), rt.take(E),
            rt.take(E), rt.take(E))
        ovcmp, ovexp, destf = rt.take(NOV + 1, E), rt.take(NOV + 1), rt.take(NT * TOPK)
        mi = sb("mi", [P, NT, 8], U32)
        desti = sb("desti", [P, NT * TOPK], I32)
        pay = sb("pay", [P, NT * TOPK, 2], I32)
        slots = sb("slots", [CAP, NB, 2], I32)
        blk_exp = sb("blk_exp", [P, NB + 1], I32)
        ex = Arena(keep, 8192)
        xg, act_rows, y_rows = (ex.take(D)[0:CAP] for _ in range(3))
        g_buf, u_buf, s_buf = (ex.take(2, 512)[0:CAP] for _ in range(3))
        b12_raw = keep[:, 20480:20480 + 3 * D]

        w_hi = parts("w_hi", [P, SPLIT, D], big_base, RAW * D)
        w_lo = parts("w_lo", [P, SPLIT, D], big_base, (RAW + SPLIT) * D)
        x_hi, x_lo = parts("x_hi", [P, KT, CAP], keep_base, 9216), parts("x_lo", [P, KT, CAP], keep_base, 9216 + D)
        a_hi, a_lo = parts("a_hi", [P, KT, CAP], keep_base, 9216 + 2 * D), parts("a_lo", [P, KT, CAP], keep_base, 9216 + 3 * D)
        bias_hl = parts("bias_hl", [2 * E, 3 * D], keep_base, 13312)
        pick1, pick2 = parts("pick1", [2 * E, CAP], keep_base, 8192), parts("pick2", [2 * E, CAP], keep_base, 8192 + P)
        spare = sb("spare", [CAP, 3])
        spare_used = [sig("spare_used0"), sig("spare_used1")]
        g_idx, s_idx = sb("g_idx", [CAP, 1], I32), sb("s_idx", [CAP, 1], I32)
        w_cur = sb("w_cur", [CAP, 1])
        b12_in, spare_ready = sem("b12_in"), sem("spare_ready")

        x_rows = x.rearrange("a s d -> (a s) d")

        with nc.Block() as block:
            def piece_of(n):
                return n if n < 3 else n + 3

            def steps_of_mixer(eng, body):
                with eng.Fori(0, HEADS - 1) as i:
                    body(i, True)
                body(HEADS - 1, False)


            @block.sync
            def _(sp):
                sp.dma_start(cst[:], consts).then_inc(consts_in, 16)
                sp.dma_start(smalls[:], small).then_inc(consts_in, 16)
                for t in range(NT):
                    sp.dma_start(xin[:, t * D:(t + 1) * D], x_rows[t * P:(t + 1) * P, :]).then_inc(x_in[t], 16)
                sp.dma_start(dT.rearrange("p a b -> p (a b)")[:, 0:KT * SSM_H], w_dt).then_inc(wdt_in, 16)
                sp.dma_start(par_sb[:], par).then_inc(consts_in, 16)
                sp.dma_start(conv.rearrange("p a b -> p (a b)")[0:32, 0:HEADS], rel_bias).then_inc(consts_in, 16)
                sp.dma_start(conv[0:32, 2, 0:GL], onehot_rows).then_inc(consts_in, 16)
                for p in range(MRAW):
                    sp.dma_start(mraw[:, p], w_mix[0, p]).then_inc(piece_in[p].sem, 16)
                sp.wait_ge(dist_read, 1)
                sp.dma_start(dist_rows, conv[0:HEADS, 1, 0:GL]).then_inc(dist_out, 16)
                sp.wait_ge(dist_out, 16)
                sp.dma_start(bias_rows, toeplitz(dist_rows)).then_inc(dist_out, 16)
                sp.wait_ge(dist_out, 32)
                sp.dma_start(biasT[:], bias_rows[0]).then_inc(bias_in.sem, 16)
                for p in range(MRAW, PIECES):
                    sp.wait_ge(plo_ready.sem, plo_ready.at(0, p - MRAW + 1))
                    sp.dma_start(mraw[:, p % MRAW], w_mix[0, p]).then_inc(piece_in[p % MRAW].sem, 16)
                with sp.Fori(0, HEADS - 1) as i:
                    for p in range(PIECES):
                        sp.wait_ge(plo_ready.sem, plo_ready.at(i + 1, p - MRAW + 1))
                        sp.dma_start(mraw[:, p % MRAW], w_mix[bass.ds(i + 1, 1), p].rearrange(
                            "a p n -> (a p) n")).then_inc(piece_in[p % MRAW].sem, 16)
                    sp.wait_ge(logits_ready.sem, logits_ready.at(i, 4))
                    sp.dma_start(biasT[:], bias_rows[bass.ds(i + 1, 1)].rearrange("a p n -> (a p) n")).then_inc(bias_in.sem, 16)

                sp.wait_ge(m0_ready.sem, m0_ready.at(HEADS - 1, 4))
                sp.dma_start(first_raw, w_tail[0]).then_inc(graw_in[0].sem, 16)
                sp.wait_ge(m0_read.sem, m0_read.at(HEADS, 0))
                sp.wait_ge(m1_read.sem, m1_read.at(HEADS, 0))
                sp.dma_start(graw[:, 1], w_tail[1]).then_inc(graw_in[1].sem, 16)

            @block.gpsimd
            def _(pool):
                prime(pool, am_ready, xs_ready, gidx_ready, sidx_ready, pick_ready, *spare_used)
                pool.wait_ge(decays_ready, 3)
                with pool.Fori(0, HEADS) as i:
                    h4 = i * HPG

                    def heads(table, u):
                        return table[:, u, bass.ds(h4, HPG)]

                    def make_am(u):
                        pool.wait_ge(seg_ready.sem, seg_ready.at(i, u))
                        pool.tensor_tensor(am, bcast_mid(tri, HPG), bcast_inner(heads(a_all, u), P),
                                           ALU.mult).then_inc(am_ready.sem, 1)

                    def make_xs(u):
                        pool.wait_ge(m0_read.sem, m0_read.at(i, u + 1))
                        pool.wait_ge(m1_ready.sem, m1_ready.at(i, min(2 * u, 6)))
                        pool.wait_ge(ydiag_ready.sem, ydiag_ready.at(i, u))
                        pool.wait_ge(y_read.sem, y_read.at(i, u))
                        xv = xb[:, u, 0:GW].rearrange("p (h c) -> p h c", h=HPG)
                        for dst, src in ((xdt, heads(dtv, u)), (xw, heads(wend, u))):
                            pool.tensor_tensor(dst.rearrange("p (h c) -> p h c", h=HPG), xv,
                                               bcast_inner(src, HD), ALU.mult)
                        dsk = SMALL["d_skip"][0]
                        pool.tensor_tensor(xd.rearrange("p (h c) -> p h c", h=HPG), xv,
                                           bcast_inner(smalls[:, bass.ds(h4 + dsk, HPG)], HD),
                                           ALU.mult).then_inc(xs_ready.sem, 1)

                    for u in range(NT):
                        make_am(u)
                        make_xs(u)

            @block.scalar
            def _(act):
                prime(act, sigz_ready, phi_ready, ghi_ready, sigm_ready, mhi_ready, taps_ready, silu_ready, proj_read, root_ready, m0_read, decay_ready, exp_ready, yn_ready,
                      osq_ready, oroot_ready, hi_ready, xh_ready, ah_ready, s_ready, yrow_ready)
                ch = act_step
                ch.start(act)
                act.preload_act_table_set("natural_log_exp_and_others")

                act.wait_ge(consts_in, 80)
                act.wait_ge(lam_ready, 1)
                for t in range(NT):
                    xt = xin[:, t * D:(t + 1) * D]
                    act.wait_ge(x_in[t], 16)
                    ch.link(act.activation(sqx, xt, ACT.Square, accum_out=st[:, t:t + 1]))
                    ch.link(act.activation(st[:, t:t + 1], st[:, t:t + 1], ACT.Ln, bias=eps[:, 0:1], scale=1.0 / D))
                    ch.link(act.activation(st[:, t:t + 1], st[:, t:t + 1], ACT.Exp, scale=-0.5))
                    act.activation(xt, xt, ACT.Copy, scale=st[:, t:t + 1]).then_inc(h_ready, 1)
                act.wait_ge(lam_ready, 2)
                ch.link(act.activation(lam_t[:, HD:HD + 2], lam_t[:, HD:HD + 2], ACT.Exp))
                act.activation(ez[:, 0:SSM_H], sm("a_log"), ACT.Exp).then_inc(lam_ready, 1)
                for b in range(2 * NT):
                    t, half = b // 2, b % 2
                    act.wait_ge(hT_read, b + 1)
                    r = (slice(None), slice(4 * half, 4 * half + 4), slice(t * P, (t + 1) * P))
                    act.activation(h_hi[r], hT[r], ACT.Copy).then_inc(hhi_ready, 1)

                def split(j, p):
                    act.wait_ge(piece_in[p % MRAW].sem, piece_in[p % MRAW].at(j, p // MRAW + 1))
                    apart(act, consts_in)
                    if 3 <= p < 6:
                        act.wait_ge(proj_done.sem, proj_done.at(j, 0))
                        act.activation(vz_hi[:, (p - 3) * D:(p - 2) * D], mraw[:, p % MRAW], ACT.Copy).then_inc(
                            phi_ready.sem, 1)
                        return
                    n = p if p < 3 else p - 3
                    if n >= 3:
                        act.wait_ge(proj_done.sem, proj_done.at(j, n - 2))
                    elif not isinstance(j, int):
                        act.wait_ge(proj_done.sem, proj_done.at(j - 1, n + 4))
                    act.activation(wm_hi[n % MSPLIT][:].rearrange("p a b -> p (a b)"), mraw[:, p % MRAW],
                                   ACT.Copy).then_inc(phi_ready.sem, 1)

                def tap(j, n):
                    act.wait_ge(proj_done.sem, proj_done.at(j, n + 1))
                    if n == 3:
                        act.wait_ge(ydiag_ready.sem, ydiag_ready.at(j, 0))
                    elif not isinstance(j, int):
                        act.wait_ge(m0_ready.sem, m0_ready.at(j - 1, 4))
                        if n == 2:
                            act.wait_ge(m1_ready.sem, m1_ready.at(j - 1, 7))
                    apart(act, consts_in)
                    p0 = j * NPAR
                    act.activation(conv[:, n], proj_b[n % 2][:], ACT.Identity,
                                   scale=par_sb[:, bass.ds(p0 + (4 * n + 3), 1)],
                                   bias=par_sb[:, bass.ds(p0 + (16 + n), 1)]).then_inc(taps_ready.sem, 1)

                for p in range(3):
                    split(0, p)
                act.wait_ge(dt_read, 1)
                ch.link(act.activation(eacum[:], wend[:], ACT.Exp, scale=-1.0))
                act.activation(eacum[:], eacum[:], ACT.Ln, bias=1.0).then_inc(dt_read, 1)
                act.wait_ge(hT_banks, 2 * NT)
                for p in range(3, 6):
                    split(0, p)
                act.wait_ge(dist_out, 32)
                tap(0, 0)
                tap(0, 1)
                split(0, 6)
                split(0, 7)
                act.wait_ge(cums_ready, 1)
                cum = y_b[:, 0:384].rearrange("p (k c h) -> p k c h", k=3, c=NT)
                act.activation(eacum[:], cum[:, 0], ACT.Exp).then_inc(decays_ready, 1)
                act.activation(wend[:], cum[:, 1], ACT.Exp)
                act.activation(eaend[:], cum[:, 2], ACT.Exp).then_inc(decays_ready, 1)
                tap(0, 2)
                split(0, 8)
                ch.end()

                ch = act_loop

                def body(i, more):
                    ch.start(act, i)

                    def silu(n):
                        act.wait_ge(conv_ready.sem, conv_ready.at(i, n + 1))
                        act.activation(conv[:, n], conv[:, n], ACT.Silu).then_inc(silu_ready.sem, 1)

                    def squares(n):
                        act.wait_ge(proj_done.sem, proj_done.at(i, 5 + n))
                        act.wait_ge(scores_ready.sem, scores_ready.at(i, 0))
                        act.wait_ge(m1_read.sem, m1_read.at(i, 0))
                        ch.link(act.activation(qk[:, n], proj_b[n][:], ACT.Copy))
                        act.activation(sq[:, n], proj_b[n][:], ACT.Square).then_inc(proj_read.sem, 1)

                    def root(n):
                        act.wait_ge(sums_ready.sem, sums_ready.at(i, n + 1))
                        ch.link(act.activation(sq[:, n], s_b[n][:], ACT.Ln, bias=eps[:, 0:1], scale=1.0 / HD))
                        act.activation(sq[:, n], sq[:, n], ACT.Exp, scale=-0.5).then_inc(root_ready.sem, 1)

                    def take_vz(t):
                        act.wait_ge(proj_done.sem, proj_done.at(i, 7 + t))
                        if t:
                            act.wait_ge(z_ready.sem, z_ready.at(i, t))
                        else:
                            act.wait_ge(m1_ready.sem, m1_ready.at(i, 0))
                            act.wait_ge(y_ready.sem, y_ready.at(i, 0))
                        ch.link(act.activation(vz[:, t], proj_b[t % 2][:, 0:VZ], ACT.Copy))
                        act.activation(ez, proj_b[t % 2][:, P:VZ], ACT.Exp, scale=-1.0).then_inc(proj_read.sem, 1)
                        act.wait_ge(proj_read.sem, proj_read.at(i, 3 + t))
                        ch.link(act.activation(ez, ez, ACT.Ln, bias=1.0))
                        act.activation(ez, ez, ACT.Exp, scale=-1.0).then_inc(sigz_ready.sem, 1)

                    def take_xb(u):
                        act.wait_ge(m0_ready.sem, m0_ready.at(i, u + 1))
                        act.wait_ge(xs_ready.sem, xs_ready.at(i, 0))
                        act.activation(xb[:, u], m0_b[:, 0:3 * P], ACT.Copy).then_inc(m0_read.sem, 1)

                    def make_decay(u):
                        act.wait_ge(seg_ready.sem, seg_ready.at(i, u + 1))
                        act.wait_ge(mix_ready.sem, mix_ready.at(i, u))
                        act.activation(decay.rearrange("p a b -> p (a b)"), seg_b[:], ACT.Exp).then_inc(
                            decay_ready.sem, 1)

                    def softmax_exp(u):
                        n = (u + 1) * P
                        act.wait_ge(max_ready.sem, max_ready.at(i, u + 1))
                        for m in range(2):
                            ins = act.activation(L[:, m, 0:n], L[:, m, 0:n], ACT.Exp, bias=st[:, 8 + m:9 + m],
                                                 accum_out=st[:, 10 + m:11 + m])
                        ins.then_inc(exp_ready.sem, 1)

                    def take_diff(u, k):
                        act.wait_ge(m0_ready.sem, m0_ready.at(i, k))
                        act.wait_ge(m1_ready.sem, m1_ready.at(i, 0))
                        src = m0_b[:, 0:(u + 1) * P].rearrange("p (a b) -> p a b", a=u + 1)
                        act.activation(dT[:, 0:u + 1, u * P:(u + 1) * P], src, ACT.Copy).then_inc(m0_read.sem, 1)

                    def norm_y(u, k):
                        act.wait_ge(y_ready.sem, y_ready.at(i, u + 1))
                        act.wait_ge(m0_ready.sem, m0_ready.at(i, k))
                        ch.link(act.activation(yn[:], ybuf, ACT.Square, accum_out=st[:, 16:17]))
                        ch.link(act.activation(st[:, 16:17], st[:, 16:17], ACT.Ln, bias=eps[:, 1:2], scale=1.0 / GW))
                        ch.link(act.activation(st[:, 16:17], st[:, 16:17], ACT.Exp, scale=-0.5))
                        act.activation(yn[:], ybuf, ACT.Copy, scale=st[:, 16:17]).then_inc(yn_ready.sem, 1)

                    def take_y(u, k):
                        act.wait_ge(m0_ready.sem, m0_ready.at(i, k))
                        apart(act, consts_in)
                        for j in range(2):
                            dst = ssmT[:, bass.ds(i * 2 + j, 1), u * P:(u + 1) * P].rearrange("p a b -> p (a b)")
                            ins = act.activation(dst, m0_b[:, j * P:(j + 1) * P], ACT.Copy,
                                                 scale=par_sb[:, bass.ds(i * NPAR + (20 + j), 1)])
                        ins.then_inc(m0_read.sem, 1)

                    silu(0)
                    silu(1)
                    silu(2)
                    tap(i, 3)
                    silu(3)
                    act.preload_act_table_set("natural_log_exp_and_others")
                    make_decay(0)
                    squares(0)
                    take_xb(0)
                    squares(1)
                    take_xb(1)
                    take_xb(2)
                    root(0)
                    make_decay(1)
                    take_vz(0)
                    root(1)
                    take_xb(3)
                    norm_y(0, 0)
                    softmax_exp(0)
                    take_vz(1)
                    if more:
                        split(i + 1, 0)
                    make_decay(2)
                    take_vz(2)
                    softmax_exp(1)
                    take_diff(0, 5)
                    if more:
                        split(i + 1, 1)
                    take_vz(3)
                    take_diff(1, 6)
                    softmax_exp(2)
                    if more:
                        split(i + 1, 2)
                    take_y(0, 7)
                    norm_y(1, 7)
                    make_decay(3)
                    if more:
                        split(i + 1, 3)
                        tap(i + 1, 0)
                    take_diff(2, 8)
                    take_y(1, 9)
                    softmax_exp(3)
                    if more:
                        split(i + 1, 4)
                    norm_y(2, 9)
                    if more:
                        tap(i + 1, 1)
                    take_diff(3, 10)
                    if more:
                        split(i + 1, 5)
                        split(i + 1, 6)
                        tap(i + 1, 2)
                    take_y(2, 11)
                    norm_y(3, 11)
                    act.wait_ge(m1_ready.sem, m1_ready.at(i, 8))
                    act.activation(sq[:, 0], m1_b[:], ACT.Square).then_inc(osq_ready.sem, 1)
                    if more:
                        split(i + 1, 7)
                    act.wait_ge(osum_ready.sem, osum_ready.at(i, 1))
                    ch.link(act.activation(sq[:, 1], s_b[0][:], ACT.Ln, bias=eps[:, 0:1], scale=1.0 / P))
                    act.activation(sq[:, 1], sq[:, 1], ACT.Exp, scale=-0.5).then_inc(oroot_ready.sem, 1)
                    take_y(3, 12)
                    if more:
                        split(i + 1, 8)
                    else:
                        act.wait_ge(graw_in[0].sem, 16)
                        act.wait_ge(proj_done.sem, proj_done.at(i, 10))
                        act.activation(g_hi[0][:].rearrange("p a b -> p (a b)"), first_raw, ACT.Copy).then_inc(
                            ghi_ready.sem, 1)
                    if more:
                        assert ch.n == ch.per_step, ("links per step", ch.n)

                steps_of_mixer(act, body)

            @block.vector
            def _(dve):
                prime(dve, plo_ready, glo_ready, mlo_ready, conv_ready, z_ready, qk_ready, m1_read, logits_ready, max_ready, diff_ready, cbm_ready,
                      mix_ready, y_read, y_ready, attn_out_read, ssm_out_read, merged_ready, lo_ready, xl_ready,
                      al_ready, g_ready, act_ready)
                ch = dve_step
                ch.start(dve)
                dve.memset(eps[:, 0:1], RMS_EPS)
                ch.link(dve.memset(eps[:, 1:2], SSM_EPS))
                dve.wait_ge(consts_in, 80)
                ch.link(dve.tensor_scalar(sm("qg"), sm("qg"), HD ** -0.5, None, ALU.mult))
                dve.tensor_scalar(sm("subg"), sm("subg"), 1.0 - LAMBDA_INIT, None, ALU.mult).then_inc(lam_ready, 1)
                ch.link(dve.tensor_tensor_reduce(lam_t[:, 0:HD], sm("lq1"), sm("lk1"), 1.0, 0.0, ALU.mult, ALU.add,
                                                 lam_t[:, HD:HD + 1]))
                dve.tensor_tensor_reduce(lam_t[:, 0:HD], sm("lq2"), sm("lk2"), 1.0, 0.0, ALU.mult, ALU.add,
                                         lam_t[:, HD + 1:HD + 2]).then_inc(lam_ready, 1)
                dve.wait_ge(dist_ready, 1)
                ch.link(dve.tensor_copy(conv[0:HEADS, 1, 0:GL], s_b[0][0:HEADS, 0:GL]))
                ch.link(dve.tensor_copy(far[:], s_b[1][:, 0:HEADS]))
                dve.memset(conv[0:HEADS, 1, 256:GL], NEG).then_inc(dist_read, 1)
                dve.wait_ge(lam_ready, 3)
                ch.link(dve.tensor_tensor(eps[:, 2:3], lam_t[:, HD + 1:HD + 2], lam_t[:, HD:HD + 1], ALU.subtract))
                ch.link(dve.tensor_scalar(eps[:, 2:3], eps[:, 2:3], -LAMBDA_INIT, None, ALU.add))
                for b in range(2 * NT):
                    t, half = b // 2, b % 2
                    dve.wait_ge(hT_banks, b + 1)
                    dve.tensor_tensor(hT[:, 4 * half:4 * half + 4, t * P:(t + 1) * P],
                                      bank[b % 2][:].rearrange("p (a b) -> p a b", a=4),
                                      bcast_inner(smalls[:, 4 * half:4 * half + 4], P), ALU.mult).then_inc(hT_read, 1)
                def split(j, p):
                    dve.wait_ge(phi_ready.sem, phi_ready.at(j, p + 1))
                    if 3 <= p < 6:
                        c = slice((p - 3) * D, (p - 2) * D)
                        hi, lo = vz_hi[:, c], vz_lo[:, c]
                    else:
                        n = (p if p < 3 else p - 3) % MSPLIT
                        hi, lo = (w[n][:].rearrange("p a b -> p (a b)") for w in (wm_hi, wm_lo))
                    dve.tensor_tensor(lo, mraw[:, p % MRAW], hi.bitcast(F32), ALU.subtract).then_inc(plo_ready.sem, 1)

                def taps(j, n):
                    dve.wait_ge(taps_ready.sem, taps_ready.at(j, n + 1))
                    for s in (1, 2, 3):
                        w = par_sb[:, bass.ds(j * NPAR + (4 * n + 3 - s), 1)]
                        ins = dve.scalar_tensor_tensor(out=conv[:, n, s:T], in0=proj_b[n % 2][:, 0:T - s],
                                                       scalar=w, in1=conv[:, n, s:T], op0=ALU.mult, op1=ALU.add)
                        if s < 3:
                            ch.link(ins)
                    ins.then_inc(conv_ready.sem, 1)

                for p in range(3):
                    split(0, p)
                dve.wait_ge(dt_ready, 1)
                dproj = m0_b[:, 0:NT * SSM_H].rearrange("p (c h) -> p c h", c=NT)
                ch.link(dve.tensor_tensor(dtv[:], dproj, bcast_mid(sm("dt_bias"), NT), ALU.add))
                ch.link(dve.tensor_scalar(a_all[:], dtv[:], -1.0, None, ALU.mult))
                ch.link(dve.tensor_scalar(eaend[:], dtv[:], 0.0, None, ALU.max))
                dve.tensor_tensor(wend[:], dtv[:], a_all[:], ALU.max).then_inc(dt_read, 1)
                for t in range(NT):
                    r = (slice(None), slice(None), slice(t * P, (t + 1) * P))
                    dve.wait_ge(hhi_ready, 2 * (t + 1))
                    dve.tensor_tensor(h_lo[r], hT[r], h_hi[r].bitcast(F32), ALU.subtract).then_inc(hlo_ready, 1)
                dve.wait_ge(dt_read, 2)
                ch.link(dve.tensor_tensor(dtv[:], eaend[:], eacum[:], ALU.add))
                ch.link(dve.tensor_tensor(a_all[:], dtv[:], bcast_mid(ez[:, 0:SSM_H], NT), ALU.mult))
                dve.tensor_scalar(a_all[:], a_all[:], -1.0, None, ALU.mult).then_inc(a_ready, 1)
                for p in range(3, 6):
                    split(0, p)
                taps(0, 0)
                taps(0, 1)
                split(0, 6)
                split(0, 7)
                dve.wait_ge(decays_ready, 2)
                dve.tensor_tensor(wend[:], wend[:], dtv[:], ALU.mult).then_inc(decays_ready, 1)
                taps(0, 2)
                split(0, 8)
                ch.end()

                ch = dve_loop

                def body(i, more):
                    ch.start(dve, i)

                    def silu_z(t):
                        dve.wait_ge(sigz_ready.sem, sigz_ready.at(i, t + 1))
                        dve.tensor_tensor(vz[:, t, P:VZ], vz[:, t, P:VZ], ez, ALU.mult).then_inc(z_ready.sem, 1)

                    def norm_qk(n):
                        dve.wait_ge(root_ready.sem, root_ready.at(i, n + 1))
                        dve.scalar_tensor_tensor(out=qk[:, n], in0=qk[:, n], scalar=sm("qg" if n == 0 else "kg"),
                                                 in1=sq[:, n], op0=ALU.mult, op1=ALU.mult).then_inc(qk_ready.sem, 1)

                    def masked_cb(u):
                        dve.wait_ge(m1_ready.sem, m1_ready.at(i, 2 * u + 1))
                        dve.wait_ge(mix_ready.sem, mix_ready.at(i, u))
                        dve.tensor_tensor(cbm, m1_b[:, 0:P], tri, ALU.mult).then_inc(m1_read.sem, 1)

                    def logits(u):
                        n = (u + 1) * P
                        near = min(2 * P, n)
                        dve.wait_ge(diff_ready.sem, diff_ready.at(i, u))
                        dve.wait_ge(scores_ready.sem, scores_ready.at(i, u + 1))
                        if u == 0:
                            dve.wait_ge(bias_in.sem, bias_in.at(i, 1))
                        for m in range(2):
                            if n > near:
                                dve.tensor_scalar(L[:, m, 0:n - near], s_b[m][:, 0:n - near],
                                                  far[:, bass.ds(i, 1)], None, ALU.add)
                            ins = dve.tensor_tensor(L[:, m, n - near:n], s_b[m][:, n - near:n],
                                                    biasT[:, 2 * P - near:2 * P], ALU.add)
                        ins.then_inc(logits_ready.sem, 1)
                        dve.wait_ge(logits_ready.sem, logits_ready.at(i, u + 1))
                        ch.link(dve.tensor_reduce(st[:, 8:10], L[:, :, 0:n], AX, ALU.max))
                        dve.tensor_scalar(st[:, 8:10], st[:, 8:10], -1.0, None, ALU.mult).then_inc(max_ready.sem, 1)

                    def make_mix(u):
                        dve.wait_ge(decay_ready.sem, decay_ready.at(i, u + 1))
                        dve.wait_ge(m1_read.sem, m1_read.at(i, 2 * u + 1))
                        dve.wait_ge(ydiag_ready.sem, ydiag_ready.at(i, u))
                        dve.tensor_tensor(mix, decay, bcast_mid(cbm, HPG), ALU.mult).then_inc(mix_ready.sem, 1)

                    def make_diff(u, k):
                        n = (u + 1) * P
                        dve.wait_ge(exp_ready.sem, exp_ready.at(i, u + 1))
                        dve.wait_ge(m0_ready.sem, m0_ready.at(i, k))
                        ch.link(dve.reciprocal(st[:, 12:14], st[:, 10:12]))
                        ch.link(dve.tensor_tensor(st[:, 13:14], st[:, 13:14], eps[:, 2:3], ALU.mult))
                        ch.link(dve.tensor_scalar(diff[:, 0:n], L[:, 0, 0:n], st[:, 12:13], None, ALU.mult))
                        dve.scalar_tensor_tensor(out=diff[:, 0:n], in0=L[:, 1, 0:n], scalar=st[:, 13:14],
                                                 in1=diff[:, 0:n], op0=ALU.mult, op1=ALU.add).then_inc(
                            diff_ready.sem, 1)

                    def next_state(u):
                        dve.wait_ge(m1_ready.sem, m1_ready.at(i, 2 * u + 2))
                        new = m1_b[:, P:P + GW]
                        if u == 0:
                            dve.tensor_copy(state, new).then_inc(m1_read.sem, 1)
                            return
                        s4 = state.rearrange("p (h c) -> p h c", h=HPG)
                        ch.link(dve.tensor_tensor(s4, s4, bcast_inner(eaend[:, u, bass.ds(i * HPG, HPG)], HD),
                                                  ALU.mult))
                        dve.tensor_tensor(state, state, new, ALU.add).then_inc(m1_read.sem, 1)

                    def sum_y(u):
                        dve.wait_ge(ydiag_ready.sem, ydiag_ready.at(i, u + 1))
                        dve.wait_ge(xs_ready.sem, xs_ready.at(i, u + 1))
                        dve.wait_ge(yn_ready.sem, yn_ready.at(i, u))
                        if u:
                            ch.link(dve.tensor_tensor(ybuf, y_b[:, 0:GW], xd, ALU.add))
                            dve.tensor_tensor(ytmp.rearrange("p (h c) -> p h c", h=HPG),
                                              y_b[:, GW:2 * GW].rearrange("p (h c) -> p h c", h=HPG),
                                              bcast_inner(eacum[:, u, bass.ds(i * HPG, HPG)], HD),
                                              ALU.mult).then_inc(y_read.sem, 1)
                            dve.wait_ge(y_read.sem, y_read.at(i, u + 1))
                            ch.link(dve.tensor_tensor(ybuf, ybuf, ytmp, ALU.add))
                        else:
                            dve.tensor_tensor(ybuf, y_b[:, 0:GW], xd, ALU.add).then_inc(y_read.sem, 1)
                            dve.wait_ge(y_read.sem, y_read.at(i, u + 1))

                    def gate_y(u):
                        dve.wait_ge(z_ready.sem, z_ready.at(i, u + 1))
                        dve.tensor_tensor(ybuf, ybuf, vz[:, u, P:VZ], ALU.mult).then_inc(y_ready.sem, 1)

                    taps(i, 3)
                    masked_cb(0)
                    make_mix(0)
                    norm_qk(0)
                    next_state(0)
                    sum_y(0)
                    masked_cb(1)
                    make_mix(1)
                    silu_z(0)
                    norm_qk(1)
                    gate_y(0)
                    logits(0)
                    make_diff(0, 0)
                    next_state(1)
                    sum_y(1)
                    silu_z(1)
                    gate_y(1)
                    if more:
                        split(i + 1, 0)
                    logits(1)
                    masked_cb(2)
                    make_mix(2)
                    make_diff(1, 5)
                    silu_z(2)
                    if more:
                        split(i + 1, 1)
                    logits(2)
                    next_state(2)
                    silu_z(3)
                    sum_y(2)
                    make_diff(2, 6)
                    if more:
                        split(i + 1, 2)
                    masked_cb(3)
                    make_mix(3)
                    logits(3)
                    gate_y(2)
                    if more:
                        split(i + 1, 3)
                        taps(i + 1, 0)
                    make_diff(3, 8)
                    sum_y(3)
                    gate_y(3)
                    if more:
                        taps(i + 1, 1)
                        split(i + 1, 4)
                        split(i + 1, 5)
                        split(i + 1, 6)
                        taps(i + 1, 2)
                        split(i + 1, 7)
                    dve.wait_ge(oroot_ready.sem, oroot_ready.at(i, 1))
                    dve.scalar_tensor_tensor(out=attnT[:, bass.ds(i, 1), :].rearrange("p a b -> p (a b)"),
                                             in0=m1_b[:], scalar=sm("subg"), in1=sq[:, 1], op0=ALU.mult,
                                             op1=ALU.mult).then_inc(m1_read.sem, 1)
                    if more:
                        split(i + 1, 8)
                    else:
                        dve.wait_ge(ghi_ready.sem, ghi_ready.at(0, 1))
                        dve.tensor_tensor(g_lo[0][:].rearrange("p a b -> p (a b)"), first_raw,
                                          g_hi[0][:].rearrange("p a b -> p (a b)").bitcast(F32),
                                          ALU.subtract).then_inc(glo_ready.sem, 1)
                    if more:
                        assert ch.n == ch.per_step, ("links per step", ch.n)

                steps_of_mixer(dve, body)

            @block.tensor
            def _(pe):
                prime(pe, proj_done, sums_ready, m0_ready, m1_ready, seg_ready, scores_ready, ydiag_ready, osum_ready,
                      gpiece_used, slab_used, tx_ready, ta_ready)
                pe.wait_ge(consts_in, 80)
                rb = conv.rearrange("p a b -> p (a b)")[0:32, 0:HEADS]
                pe.matmul(s_b[0][0:HEADS, 0:GL], rb, conv[0:32, 2, 0:GL], start=True, stop=True)
                pe.matmul(s_b[1][:, 0:HEADS], conv[0:32, 2, 0:1].to_broadcast([32, P]), rb,
                          start=True, stop=True).then_inc(dist_ready, 1)
                for b in range(2 * NT):
                    t, half = b // 2, b % 2
                    pe.wait_ge(h_ready, t + 1)
                    if b >= 2:
                        pe.wait_ge(hT_read, b - 1)
                    for k in range(4):
                        c = t * D + (4 * half + k) * P
                        ins = pe.transpose(bank[b % 2][:, k * P:(k + 1) * P], xin[:, c:c + P], ident)
                    ins.then_inc(hT_banks, 1)
                pe.wait_ge(hT_read, 2 * NT)
                pe.wait_ge(wdt_in, 16)
                wdt = dT.rearrange("p a b -> p (a b)")[:, 0:KT * SSM_H].rearrange("p (k h) -> p k h", k=KT)
                for t in range(NT):
                    for k in range(KT):
                        ins = pe.matmul(m0_b[:, t * SSM_H:(t + 1) * SSM_H], hT[:, k, t * P:(t + 1) * P], wdt[:, k],
                                        start=(k == 0), stop=(k == KT - 1))
                ins.then_inc(dt_ready, 1)
                def free_proj(j, use):
                    if use < 2:
                        pe.wait_ge(proj_read.sem, proj_read.at(j, 0))
                    elif use < 6:
                        pe.wait_ge(conv_ready.sem, conv_ready.at(j, use - 1))
                    else:
                        pe.wait_ge(proj_read.sem, proj_read.at(j, use - 5))

                def project(j, n):
                    free_proj(j, n)
                    pe.wait_ge(plo_ready.sem, plo_ready.at(j, piece_of(n) + 1))
                    hi, lo = wm_hi[n % MSPLIT], wm_lo[n % MSPLIT]
                    for k in range(KT):
                        for w, h in ((hi, h_hi), (hi, h_lo), (lo, h_hi)):
                            ins = pe.matmul(proj_b[n % 2][:], w[:, k], h[:, k], start=(k == 0 and w is hi and h is h_hi),
                                            stop=(k == KT - 1 and w is lo))
                    ins.then_inc(proj_done.sem, 1)

                pe.wait_ge(hlo_ready, NT)
                project(0, 0)
                project(0, 1)
                pe.wait_ge(a_ready, 1)
                av = a_all[:].rearrange("p c h -> p (c h)")
                for n, m in enumerate((tri, after, ones)):
                    ins = pe.matmul(y_b[:, n * P:(n + 1) * P], m, av, start=True, stop=True)
                ins.then_inc(cums_ready, 1)
                project(0, 2)
                pe.wait_ge(decays_ready, 3)

                def body(i, more):
                    def project_vz(t):
                        free_proj(i, 6 + t)
                        pe.wait_ge(plo_ready.sem, plo_ready.at(i, 6))
                        hi, lo = (w[:].rearrange("p (a b) -> p a b", a=KT) for w in (vz_hi, vz_lo))
                        for k in range(KT):
                            for h, w in ((h_hi, hi), (h_hi, lo), (h_lo, hi)):
                                ins = pe.matmul(proj_b[t % 2][:, 0:VZ], h[:, k, t * P:(t + 1) * P], w[:, k],
                                                start=(k == 0 and h is h_hi and w is hi),
                                                stop=(k == KT - 1 and h is h_lo))
                        ins.then_inc(proj_done.sem, 1)

                    def turn_xb(u):
                        if u == 0:
                            pe.wait_ge(silu_ready.sem, silu_ready.at(i, 3))
                        pe.wait_ge(m0_read.sem, m0_read.at(i, u))
                        for n in range(3):
                            ins = pe.transpose(m0_b[:, n * P:(n + 1) * P], conv[:, n, u * P:(u + 1) * P], ident)
                        ins.then_inc(m0_ready.sem, 1)

                    def sum_squares(n):
                        pe.wait_ge(proj_read.sem, proj_read.at(i, n + 1))
                        if n == 0:
                            pe.wait_ge(oroot_ready.sem, oroot_ready.at(i, 0))
                            pe.wait_ge(logits_ready.sem, logits_ready.at(i, 0))
                        pe.matmul(s_b[n][:], block_ones, sq[:, n], start=True, stop=True).then_inc(sums_ready.sem, 1)

                    def seg(u):
                        pe.wait_ge(am_ready.sem, am_ready.at(i, u + 1))
                        pe.wait_ge(decay_ready.sem, decay_ready.at(i, u))
                        pe.matmul(seg_b[:], after, am.rearrange("p a b -> p (a b)"), start=True,
                                  stop=True).then_inc(seg_ready.sem, 1)

                    def scores(u):
                        n = (u + 1) * P
                        if u == 0:
                            pe.wait_ge(qk_ready.sem, qk_ready.at(i, 2))
                            pe.wait_ge(root_ready.sem, root_ready.at(i, 2))
                        pe.wait_ge(logits_ready.sem, logits_ready.at(i, u))
                        for m in range(2):
                            r = slice(m * HD, (m + 1) * HD)
                            ins = pe.matmul(s_b[m][:, 0:n], qk[r, 0, u * P:(u + 1) * P], qk[r, 1, 0:n], start=True,
                                            stop=True)
                        ins.then_inc(scores_ready.sem, 1)

                    def cb(u):
                        if u == 0:
                            pe.wait_ge(silu_ready.sem, silu_ready.at(i, 4))
                        pe.wait_ge(m1_read.sem, m1_read.at(i, 2 * u))
                        c = slice(u * P, (u + 1) * P)
                        pe.matmul(m1_b[:, 0:P], conv[:, 2, c], conv[:, 3, c], start=True, stop=True).then_inc(
                            m1_ready.sem, 1)

                    def y_and_state(u):
                        pe.wait_ge(y_read.sem, y_read.at(i, u))
                        pe.wait_ge(mix_ready.sem, mix_ready.at(i, u + 1))
                        pe.wait_ge(xs_ready.sem, xs_ready.at(i, u + 1))
                        for h in range(HPG):
                            ins = pe.matmul(y_b[:, h * HD:(h + 1) * HD], mix[:, h], xdt[:, h * HD:(h + 1) * HD],
                                            start=True, stop=True)
                        if u:
                            pe.wait_ge(m1_read.sem, m1_read.at(i, 2 * u))
                            ins = pe.matmul(y_b[:, GW:2 * GW], conv[:, 3, u * P:(u + 1) * P], state, start=True,
                                            stop=True)
                        ins.then_inc(ydiag_ready.sem, 1)
                        if u < NT - 1:
                            pe.wait_ge(m1_read.sem, m1_read.at(i, 2 * u + 1))
                            pe.matmul(m1_b[:, P:P + GW], xb[:, u, 2 * P:3 * P], xw, start=True, stop=True).then_inc(
                                m1_ready.sem, 1)

                    def turn_diff(u, k):
                        pe.wait_ge(diff_ready.sem, diff_ready.at(i, u + 1))
                        pe.wait_ge(m0_read.sem, m0_read.at(i, k))
                        for j in range(u + 1):
                            ins = pe.transpose(m0_b[:, j * P:(j + 1) * P], diff[:, j * P:(j + 1) * P], ident)
                        ins.then_inc(m0_ready.sem, 1)

                    def turn_y(u, k):
                        pe.wait_ge(yn_ready.sem, yn_ready.at(i, u + 1))
                        pe.wait_ge(m0_read.sem, m0_read.at(i, k))
                        for j in range(2):
                            ins = pe.transpose(m0_b[:, j * P:(j + 1) * P], yn[:, j * P:(j + 1) * P], ident)
                        ins.then_inc(m0_ready.sem, 1)

                    project(i, 3)
                    seg(0)
                    project(i, 4)
                    turn_xb(0)
                    cb(0)
                    project(i, 5)
                    turn_xb(1)
                    sum_squares(0)
                    y_and_state(0)
                    turn_xb(2)
                    seg(1)
                    project_vz(0)
                    sum_squares(1)
                    turn_xb(3)
                    cb(1)
                    project_vz(1)
                    scores(0)
                    y_and_state(1)
                    seg(2)
                    project_vz(2)
                    scores(1)
                    turn_diff(0, 4)
                    cb(2)
                    project_vz(3)
                    scores(2)
                    y_and_state(2)
                    turn_diff(1, 5)
                    seg(3)
                    turn_y(0, 6)
                    if more:
                        project(i + 1, 0)
                    cb(3)
                    turn_diff(2, 7)
                    scores(3)
                    turn_y(1, 8)
                    if more:
                        project(i + 1, 1)
                    y_and_state(3)
                    turn_diff(3, 9)
                    if more:
                        project(i + 1, 2)
                    turn_y(2, 10)
                    pe.wait_ge(m1_read.sem, m1_read.at(i, 7))
                    pe.wait_ge(m0_read.sem, m0_read.at(i, 10))
                    pe.wait_ge(proj_read.sem, proj_read.at(i, 6))
                    for k in range(NT):
                        ins = pe.matmul(m1_b[:, k * P:T], vz[:, k, 0:P], dT[:, k, k * P:T], start=(k == 0),
                                        stop=(k == NT - 1))
                    ins.then_inc(m1_ready.sem, 1)
                    turn_y(3, 11)
                    pe.wait_ge(osq_ready.sem, osq_ready.at(i, 1))
                    pe.wait_ge(logits_ready.sem, logits_ready.at(i, 4))
                    pe.matmul(s_b[0][:], ones, sq[:, 0], start=True, stop=True).then_inc(osum_ready.sem, 1)

                steps_of_mixer(pe, body)

        with nc.Block() as block:
            out_rows = out

            @block.sync
            def _(sp):
                with sp.Fori(0, KT // 2) as i:
                    for m in range(GSTEP):
                        sp.wait_ge(glo_ready.sem, glo_ready.at(i, m + 1))
                        sp.dma_start(graw[:, m % GRAW], w_tail[bass.ds(i * GSTEP + (m + GRAW), 1)].rearrange(
                            "a p n -> (a p) n")).then_inc(graw_in[m % GRAW].sem, 16)
                N = KT * TILE_PIECES
                for q in range(N + GRAW, N + KT):
                    sp.wait_ge(glo_ready.sem, glo_ready.at(0, q - GRAW + 1))
                    sp.dma_start(graw[:, q % GRAW], w_tail[q]).then_inc(graw_in[q % GRAW].sem, 16)
                sp.wait_ge(gpiece_used.sem, gpiece_used.at(0, N))
                sp.dma_start(gffn_sb, gffn).then_inc(gffn_in, 16)
                sp.dma_start(wrt_sb.rearrange("p a b -> p (a b)"), w_rt).then_inc(wrt_in, 16)
                for t in range(2):
                    sp.dma_start(xr_sb[:, t], x_rows[t * P:(t + 1) * P, :]).then_inc(xr_in[t], 16)
                sp.dma_start(slot_rows.rearrange("(s b) c -> s (b c)", s=CAP), pads).then_inc(pads_out, 16)
                sp.dma_start(pay[:].rearrange("p a b -> p (a b)"), tok_ids).then_inc(wrt_in, 16)
                sp.wait_ge(zero_ready, 1)
                sp.dma_start(h2_rows[T:ROWS, :], zero_rows(zeros)).then_inc(pads_out, 16)
                sp.dma_start(out_rows[T:ROWS, :], zero_rows(zeros)).then_inc(pads_out, 16)
                sp.wait_ge(pads_out, 48)
                for t in range(NT):
                    rows = slice(t * P, (t + 1) * P)
                    sp.wait_ge(x1_ready, 2 * (t + 1))
                    if t < 2:
                        sp.dma_start(xr_sb[:, t], x_rows[(t + 2) * P:(t + 3) * P, :]).then_inc(
                            xr_in[t + 2], 16)
                    sp.dma_start(out_rows[rows, :], x1_buf[:, t % 2]).then_inc(x1_out, 16)
                    sp.wait_ge(h2_ready, t + 1)
                    sp.dma_start(h2_rows[rows, :], h2_buf[:, t % 2]).then_inc(h2_out, 16)
                    sp.wait_ge(x1_out, 16 * (t + 1))
                    sp.wait_ge(h2_out, 16 * (t + 1))
                sp.wait_ge(res_ready, NT)
                for n in range(RAW):
                    sp.dma_start(raw[:, n], w1[0, n // 2, :, (n % 2) * D:(n % 2 + 1) * D]).then_inc(raw_in[n], 16)
                sp.dma_start(b12_raw[0:E, :], b12).then_inc(b12_in, 16)
                sp.wait_ge(slots_out, 16 * NT * TOPK)
                sp.dma_start(slots[:].rearrange("s b c -> s (b c)"),
                             slot_rows.rearrange("(s b) c -> s (b c)", s=CAP)).then_inc(slots_in, 16)
                sp.wait_ge(slots_in, 16)
                sp.wait_ge(b12_in, 16)

            @block.tensor
            def _(pe):
                def piece(i, m, to, x, start, stop):
                    pe.wait_ge(glo_ready.sem, glo_ready.at(i, m + 1))
                    hi, lo = g_hi[m % GSPLIT], g_lo[m % GSPLIT]
                    x_hi_, x_lo_ = (h_hi, h_lo) if x is None else (mix_hi, mix_lo)
                    for k in range(KT):
                        for w, v in ((hi, x_hi_), (hi, x_lo_), (lo, x_hi_)):
                            ins = pe.matmul(bank[to][:], w[:, k], v[:, (x or 0) + k],
                                            start=(start and k == 0 and w is hi and v is x_hi_),
                                            stop=(stop and k == KT - 1 and w is lo))
                    ins.then_inc(gpiece_used.sem, 1)

                with pe.Fori(0, KT // 2) as i:
                    for j in range(2):
                        m = j * TILE_PIECES
                        for g in range(2):
                            pe.wait_ge(sigm_ready.sem, sigm_ready.at(i, 2 * j))
                            piece(i, m + g, g, None, True, True)
                        pe.wait_ge(attn_out_read.sem, attn_out_read.at(i, j))
                        pe.wait_ge(mixlo_ready, KT // 2)
                        piece(i, m + 2, 2, 0, True, True)
                        pe.wait_ge(ssm_out_read.sem, ssm_out_read.at(i, j))
                        pe.wait_ge(mixlo_ready, KT)
                        piece(i, m + 3, 3, KT, True, False)
                        pe.wait_ge(mixlo_ready, 3 * KT // 2)
                        piece(i, m + 4, 3, 2 * KT, False, True)
                def residual(t):
                    if t >= 2:
                        pe.wait_ge(x1_ready, 2 * (t - 1))
                    for k in range(KT):
                        pe.wait_ge(mlo_ready.sem, mlo_ready.at(0, k + 1))
                        pe.wait_ge(glo_ready.sem, glo_ready.at(0, KT * TILE_PIECES + k + 1))
                        for v, w in ((merged_hi, wout_hi[k]), (merged_hi, wout_lo[k]), (merged_lo, wout_hi[k])):
                            for half in range(2):
                                ins = pe.matmul(bank[2 * (t % 2) + half][:], v[:, k, t * P:(t + 1) * P],
                                                w[:, half * 512:(half + 1) * 512],
                                                start=(k == 0 and v is merged_hi and w is wout_hi[k]),
                                                stop=(k == KT - 1 and v is merged_lo))
                    ins.then_inc(res_ready, 1)

                def router(t):
                    pe.wait_ge(h2_ready, t + 1)
                    if t:
                        pe.wait_ge(h2T_read, 2 * t)
                    for half in range(2):
                        for k in range(4):
                            c = (4 * half + k) * P
                            ins = pe.transpose(bank[4 + half][:, k * P:(k + 1) * P], h2_buf[:, t % 2, c:c + P], ident)
                        ins.then_inc(h2T_ready, 1)
                    pe.wait_ge(h2T_read, 2 * (t + 1))
                    pe.wait_ge(wrt_in, 32)
                    for k in range(KT):
                        ins = pe.matmul(bank[6][:, t * E:(t + 1) * E], h2T[:, k], wrt_sb[:, k], start=(k == 0),
                                        stop=(k == KT - 1))
                    ins.then_inc(logit_ready, 1)

                residual(0)
                for t in range(1, NT):
                    residual(t)
                    router(t - 1)
                router(NT - 1)
                pe.wait_ge(mask_ready, 1)
                for t in range(NT):
                    for s in range(t + 1):
                        ins = pe.matmul(bank[7][:, t * E:(t + 1) * E], tri if s == t else ones, mask[:, s],
                                        start=(s == 0), stop=(s == t))
                for s in range(NT):
                    ins = pe.matmul(bank[7][:, NT * E:(NT + 1) * E], ones, mask[:, s], start=(s == 0),
                                    stop=(s == NT - 1))
                ins.then_inc(pos_ready, 1)

            @block.scalar
            def _(act):
                def split(i, m):
                    act.wait_ge(graw_in[m % GRAW].sem, graw_in[m % GRAW].at(i, m // GRAW + 1))
                    act.activation(g_hi[m % GSPLIT][:].rearrange("p a b -> p (a b)"), graw[:, m % GRAW],
                                   ACT.Copy).then_inc(ghi_ready.sem, 1)

                def split_out(k, used):
                    q = KT * TILE_PIECES + k
                    act.wait_ge(gpiece_used.sem, gpiece_used.at(0, used))
                    act.wait_ge(graw_in[q % GRAW].sem, graw_in[q % GRAW].at(0, q // GRAW + 1))
                    act.activation(wout_hi[k][:], graw[:, q % GRAW], ACT.Copy).then_inc(ghi_ready.sem, 1)

                def ahead(i, m):
                    if isinstance(i, int) and i > 0 and m + GSPLIT >= GSTEP:
                        split_out(m + GSPLIT - GSTEP, KT * TILE_PIECES - 3)
                        return
                    act.wait_ge(gpiece_used.sem, gpiece_used.at(i, m + 1))
                    n = m + GSPLIT
                    act.wait_ge(graw_in[n % GRAW].sem, graw_in[n % GRAW].at(i, n // GRAW + 1))
                    act.activation(g_hi[n % GSPLIT][:].rearrange("p a b -> p (a b)"), graw[:, n % GRAW],
                                   ACT.Copy).then_inc(ghi_ready.sem, 1)

                def split_mix(a, b):
                    for n in range(a, b):
                        act.activation(mix_hi[:, 2 * n:2 * n + 2], mixT[:, 2 * n:2 * n + 2], ACT.Copy).then_inc(
                            mixhi_ready, 1)

                split(0, 1)
                split_mix(0, KT // 2)

                def body(i):
                    for j in range(2):
                        m = j * TILE_PIECES
                        for g in range(2):
                            act.wait_ge(attn_out_read.sem if g == 0 else ssm_out_read.sem,
                                        (attn_out_read if g == 0 else ssm_out_read).at(i, j))
                            act.wait_ge(gpiece_used.sem, gpiece_used.at(i, m + g + 1))
                            act.activation(sg[:, g], bank[g][:], ACT.Sigmoid).then_inc(sigm_ready.sem, 1)
                            ahead(i, m + g)
                            if isinstance(i, int) and i == j == 0:
                                split_mix((g + 1) * KT // 2, (g + 2) * KT // 2)
                        for n in (2, 3, 4):
                            ahead(i, m + n)
                        act.wait_ge(merged_ready.sem, merged_ready.at(i, j + 1))
                        apart(act, consts_in)
                        r = (slice(None), bass.ds(2 * i + j, 1), slice(None))
                        act.activation(merged_hi[r].rearrange("p a b -> p (a b)"),
                                       mergedT[r].rearrange("p a b -> p (a b)"), ACT.Copy).then_inc(mhi_ready.sem, 1)

                body(0)
                with act.Fori(1, KT // 2 - 1) as i:
                    body(i)
                body(KT // 2 - 1)
                N = KT * TILE_PIECES
                for k in range(2, KT):
                    split_out(k, N - 3 if k < 4 else N - 2 if k < 6 else N)
                ch = act_step
                ch.start(act)
                act.preload_act_table_set("natural_log_exp_and_others")
                for t in range(NT):
                    act.wait_ge(x1_ready, 2 * (t + 1))
                    if t >= 2:
                        act.wait_ge(h2_out, 16 * (t - 1))
                        act.wait_ge(h2T_ready, 2 * (t - 1))
                    else:
                        act.wait_ge(gpiece_used.sem, gpiece_used.at(KT // 2, 0))
                    h2 = h2_buf[:, t % 2]
                    ch.link(act.activation(h2, x1_buf[:, t % 2], ACT.Square, accum_out=st[:, 20:21]))
                    ch.link(act.activation(st[:, 20:21], st[:, 20:21], ACT.Ln, bias=eps[:, 0:1], scale=1.0 / D))
                    ch.link(act.activation(st[:, 20:21], st[:, 20:21], ACT.Exp, scale=-0.5))
                    act.activation(h2, x1_buf[:, t % 2], ACT.Copy, scale=st[:, 20:21]).then_inc(x1n_ready, 1)
                    for half in range(2):
                        act.wait_ge(h2T_ready, 2 * t + half + 1)
                        if t:
                            act.wait_ge(logit_ready, t)
                        act.activation(h2T[:, 4 * half:4 * half + 4],
                                       bank[4 + half][:].rearrange("p (a b) -> p a b", a=4),
                                       ACT.Copy).then_inc(h2T_read, 1)
                act.wait_ge(rt_exp, 1)
                act.activation(wgt, wgt, ACT.Exp).then_inc(rt_exp, 1)
                ch.end()

            @block.vector
            def _(dve):
                def split(i, m):
                    dve.wait_ge(ghi_ready.sem, ghi_ready.at(i, m + 1))
                    if isinstance(i, int) and i * GSTEP + m >= KT * TILE_PIECES:
                        k = i * GSTEP + m - KT * TILE_PIECES
                        hi, lo = wout_hi[k][:], wout_lo[k][:]
                    else:
                        hi, lo = (w[m % GSPLIT][:].rearrange("p a b -> p (a b)") for w in (g_hi, g_lo))
                    dve.tensor_tensor(lo, graw[:, m % GRAW], hi.bitcast(F32), ALU.subtract).then_inc(glo_ready.sem, 1)

                def split_mix(a, b):
                    for n in range(a, b):
                        r = (slice(None), slice(2 * n, 2 * n + 2))
                        dve.wait_ge(mixhi_ready, n + 1)
                        dve.tensor_tensor(mix_lo[r], mixT[r], mix_hi[r].bitcast(F32), ALU.subtract).then_inc(
                            mixlo_ready, 1)

                split(0, 1)
                split_mix(0, KT // 2)

                def body(i):
                    for j in range(2):
                        m = j * TILE_PIECES
                        r = (slice(None), bass.ds(2 * i + j, 1), slice(None))
                        merged = mergedT[r].rearrange("p a b -> p (a b)")
                        for n in (0, 1, 2):
                            split(i, m + n + GSPLIT)
                            if isinstance(i, int) and i == j == 0 and n < 2:
                                split_mix((n + 1) * KT // 2, (n + 2) * KT // 2)
                        dve.wait_ge(gpiece_used.sem, gpiece_used.at(i, m + 3))
                        dve.wait_ge(sigm_ready.sem, sigm_ready.at(i, 2 * j + 1))
                        dve.tensor_tensor(L[:, 0], bank[2][:], sg[:, 0], ALU.mult).then_inc(attn_out_read.sem, 1)
                        for n in (3, 4):
                            split(i, m + n + GSPLIT)
                        dve.wait_ge(gpiece_used.sem, gpiece_used.at(i, m + 5))
                        dve.wait_ge(sigm_ready.sem, sigm_ready.at(i, 2 * j + 2))
                        dve.tensor_tensor(L[:, 1], bank[3][:], sg[:, 1], ALU.mult).then_inc(ssm_out_read.sem, 1)
                        dve.wait_ge(attn_out_read.sem, attn_out_read.at(i, j + 1))
                        dve.wait_ge(ssm_out_read.sem, ssm_out_read.at(i, j + 1))
                        dve.tensor_tensor(merged, L[:, 0], L[:, 1], ALU.add).then_inc(merged_ready.sem, 1)
                        dve.wait_ge(mhi_ready.sem, mhi_ready.at(i, j + 1))
                        dve.tensor_tensor(merged_lo[r].rearrange("p a b -> p (a b)"), merged,
                                          merged_hi[r].rearrange("p a b -> p (a b)").bitcast(F32),
                                          ALU.subtract).then_inc(mlo_ready.sem, 1)

                body(0)
                with dve.Fori(1, KT // 2 - 1) as i:
                    body(i)
                body(KT // 2 - 1)
                for k in range(2, KT):
                    split(KT // 2, k)
                dve.wait_ge(gpiece_used.sem, gpiece_used.at(KT // 2, 0))
                dve.memset(zeros, 0.0).then_inc(zero_ready, 1)
                ch = dve_step
                ch.start(dve)
                dve.wait_ge(gffn_in, 16)

                def residual(t):
                    dve.wait_ge(xr_in[t], 16)
                    if t >= 2:
                        dve.wait_ge(x1_out, 16 * (t - 1))
                        dve.wait_ge(x1n_ready, t - 1)
                    dve.wait_ge(res_ready, t + 1)
                    for half in range(2):
                        c = slice(half * 512, (half + 1) * 512)
                        dve.tensor_tensor(x1_buf[:, t % 2, c], bank[2 * (t % 2) + half][:], xr_sb[:, t % 2, c],
                                          ALU.add).then_inc(x1_ready, 1)

                def gain(t):
                    dve.wait_ge(x1n_ready, t + 1)
                    dve.tensor_tensor(h2_buf[:, t % 2], h2_buf[:, t % 2], gffn_sb, ALU.mult).then_inc(h2_ready, 1)

                for t in range(NT):
                    residual(t)
                    gain(t)
                dve.wait_ge(logit_ready, NT)
                ch.link(dve.tensor_tensor(lg, bank[6][:, 0:NT * E].rearrange("p (t e) -> p t e", t=NT),
                                          bcast_mid(sm("b_router"), NT), ALU.add))
                for t in range(NT):
                    ch.link(dve.max(mv[:, t], lg[:, t]))
                    ch.link(dve.max_index(mi[:, t], mv[:, t], lg[:, t]))
                ch.link(dve.tensor_copy(mif, mi[:, :, 0:TOPK]))
                dve.tensor_tensor(wgt, mv[:, :, 0:TOPK], mv[:, :, 0:1].to_broadcast([P, NT, TOPK]),
                                  ALU.subtract).then_inc(rt_exp, 1)
                iota_e = cn("iota_e")
                ch.link(dve.tensor_tensor(onehot, bcast_mid(iota_e, NT * TOPK),
                                          bcast_inner(mif.rearrange("p t k -> p (t k)"), E), ALU.is_equal))
                for t in range(NT):
                    ins = dve.tensor_reduce(mask[:, t], onehot[:, TOPK * t:TOPK * (t + 1)].rearrange("p k e -> p e k"),
                                            AX, ALU.add)
                ins.then_inc(mask_ready, 1)
                dve.wait_ge(rt_exp, 2)
                ch.link(dve.tensor_reduce(wsum, wgt, AX, ALU.add))
                ch.link(dve.reciprocal(wsum, wsum))
                dve.wait_ge(wrt_in, 32)
                ch.link(dve.tensor_tensor(pay[:, :, 1:2].bitcast(F32).rearrange("p (t k) o -> p t (k o)", t=NT), wgt,
                                          bcast_inner(wsum, TOPK), ALU.mult))
                dve.wait_ge(pos_ready, 1)
                dve.wait_ge(mask_ready, 1)
                ch.link(dve.tensor_tensor(pos, bank[7][:, 0:NT * E].rearrange("p (t e) -> p t e", t=NT), mask,
                                          ALU.subtract))
                ch.link(dve.tensor_copy(cnt, bank[7][:, NT * E:(NT + 1) * E]))
                ch.link(dve.tensor_scalar(quo, pos, float(CAP), None, ALU.is_ge))
                ch.link(dve.tensor_scalar(ov, cnt, float(CAP), None, ALU.is_gt))
                for j in range(2, MAXQ + 1):
                    ch.link(dve.scalar_tensor_tensor(out=quo, in0=pos, scalar=float(j * CAP), in1=quo,
                                                     op0=ALU.is_ge, op1=ALU.add))
                    ch.link(dve.scalar_tensor_tensor(out=ov, in0=cnt, scalar=float(j * CAP), in1=ov,
                                                     op0=ALU.is_gt, op1=ALU.add))
                src, dst = ov, ova
                for s in (1, 2, 4, 8, 16):
                    ch.link(dve.tensor_copy(dst[:, 0:s], src[:, 0:s]))
                    ch.link(dve.tensor_tensor(dst[:, s:E], src[:, s:E], src[:, 0:E - s], ALU.add))
                    src, dst = dst, (ovb if dst is ova else ova)
                ovend = src
                ch.link(dve.tensor_tensor(ovbase, ovend, ov, ALU.subtract))
                ch.link(dve.tensor_tensor(ovbase, ovbase, iota_e, ALU.subtract))
                ch.link(dve.tensor_scalar(ovbase, ovbase, float(E - 1), None, ALU.add))
                ch.link(dve.tensor_tensor(blk, quo, bcast_mid(ovbase, NT), ALU.add))
                ch.link(dve.scalar_tensor_tensor(out=blk, in0=quo, scalar=1.0, in1=blk, op0=ALU.is_ge,
                                                 op1=ALU.mult))
                ch.link(dve.tensor_tensor(blk, blk, bcast_mid(iota_e, NT), ALU.add))
                ch.link(dve.scalar_tensor_tensor(out=dest, in0=quo, scalar=-float(CAP), in1=pos, op0=ALU.mult,
                                                 op1=ALU.add))
                ch.link(dve.scalar_tensor_tensor(out=dest, in0=dest, scalar=float(NB), in1=blk, op0=ALU.mult,
                                                 op1=ALU.add))
                for t in range(NT):
                    ch.link(dve.tensor_tensor(sel[:, TOPK * t:TOPK * (t + 1)], onehot[:, TOPK * t:TOPK * (t + 1)],
                                              bcast_mid(dest[:, t], TOPK), ALU.mult))
                ch.link(dve.tensor_reduce(destf, sel, AX, ALU.add))
                dve.tensor_copy(desti[:], destf).then_inc(dest_ready, 1)
                ch.link(dve.tensor_tensor(ovcmp, bcast_mid(ovend, NOV + 1), bcast_inner(cn("iota_b"), E), ALU.is_le))
                ch.link(dve.tensor_reduce(ovexp, ovcmp, AX, ALU.add))
                ch.link(dve.tensor_scalar(ovexp, ovexp, float(E - 1), None, ALU.min))
                ch.link(dve.tensor_copy(blk_exp[:, E:NB], ovexp))
                ch.link(dve.tensor_copy(blk_exp[:, 0:E], iota_e))
                dve.tensor_copy(blk_exp[:, NB:NB + 1], ovend[:, E - 1:E]).then_inc(dest_ready, 1)
                ch.end()

            @block.gpsimd
            def _(pool):
                pool.wait_ge(dest_ready, 1)
                pool.wait_ge(pads_out, 48)
                for n in range(NT * TOPK):
                    pool.indirect_dma_start(slot_rows, bass.IndirectOffsetOnAxis(ap=desti[:, n:n + 1], axis=0),
                                            pay[:, n, :], None).then_inc(slots_out, 16)
                pool.wait_ge(slots_out, 16 * NT * TOPK)

        with nc.Block() as block:
            def count(b, n):
                return n + 1 if isinstance(b, int) and b == 0 else b * SLABS + (n - 7)

            def place(b, n, ring):
                return (n if isinstance(b, int) and b == 0 else n - 8) % ring

            def raw_count(b, n):
                first = isinstance(b, int) and b == 0
                return (n // RAW + 1) if first else b * (SLABS // RAW) + ((n - 8) // RAW + 1)

            def steps(eng, body, last):
                many = eng.value_load(blk_exp[0:1, NB:NB + 1], min_val=0, max_val=NOV)
                body(0)
                body(1)
                with eng.Fori(2, E) as b:
                    body(b)
                with eng.If(many > 0):
                    with eng.Fori(0, NOV) as o:
                        with eng.If(o < many):
                            body(o + E)
                last(many + E)

            @block.sync
            def _(sp):
                def load(b, n, at_n, e):
                    c = count(b, at_n)
                    if not isinstance(b, int) or b > 0 or at_n >= RAW:
                        sp.wait_ge(lo_ready.sem, c - RAW + 1)
                    if n < 16:
                        src = w1[bass.ds(e, 1), n // 2, :, (n % 2) * D:(n % 2 + 1) * D]
                    else:
                        src = w2[bass.ds(e, 1), n - 16]
                    s = place(b, at_n, RAW)
                    sp.dma_start(raw[:, s], src.rearrange("a p n -> (a p) n")).then_inc(raw_in[s], 16)

                def expert(b):
                    return sp.value_load(blk_exp[0:1, bass.ds(b, 1)], min_val=0, max_val=E - 1)

                def body(b):
                    if isinstance(b, int) and b == 0:
                        for n in range(RAW, 16):
                            load(0, n, n, 0)
                        return
                    e = b if isinstance(b, int) else expert(b)
                    for n in range(16):
                        load(b, n, n, e)
                    e = b - 1 if isinstance(b, int) else expert(b - 1)
                    for n in range(16, SLABS):
                        load(b, n, n, e)

                def last(b):
                    e = expert(b - 1)
                    for n in range(16, SLABS):
                        load(b, n, n - 16, e)

                steps(sp, body, last)

            @block.tensor
            def _(pe):
                def turn_x(b):
                    pe.wait_ge(gather_in.sem, gather_in.at(b, 1))
                    for half in range(2):
                        if not isinstance(b, int) or b > 1:
                            pe.wait_ge(al_ready.sem, al_ready.at(b - 2, half + 1))
                        for k in range(4):
                            c = (4 * half + k) * P
                            ins = pe.transpose(bank[6 + half][:, k * CAP:(k + 1) * CAP], xg[:, c:c + P],
                                               ident[0:CAP, 0:CAP])
                        ins.then_inc(tx_ready.sem, 1)

                def turn_act(b):
                    for half in range(2):
                        pe.wait_ge(act_ready.sem, act_ready.at(b, half + 1))
                        pe.wait_ge(xl_ready.sem, xl_ready.at(b + 1, half + 1))
                        for k in range(4):
                            c = (4 * half + k) * P
                            ins = pe.transpose(bank[6 + half][:, k * CAP:(k + 1) * CAP], act_rows[:, c:c + P],
                                               ident[0:CAP, 0:CAP])
                        ins.then_inc(ta_ready.sem, 1)

                def slab(b, at_n, hi, lo, banks, stop):
                    pe.wait_ge(lo_ready.sem, count(b, at_n) + 1)
                    s = place(b, at_n, SPLIT)
                    for x_part, w_part in ((hi, w_hi), (hi, w_lo), (lo, w_hi)):
                        for c in range(2):
                            ins = pe.matmul(banks[c][0:CAP], x_part, w_part[:, s, c * 512:(c + 1) * 512], start=False,
                                            stop=stop and w_part is w_hi and x_part is lo)
                    ins.then_inc(slab_used.sem, 1)

                def first(b):
                    pe.wait_ge(xl_ready.sem, xl_ready.at(b, 2))
                    pe.wait_ge(act_ready.sem, act_ready.at(b, 0))
                    pe.wait_ge(pick_ready.sem, pick_ready.at(b, 1))
                    for c in range(4):
                        pe.matmul(bank[c][0:CAP], pick1[:], bias_hl[:, c * 512:(c + 1) * 512], start=True, stop=False)
                    for n in range(16):
                        slab(b, n, x_hi[:, n // 2], x_lo[:, n // 2], bank[2 * (n % 2):2 * (n % 2) + 2], n >= 14)

                def second(b, step, at):
                    pe.wait_ge(al_ready.sem, al_ready.at(b, 2))
                    pe.wait_ge(yrow_ready.sem, yrow_ready.at(b, 0))
                    pe.wait_ge(pick_ready.sem, pick_ready.at(b, 2))
                    for c in range(2):
                        pe.matmul(bank[4 + c][0:CAP], pick2[:], bias_hl[:, 2 * D + c * 512:2 * D + (c + 1) * 512],
                                  start=True, stop=False)
                    for n in range(8):
                        slab(step, at + n, a_hi[:, n], a_lo[:, n], bank[4:6], n == 7)

                def body(b):
                    first(b)
                    turn_x(b + 1)
                    if not isinstance(b, int) or b > 0:
                        second(b - 1, b, 16)
                    turn_act(b)

                turn_x(0)
                steps(pe, body, lambda b: second(b - 1, b, 0))

            def take_turned(eng, b, ready, hi, lo, hi_ready_, lo_ready_):
                for half in range(2):
                    src = bank[6 + half][:, 0:4 * CAP].rearrange("p (a b) -> p a b", a=4)
                    k = slice(4 * half, 4 * half + 4)
                    if eng is nc.scalar:
                        eng.wait_ge(ready.sem, ready.at(b, half + 1))
                        eng.activation(hi[:, k], src, ACT.Copy).then_inc(hi_ready_.sem, 1)
                    else:
                        eng.wait_ge(hi_ready_.sem, hi_ready_.at(b, half + 1))
                        eng.tensor_tensor(lo[:, k], src, hi[:, k].bitcast(F32), ALU.subtract).then_inc(
                            lo_ready_.sem, 1)

            @block.scalar
            def _(act):
                def split(b, at_n):
                    act.wait_ge(raw_in[place(b, at_n, RAW)], raw_count(b, at_n) * 16)
                    c = count(b, at_n)
                    if not isinstance(b, int) or b > 0 or at_n >= SPLIT:
                        act.wait_ge(slab_used.sem, c - SPLIT + 1)
                    act.activation(w_hi[:, place(b, at_n, SPLIT)], raw[:, place(b, at_n, RAW)], ACT.Copy).then_inc(
                        hi_ready.sem, 1)

                def take_x(b):
                    take_turned(nc.scalar, b, tx_ready, x_hi, x_lo, xh_ready, xl_ready)

                def take_act(b):
                    take_turned(nc.scalar, b, ta_ready, a_hi, a_lo, ah_ready, al_ready)

                def swish(b, c):
                    act.wait_ge(g_ready.sem, g_ready.at(b, c + 1))
                    act.activation(s_buf[:, c], g_buf[:, c], ACT.Sigmoid, scale=SWIGLU_ALPHA).then_inc(s_ready.sem, 1)

                def take_y(b, step, at_n):
                    act.wait_ge(slab_used.sem, count(step, at_n) + 1)
                    act.wait_ge(sidx_ready.sem, sidx_ready.at(b, 1))
                    for c in range(2):
                        act.activation(y_rows[:, c * 512:(c + 1) * 512], bank[4 + c][0:CAP], ACT.Copy,
                                       scale=w_cur[:, 0:1]).then_inc(yrow_ready.sem, 1)

                def body(b):
                    peeled = isinstance(b, int)
                    for n in range(SLABS):
                        if n == 5 and (not peeled or b > 0):
                            take_act(b - 1)
                        if n == 6 and (not peeled or b > 1):
                            take_y(b - 2, b - 1, SLABS - 1)
                        if n < 16 or not peeled or b > 0:
                            split(b, n)
                        if n == 21:
                            take_x(b + 1)
                            swish(b, 0)
                        if n == 22:
                            swish(b, 1)

                def last(b):
                    for n in range(8):
                        if n == 5:
                            take_act(b - 1)
                        split(b, n)
                        if n == 5:
                            take_y(b - 2, b - 1, SLABS - 1)
                    take_y(b - 1, b, 7)

                act.activation(bias_hl[0:E, :], b12_raw[0:E, :], ACT.Copy).then_inc(bias_ready, 1)
                take_x(0)
                steps(act, body, last)

            @block.vector
            def _(dve):
                ch = dve_moe

                def split(b, at_n):
                    dve.wait_ge(hi_ready.sem, count(b, at_n) + 1)
                    s = place(b, at_n, SPLIT)
                    dve.tensor_tensor(w_lo[:, s], raw[:, place(b, at_n, RAW)], w_hi[:, s].bitcast(F32),
                                      ALU.subtract).then_inc(lo_ready.sem, 1)

                def take_x(b):
                    take_turned(nc.vector, b, tx_ready, x_hi, x_lo, xh_ready, xl_ready)

                def take_act(b):
                    take_turned(nc.vector, b, ta_ready, a_hi, a_lo, ah_ready, al_ready)

                def clamp_gate(b, c):
                    dve.wait_ge(slab_used.sem, count(b, 15) + 1)
                    dve.wait_ge(act_ready.sem, act_ready.at(b, 0))
                    dve.tensor_scalar(g_buf[:, c], bank[c][0:CAP], SWIGLU_LIMIT, None, ALU.min).then_inc(g_ready.sem, 1)

                def swiglu(b, c):
                    ch.link(dve.tensor_scalar(u_buf[:, c], bank[2 + c][0:CAP], SWIGLU_LIMIT, -SWIGLU_LIMIT, ALU.min,
                                              ALU.max))
                    dve.wait_ge(s_ready.sem, s_ready.at(b, c + 1))
                    ch.link(dve.tensor_tensor(g_buf[:, c], g_buf[:, c], s_buf[:, c], ALU.mult))
                    dve.wait_ge(ta_ready.sem, ta_ready.at(b, 0))
                    dve.scalar_tensor_tensor(out=act_rows[:, c * 512:(c + 1) * 512], in0=u_buf[:, c], scalar=1.0,
                                             in1=g_buf[:, c], op0=ALU.add, op1=ALU.mult).then_inc(act_ready.sem, 1)

                def body(b):
                    peeled = isinstance(b, int)
                    ch.start(dve, b)
                    for n in range(SLABS):
                        if n == 5 and (not peeled or b > 0):
                            take_act(b - 1)
                        if n < 16 or not peeled or b > 0:
                            split(b, n)
                        if n == 20:
                            clamp_gate(b, 0)
                            clamp_gate(b, 1)
                        if n == 21:
                            swiglu(b, 0)
                        if n == 22:
                            take_x(b + 1)
                            swiglu(b, 1)
                    assert ch.n == ch.per_step, ("links per block", ch.n)

                def last(b):
                    for n in range(8):
                        if n == 5:
                            take_act(b - 1)
                        split(b, n)

                dve.wait_ge(bias_ready, 1)
                dve.tensor_tensor(bias_hl[E:2 * E, :], b12_raw[0:E, :], bias_hl[0:E, :].bitcast(F32),
                                  ALU.subtract).then_inc(bias_ready, 1)
                take_x(0)
                steps(dve, body, last)

            @block.gpsimd
            def _(pool):
                def carry_waits(n, b):
                    pool.wait_ge(spare_used[n].sem, spare_used[n].at(b, 0))
                    pool.tensor_tensor(spare[:, n:n + 1], spare[:, 2:3], spare[:, 2:3], ALU.add).then_inc(
                        spare_used[n].sem, 1)

                def gather(b):
                    pool.tensor_copy(g_idx[:], slots[:, bass.ds(b, 1), 0:1].rearrange("s a c -> s (a c)")).then_inc(
                        gidx_ready.sem, 1)
                    pool.wait_ge(gidx_ready.sem, gidx_ready.at(b, 1))
                    carry_waits(0, b)
                    pool.indirect_dma_start(xg, None, h2_rows,
                                            bass.IndirectOffsetOnAxis(ap=g_idx[:, 0:1], axis=0)).then_inc(
                        gather_in.sem, 16)

                def pick(b, tile):
                    e = pool.value_load(blk_exp[0:1, bass.ds(b, 1)], min_val=0, max_val=E - 1)
                    o = CONST["pick"][0]
                    pool.tensor_copy(tile[:], cst[0:2 * E, bass.ds(e + o, 1)].to_broadcast([2 * E, CAP])).then_inc(
                        pick_ready.sem, 1)

                def scatter(b):
                    pool.tensor_copy(w_cur[:], slots[:].bitcast(F32)[:, bass.ds(b, 1), 1:2].rearrange(
                        "s a c -> s (a c)"))
                    pool.tensor_copy(s_idx[:], slots[:, bass.ds(b, 1), 0:1].rearrange("s a c -> s (a c)")).then_inc(
                        sidx_ready.sem, 1)
                    pool.wait_ge(yrow_ready.sem, yrow_ready.at(b, 2))
                    carry_waits(1, b)
                    pool.indirect_dma_start(out, bass.IndirectOffsetOnAxis(ap=s_idx[:, 0:1], axis=0),
                                            y_rows, None, compute_op=ALU.add).then_inc(scatter_done.sem, 16)
                    pool.wait_ge(scatter_done.sem, scatter_done.at(b, 1))

                def body(b):
                    peeled = isinstance(b, int)
                    pool.wait_ge(tx_ready.sem, tx_ready.at(b, 2))
                    gather(b + 1)
                    if not peeled or b > 1:
                        scatter(b - 2)
                    if not peeled or b > 0:
                        pool.wait_ge(slab_used.sem, count(b, 16) + 1)
                    else:
                        pool.wait_ge(slab_used.sem, count(b, 0) + 1)
                    pick(b, pick2)
                    pick(b + 1, pick1)

                def last(b):
                    scatter(b - 2)
                    scatter(b - 1)

                pool.memset(spare[:], 0.0).then_inc(spare_ready, 1)
                pool.wait_ge(spare_ready, 1)
                pick(0, pick1)
                gather(0)
                steps(pool, body, last)


def toeplitz(rows):
    return bass.AP(tensor=rows.tensor, offset=rows.offset + (P - 1), ap=[[GL, HEADS], [-1, P], [1, 2 * P]])


def zero_rows(zeros):
    return zeros[0:CAP].unsqueeze(1).to_broadcast([CAP, D // 32, 32])


def constants():
    c = np.zeros((P, N_CONST), np.float32)
    r = np.arange(P)

    def put(name, a):
        o, w = CONST[name]
        c[:a.shape[0], o:o + w] = a

    put("ident", np.eye(P))
    put("tri", r[:, None] <= r[None, :])
    put("after", r[:, None] > r[None, :])
    put("ones", np.ones((P, P)))
    put("block", r[:, None] // HD == r[None, :] // HD)
    dist = np.maximum(2 * P - 1 - np.arange(GL), 0)
    exact = 16
    scaled = np.log(np.maximum(dist, 1).astype(np.float32) / exact) / np.float32(math.log(128 / exact))
    large = np.minimum(exact + (scaled * exact).astype(np.int32), 31)
    bucket = np.where(dist < exact, dist, large)
    onehot = (np.arange(32)[:, None] == bucket[None, :]).astype(np.float32)
    put("iota_e", np.tile(np.arange(E), (P, 1)))
    put("pick", r[:2 * E, None] % E == np.arange(E)[None, :])
    put("iota_b", np.tile(np.arange(NOV + 1), (P, 1)))
    ids = np.zeros((P, NT * TOPK, 2), np.int32)
    ids[:, :, 0] = np.arange(NT * TOPK)[None, :] // TOPK * P + r[:, None]
    pads = np.zeros((CAP, NB, 2), np.int32)
    pads[:, :, 0] = T + np.arange(CAP)[:, None]
    return c, onehot, ids.reshape(P, -1), pads.reshape(CAP, -1)


def lay_out(i):
    def rep(a):
        return np.broadcast_to(np.asarray(a).reshape(1, -1), (P, np.asarray(a).size))

    def cols(a):
        return np.asarray(a).reshape(-1, P).T

    parts = {"g_mix": cols(i["g_mix"]), "qg": np.tile(i["q_norm_g"][0], 2)[:, None],
             "kg": np.tile(i["k_norm_g"][0], 2)[:, None], "subg": i["attn_sub_g"][0][:, None],
             "lq1": rep(i["lambda_q1"]), "lk1": rep(i["lambda_k1"]), "lq2": rep(i["lambda_q2"]),
             "lk2": rep(i["lambda_k2"]), "dt_bias": rep(i["dt_bias"]), "a_log": rep(i["a_log"]),
             "d_skip": rep(i["d_skip"]), "b_router": rep(i["b_router"])}
    small = np.concatenate([parts[n] for n in SMALL], axis=1)
    w = np.asarray(i["w_in"][0]).reshape(KT, P, -1)
    q0, k0, v0, z0, x0, b0, c0, dt0, g0 = 0, 1024, 2048, 3072, 5120, 7168, 8192, 9216, 9248

    def step(n):
        starts = (x0 + n * GW, x0 + n * GW + P, b0 + n * P, c0 + n * P, q0 + n * P, k0 + n * P)
        tiles = [w[:, :, s:s + P].transpose(1, 0, 2).reshape(P, D) for s in starts]
        vz = np.concatenate([w[:, :, v0 + n * P:v0 + (n + 1) * P], w[:, :, z0 + n * GW:z0 + (n + 1) * GW]], 2)
        vz = vz.transpose(1, 0, 2).reshape(P, 3, D).transpose(1, 0, 2)
        return np.stack(tiles[:3] + list(vz) + tiles[3:])

    w_mix = np.stack([step(n) for n in range(HEADS)])
    w_dt = w[:, :, dt0:dt0 + SSM_H].transpose(1, 0, 2).reshape(P, -1)
    taps = np.concatenate([np.asarray(i["conv_w"][0]), np.asarray(i["conv_b"])])
    par = []
    for n in range(HEADS):
        tiles = [taps[:, s:s + P] for s in (n * GW, n * GW + P, 2048 + n * P, 3072 + n * P)]
        par += [t[j] for t in tiles for j in range(4)] + [t[4] for t in tiles]
        par += [np.asarray(i["ssm_norm_g"][0])[n * GW + j * P:n * GW + (j + 1) * P] for j in range(2)]
    par = np.stack(par, 1)
    wo = np.concatenate([np.asarray(i["w_attn_o"][0]), np.asarray(i["w_ssm_o"][0])])
    w_o = wo.reshape(3, KT, P, KT, P).transpose(3, 0, 2, 1, 4).reshape(KT, 3, P, D)
    gates = np.stack([w[:, :, s:s + D] for s in (g0, g0 + D)]).reshape(2, KT, P, KT, P)
    gates = gates.transpose(3, 0, 2, 1, 4).reshape(KT, 2, P, D)
    w_tail = np.concatenate([np.concatenate([gates, w_o], 1).reshape(-1, P, D),
                             np.asarray(i["w_out"][0]).reshape(KT, P, D)])
    w_rt = np.asarray(i["w_router"][0]).reshape(KT, P, E).transpose(1, 0, 2).reshape(P, -1)
    w1 = np.asarray(i["w1"][0]).reshape(E, KT, P, 2 * D)
    w2 = np.asarray(i["w2"][0]).reshape(E, 8, P, D)
    b12 = np.concatenate([i["b1"][0], i["b2"][0]], 1)
    consts, onehot, ids, pads = constants()
    return {"x": i["x"], "small": small, "consts": consts, "onehot": onehot, "gffn": rep(i["g_ffn"]), "rel_bias": i["rel_bias"],
            "par": par, "w_mix": w_mix, "w_dt": w_dt, "w_tail": w_tail, "w_rt": w_rt,
            "w1": w1, "w2": w2, "b12": b12, "tok_ids": ids, "pads": pads}


def kernel(**inputs):
    import concourse.bacc as bacc
    from concourse.bass_utils import run_bass_kernel_spmd as run

    nc = bacc.Bacc("TRN2", target_bir_lowering=False, num_devices=1)
    arrays, args = {}, []
    for name, a in lay_out(inputs).items():
        a = np.ascontiguousarray(a)
        arrays[f"in_{name}"] = a
        args.append(nc.dram_tensor(f"in_{name}", a.shape, mybir.dt.from_np(a.dtype), kind="ExternalInput").ap())
    args.append(nc.dram_tensor("out_rows", (ROWS, D), F32, kind="ExternalOutput").ap())
    decoder_layer(nc, *args)
    r = run(nc, [arrays], core_ids=[0])
    return r.results[0]["out_rows"][:T].reshape(1, T, D)
```
